# Optimizing a Trainium2 kernel written in Bass

```python
import math
import jax
import jax.numpy as jnp
from jax import lax
import numpy as np

D_MODEL = 1024
BATCH = 1
SEQ = 512
DEPTH = 2
DEC_BATCH = 8
DEC_SEQ = 8
PAST_LEN = 256
PAGE_SIZE = 128

N_HEADS = 4
HEAD_K = 128
HEAD_V = 128
MIX_W = N_HEADS * HEAD_V
N_BRANCH = 4
CHUNK = 64
CONV_W = 4
GDN_CONV_CH = 3 * MIX_W
DIFF_DK = 64
Q_BLOCK = 128
N_KEYS = 128
N_EXPERTS = N_KEYS * N_KEYS
PEER_HEADS = 8
PEER_DK = 128
PEER_TOPK = 16
PEER_BLOCK = 256
EPS = 1e-6
SPLIT_SIZES = (MIX_W, MIX_W, MIX_W, MIX_W,
               MIX_W, MIX_W, MIX_W, MIX_W,
               GDN_CONV_CH, MIX_W, N_HEADS, N_HEADS,
               N_HEADS * 2 * DIFF_DK, N_HEADS * 2 * DIFF_DK, MIX_W,
               N_BRANCH * D_MODEL)
N_IN = sum(SPLIT_SIZES)

kernel_name = 'hybrid_retention_hgrn2_gdn_diffattn_peer_step'

def rms_norm(x, g):
    xf = x.astype(jnp.float32)
    y = xf * lax.rsqrt(jnp.mean(xf * xf, axis=-1, keepdims=True) + EPS)
    return (y * g.astype(jnp.float32)).astype(x.dtype)

def head_rms_norm(o, g):
    of = o.astype(jnp.float32)
    y = of * lax.rsqrt(jnp.mean(of * of, axis=-1, keepdims=True) + EPS)
    return y * g.astype(jnp.float32).reshape(N_HEADS, -1)

def l2_norm(x):
    xf = x.astype(jnp.float32)
    return xf * lax.rsqrt(jnp.sum(xf * xf, axis=-1, keepdims=True) + EPS)

def alibi_slopes():
    return jnp.exp2(-8.0 * jnp.arange(1, N_HEADS + 1, dtype=jnp.float32) / N_HEADS)

def to_chunks(x, c):
    b, t = x.shape[:2]
    return jnp.swapaxes(jnp.moveaxis(x.reshape(b, t // c, c, *x.shape[2:]), 1, 0), 2, 3)

def from_chunks(x):
    n, b, h, c = x.shape[:4]
    return jnp.moveaxis(jnp.swapaxes(x, 2, 3), 0, 1).reshape(b, n * c, h, *x.shape[4:])

def retention_chunked(q, k, v, log_gamma, s0):
    f32 = jnp.float32
    c = math.gcd(q.shape[1], CHUNK)
    pos = jnp.arange(c, dtype=f32)
    gap = pos[:, None] - pos[None, :]
    intra = jnp.where(gap >= 0, jnp.exp(jnp.maximum(gap, 0.0) * log_gamma[:, None, None]), 0.0)
    q_dec = jnp.exp((pos + 1.0) * log_gamma[:, None])[..., None]
    k_dec = jnp.exp((c - 1.0 - pos) * log_gamma[:, None])[..., None]
    chunk_dec = jnp.exp(c * log_gamma)[:, None, None]

    def step(s, inp):
        qi, ki, vi = inp
        scores = jnp.einsum('bhik,bhjk->bhij', qi, ki) * intra
        o = jnp.einsum('bhij,bhjv->bhiv', scores, vi) + jnp.einsum('bhik,bhkv->bhiv', qi * q_dec, s)
        s_new = chunk_dec * s + jnp.einsum('bhjk,bhjv->bhkv', ki * k_dec, vi)
        return s_new, o

    xs = tuple(to_chunks(a.astype(f32), c) for a in (q, k, v))
    s_fin, oc = lax.scan(step, s0.astype(f32), xs)
    return from_chunks(oc), s_fin.astype(s0.dtype)

def gla_chunked(q, k, v, log_f, s0):
    f32 = jnp.float32
    c = math.gcd(q.shape[1], CHUNK)
    incl = jnp.tril(jnp.ones((c, c), bool))

    def step(s, inp):
        qi, ki, vi, fi = inp
        cum = jnp.cumsum(fi, axis=2)
        rel = cum[:, :, :, None, :] - cum[:, :, None, :, :]
        rel = jnp.exp(jnp.where(incl[:, :, None], rel, -jnp.inf))
        scores = jnp.einsum('bhik,bhjk,bhijk->bhij', qi, ki, rel)
        o = jnp.einsum('bhij,bhjv->bhiv', scores, vi) + jnp.einsum('bhik,bhkv->bhiv', qi * jnp.exp(cum), s)
        last = cum[:, :, -1:, :]
        s_new = jnp.exp(last[:, :, 0, :, None]) * s + jnp.einsum('bhjk,bhjv->bhkv', ki * jnp.exp(last - cum), vi)
        return s_new, o

    xs = tuple(to_chunks(a.astype(f32), c) for a in (q, k, v, log_f))
    s_fin, oc = lax.scan(step, s0.astype(f32), xs)
    return from_chunks(oc), s_fin.astype(s0.dtype)

def gated_delta_chunked(q, k, v, log_g, beta, s0):
    f32 = jnp.float32
    c = math.gcd(q.shape[1], CHUNK)
    dv = v.shape[-1]
    incl = jnp.tril(jnp.ones((c, c), bool))
    strict = jnp.tril(jnp.ones((c, c), bool), -1)
    eye = jnp.eye(c, dtype=f32)

    def step(s, inp):
        qi, ki, vi, gi, bi = inp
        cum = jnp.cumsum(gi, axis=-1)
        dec = jnp.exp(jnp.where(incl, cum[..., :, None] - cum[..., None, :], -jnp.inf))
        kk = jnp.einsum('bhik,bhjk->bhij', ki, ki)
        a = jnp.where(strict, bi[..., None] * kk * dec, 0.0)
        rhs = jnp.concatenate([bi[..., None] * vi, (bi * jnp.exp(cum))[..., None] * ki], axis=-1)
        sol = lax.linalg.triangular_solve(eye + a, rhs, left_side=True, lower=True, unit_diagonal=True)
        u, w = sol[..., :dv], sol[..., dv:]
        delta = u - jnp.einsum('bhik,bhkv->bhiv', w, s)
        qk = jnp.einsum('bhik,bhjk->bhij', qi, ki) * dec
        o = jnp.einsum('bhij,bhjv->bhiv', qk, delta) + jnp.einsum('bhik,bhkv->bhiv', qi * jnp.exp(cum)[..., None], s)
        s_new = jnp.exp(cum[..., -1])[..., None, None] * s + jnp.einsum(
            'bhjk,bhjv->bhkv', ki * jnp.exp(cum[..., -1:] - cum)[..., None], delta)
        return s_new, o

    xs = tuple(to_chunks(a.astype(f32), c) for a in (q, k, v, log_g, beta))
    s_fin, oc = lax.scan(step, s0.astype(f32), xs)
    return from_chunks(oc), s_fin.astype(s0.dtype)

def causal_conv(x, buf, w):
    t = x.shape[1]
    xp = jnp.concatenate([buf.astype(x.dtype), x], axis=1)
    y = sum(xp[:, j:j + t] * w[j] for j in range(CONV_W))
    return y, xp[:, t:]

def diff_attn_block(q, k, v, q_pos, k_pos, lam):
    f32 = jnp.float32
    s = jnp.einsum('bqhcd,bkhcd->bhcqk', q, k).astype(f32) * DIFF_DK ** -0.5
    dist = q_pos[:, None] - k_pos[None, :]
    s = s - alibi_slopes()[:, None, None, None] * dist.astype(f32)
    s = jnp.where(dist >= 0, s, -jnp.inf)
    p = jax.nn.softmax(s, axis=-1)
    attn = p[:, :, 0] - lam * p[:, :, 1]
    return jnp.einsum('bhqk,bkhd->bqhd', attn, v.astype(f32))

def diff_attn_prompt(q, k, v, lam):
    b, t = q.shape[:2]
    qb = math.gcd(t, Q_BLOCK)
    nb = t // qb
    k_pos = jnp.arange(t)
    qs = jnp.moveaxis(q.reshape(b, nb, qb, *q.shape[2:]), 1, 0)
    starts = jnp.arange(nb) * qb

    def blk(args):
        qi, st = args
        return diff_attn_block(qi, k, v, st + jnp.arange(qb), k_pos, lam)

    o = lax.map(blk, (qs, starts))
    return jnp.moveaxis(o, 0, 1).reshape(b, t, N_HEADS, -1)

def peer_ffn(x, wq, keys, u_tab, v_tab):
    b, t, d = x.shape
    n = b * t
    blk = math.gcd(n, PEER_BLOCK)

    def block(xb):
        q = (xb @ wq).reshape(blk, PEER_HEADS, 2, PEER_DK)
        s = jnp.einsum('nhpd,hpkd->nhpk', q, keys)
        s1, i1 = lax.top_k(s[:, :, 0], PEER_TOPK)
        s2, i2 = lax.top_k(s[:, :, 1], PEER_TOPK)
        cand = (s1[..., :, None] + s2[..., None, :]).reshape(blk, PEER_HEADS, PEER_TOPK * PEER_TOPK)
        cidx = (i1[..., :, None] * N_KEYS + i2[..., None, :]).reshape(blk, PEER_HEADS, PEER_TOPK * PEER_TOPK)
        sc, pos = lax.top_k(cand, PEER_TOPK)
        idx = jnp.take_along_axis(cidx, pos, axis=-1)
        g = jax.nn.softmax(sc.astype(jnp.float32), axis=-1)
        act = jax.nn.gelu(jnp.einsum('nhkd,nd->nhk', u_tab[idx], xb), approximate=False)
        return jnp.einsum('nhk,nhkd->nd', (g * act).astype(v_tab.dtype), v_tab[idx])

    out = lax.map(block, x.reshape(n // blk, blk, d))
    return out.reshape(b, t, d)

def hgrn_lower_bounds(logits):
    c = jnp.cumsum(jax.nn.softmax(logits.astype(jnp.float32), axis=0), axis=0)
    return c - c[0:1]

def trunk_layer(x, s_ret, s_hgrn, s_gdn, conv_buf, k_past, v_past, layer_idx, lb,
                norm_mix, w_in, ret_norm, hgrn_norm, gdn_conv, gdn_a_log, gdn_dt_bias, gdn_norm,
                diff_q_norm, diff_k_norm, diff_lambda, diff_norm, w_branch, w_out, norm_ffn,
                peer_wq, peer_keys, peer_u, peer_v):
    f32 = jnp.float32
    b, t, _ = x.shape
    xn = rms_norm(x, norm_mix)
    (r_q, r_k, r_v, r_g, h_q, h_f, h_i, h_g, g_qkv, g_g, g_a, g_b, d_q, d_k, d_v, gate_in) = jnp.split(
        xn @ w_in, np.cumsum(SPLIT_SIZES)[:-1].tolist(), axis=-1)
    heads = lambda z: z.reshape(b, t, N_HEADS, -1)

    log_gamma = jnp.log1p(-jnp.exp2(-5.0 - jnp.arange(N_HEADS, dtype=f32)))
    o, s_ret_new = retention_chunked(heads(r_q), heads(r_k) * HEAD_K ** -0.5, heads(r_v), log_gamma, s_ret)
    o_ret = head_rms_norm(o, ret_norm) * jax.nn.silu(heads(r_g).astype(f32))

    z = heads(h_f).astype(f32)
    lbh = lb.reshape(N_HEADS, HEAD_K)
    log_f = jnp.logaddexp(jnp.log(lbh), jnp.log1p(-lbh) + jax.nn.log_sigmoid(z))
    k_in = (1.0 - lbh) * jax.nn.sigmoid(-z)
    o, s_hgrn_new = gla_chunked(heads(h_q) * HEAD_K ** -0.5, k_in, heads(h_i), log_f, s_hgrn)
    o_hgrn = head_rms_norm(o, hgrn_norm) * jax.nn.silu(heads(h_g).astype(f32))

    qkv, conv_new = causal_conv(g_qkv, conv_buf, gdn_conv)
    gq, gk, gv = jnp.split(jax.nn.silu(qkv), 3, axis=-1)
    log_g = -jnp.exp(gdn_a_log.astype(f32)) * jax.nn.softplus(g_a.astype(f32) + gdn_dt_bias.astype(f32))
    beta = jax.nn.sigmoid(g_b.astype(f32))
    o, s_gdn_new = gated_delta_chunked(l2_norm(heads(gq)) * HEAD_K ** -0.5, l2_norm(heads(gk)), heads(gv),
                                       log_g, beta, s_gdn)
    o_gdn = head_rms_norm(o, gdn_norm) * jax.nn.silu(heads(g_g).astype(f32))

    dq = rms_norm(d_q.reshape(b, t, N_HEADS, 2, DIFF_DK), diff_q_norm)
    dk = rms_norm(d_k.reshape(b, t, N_HEADS, 2, DIFF_DK), diff_k_norm)
    dv = heads(d_v)
    lam_init = 0.8 - 0.6 * math.exp(-0.3 * layer_idx)
    lp = diff_lambda.astype(f32)
    lam = jnp.exp(jnp.sum(lp[0] * lp[1])) - jnp.exp(jnp.sum(lp[2] * lp[3])) + lam_init
    if k_past is None:
        o = diff_attn_prompt(dq, dk, dv, lam)
    else:
        past = k_past.shape[1]
        k_all = jnp.concatenate([k_past.astype(dk.dtype), dk], axis=1)
        v_all = jnp.concatenate([v_past.astype(dv.dtype), dv], axis=1)
        o = diff_attn_block(dq, k_all, v_all, past + jnp.arange(t), jnp.arange(past + t), lam)
    o_diff = head_rms_norm(o, diff_norm) * (1.0 - lam_init)

    branches = jnp.stack([o_ret, o_hgrn, o_gdn, o_diff], axis=2).reshape(b, t, N_BRANCH, MIX_W).astype(x.dtype)
    gates = jax.nn.sigmoid(gate_in.reshape(b, t, N_BRANCH, D_MODEL))
    merged = jnp.einsum('btnc,ncd->btnd', branches, w_branch)
    h = x + jnp.sum(gates * merged, axis=2) @ w_out
    y = h + peer_ffn(rms_norm(h, norm_ffn), peer_wq, peer_keys, peer_u, peer_v)
    return y, s_ret_new, s_hgrn_new, s_gdn_new, conv_new, dk, dv

def setup_inputs(seed: int = 0) -> dict:
    key = jax.random.key(seed)
    ks = jax.random.split(key, 40)
    f32 = jnp.float32
    n_pages = PAST_LEN // PAGE_SIZE
    n_used = DEC_BATCH * n_pages
    n_phys = n_used + n_used // 4
    nrm = lambda k, shape, scale: scale * jax.random.normal(k, shape, f32)
    gain = lambda k, shape: 1.0 + 0.02 * jax.random.normal(k, shape, f32)
    dt = jnp.exp(math.log(1e-3) + jax.random.uniform(ks[20], (DEPTH, N_HEADS), f32) * (math.log(1e-1) - math.log(1e-3)))
    return {
        'x_prompt': nrm(ks[0], (BATCH, SEQ, D_MODEL), 1.0),
        'x_sample': nrm(ks[1], (DEC_BATCH, DEC_SEQ, D_MODEL), 1.0),
        'state_ret': nrm(ks[2], (DEPTH, DEC_BATCH, N_HEADS, HEAD_K, HEAD_V), 0.5),
        'state_hgrn': nrm(ks[3], (DEPTH, DEC_BATCH, N_HEADS, HEAD_K, HEAD_V), 0.5),
        'state_gdn': nrm(ks[4], (DEPTH, DEC_BATCH, N_HEADS, HEAD_K, HEAD_V), 0.5),
        'state_gdn_conv': nrm(ks[5], (DEPTH, DEC_BATCH, CONV_W - 1, GDN_CONV_CH), 1.0),
        'cache_k': nrm(ks[6], (DEPTH, n_phys, PAGE_SIZE, N_HEADS, 2, DIFF_DK), 1.0),
        'cache_v': nrm(ks[7], (DEPTH, n_phys, PAGE_SIZE, N_HEADS, HEAD_V), 1.0),
        'page_table': jax.random.permutation(ks[8], n_phys)[:n_used].reshape(DEC_BATCH, n_pages).astype(jnp.int32),
        'norm_mix': gain(ks[9], (DEPTH, D_MODEL)),
        'w_in': nrm(ks[10], (DEPTH, D_MODEL, N_IN), D_MODEL ** -0.5),
        'ret_norm': gain(ks[11], (DEPTH, MIX_W)),
        'hgrn_lb_logits': nrm(ks[12], (DEPTH, MIX_W), 0.5),
        'hgrn_norm': gain(ks[13], (DEPTH, MIX_W)),
        'gdn_conv': nrm(ks[14], (DEPTH, CONV_W, GDN_CONV_CH), CONV_W ** -0.5),
        'gdn_a_log': jnp.log(jax.random.uniform(ks[15], (DEPTH, N_HEADS), f32, 1.0, 16.0)),
        'gdn_dt_bias': dt + jnp.log(-jnp.expm1(-dt)),
        'gdn_norm': gain(ks[16], (DEPTH, MIX_W)),
        'diff_q_norm': gain(ks[17], (DEPTH, DIFF_DK)),
        'diff_k_norm': gain(ks[18], (DEPTH, DIFF_DK)),
        'diff_lambda': nrm(ks[19], (DEPTH, 4, DIFF_DK), 0.1),
        'diff_norm': gain(ks[21], (DEPTH, MIX_W)),
        'w_branch': nrm(ks[22], (DEPTH, N_BRANCH, MIX_W, D_MODEL), MIX_W ** -0.5),
        'w_out': nrm(ks[23], (DEPTH, D_MODEL, D_MODEL), D_MODEL ** -0.5),
        'norm_ffn': gain(ks[24], (DEPTH, D_MODEL)),
        'peer_wq': nrm(ks[25], (DEPTH, D_MODEL, PEER_HEADS * 2 * PEER_DK), D_MODEL ** -0.5),
        'peer_keys': nrm(ks[26], (DEPTH, PEER_HEADS, 2, N_KEYS, PEER_DK), PEER_DK ** -0.5),
        'peer_u': nrm(ks[27], (DEPTH, N_EXPERTS, D_MODEL), D_MODEL ** -0.5),
        'peer_v': nrm(ks[28], (DEPTH, N_EXPERTS, D_MODEL), PEER_HEADS ** -0.5),
    }

def reference(x_prompt, x_sample, state_ret, state_hgrn, state_gdn, state_gdn_conv, cache_k, cache_v, page_table,
              norm_mix, w_in, ret_norm, hgrn_lb_logits, hgrn_norm, gdn_conv, gdn_a_log, gdn_dt_bias, gdn_norm,
              diff_q_norm, diff_k_norm, diff_lambda, diff_norm, w_branch, w_out, norm_ffn,
              peer_wq, peer_keys, peer_u, peer_v):
    f32 = jnp.float32
    n_pages = PAST_LEN // PAGE_SIZE
    bp = x_prompt.shape[0]
    bs = x_sample.shape[0]
    lower_bounds = hgrn_lower_bounds(hgrn_lb_logits)
    zero_state = jnp.zeros((bp, N_HEADS, HEAD_K, HEAD_V), f32)
    zero_conv = jnp.zeros((bp, CONV_W - 1, GDN_CONV_CH), x_prompt.dtype)
    yp, ys = x_prompt, x_sample
    ret_p, ret_s, hg_p, hg_s, gd_p, gd_s, cv_p, cv_s, k_p, v_p, k_s, v_s = ([] for _ in range(12))
    for l in range(DEPTH):
        lw = (norm_mix[l], w_in[l], ret_norm[l], hgrn_norm[l], gdn_conv[l], gdn_a_log[l], gdn_dt_bias[l],
              gdn_norm[l], diff_q_norm[l], diff_k_norm[l], diff_lambda[l], diff_norm[l], w_branch[l], w_out[l],
              norm_ffn[l], peer_wq[l], peer_keys[l], peer_u[l], peer_v[l])
        yp, rp, hp, gp, cp, kp, vp = trunk_layer(yp, zero_state, zero_state, zero_state, zero_conv, None, None,
                                                 l, lower_bounds[l], *lw)
        k_past = cache_k[l][page_table].reshape(bs, n_pages * PAGE_SIZE, N_HEADS, 2, DIFF_DK)
        v_past = cache_v[l][page_table].reshape(bs, n_pages * PAGE_SIZE, N_HEADS, HEAD_V)
        ys, rs, hs, gs, cs, kn, vn = trunk_layer(ys, state_ret[l], state_hgrn[l], state_gdn[l], state_gdn_conv[l],
                                                 k_past, v_past, l, lower_bounds[l], *lw)
        ret_p.append(rp); ret_s.append(rs); hg_p.append(hp); hg_s.append(hs)
        gd_p.append(gp); gd_s.append(gs); cv_p.append(cp); cv_s.append(cs)
        k_p.append(kp); v_p.append(vp); k_s.append(kn); v_s.append(vn)
    st = lambda xs: jnp.stack(xs, axis=0)
    return (yp, ys, st(ret_p), st(ret_s), st(hg_p), st(hg_s), st(gd_p), st(gd_s), st(cv_p), st(cv_s),
            st(k_p), st(v_p), st(k_s), st(v_s))


_drawn_inputs = setup_inputs


def setup_inputs(seed=0):
    import zlib

    import numpy as np

    out = dict(_drawn_inputs(seed))
    spreads = {}
    factors = {}
    for name, (base, spread) in spreads.items():
        noise = np.random.default_rng([zlib.crc32(name.encode()), seed]).standard_normal(out[name].shape)
        drawn = base * np.exp(spread * noise) if base else spread * noise
        out[name] = jnp.asarray(drawn.astype(out[name].dtype))
    for name, factor in factors.items():
        out[name] = (out[name] * factor).astype(out[name].dtype)
    return out
```

```python
from contextlib import ExitStack, contextmanager

import numpy as np
import concourse.bass as bass
from concourse import mybir

F32 = mybir.dt.float32
BF16 = mybir.dt.bfloat16
U32 = mybir.dt.uint32
I32 = mybir.dt.int32
ALU = mybir.AluOpType
ACT = mybir.ActivationFunctionType
AX_X = mybir.AxisListType.X

P = 128
D = 1024
KD = D // P
DEPTH = 2
SEQ = 512
DEC_B, DEC_T = 8, 8
NS = DEC_B * DEC_T
N = SEQ + NS
TILES = 5
NP_ = TILES * P
HALF = N // 2
H = 4
LEVELS = 7
W_HEAD = 12
PAGES = 2
PAGE = 128
PAST = PAGES * PAGE
N_PHYS = DEC_B * PAGES + DEC_B * PAGES // 4
DK = 64
EPS = 1e-6
K_SCALE = float(P) ** -0.5
S_SCALE = float(DK) ** -0.5
PH_HEADS = 8
TOPK = 16
NKEY = 128
HJ = NKEY // 2
FAR = 1e30
BANK = 512
GT = 8

C_MSK = 0
C_ONES = C_MSK + (1 + LEVELS) * P
C_UT = C_ONES + P
C_BLK = C_UT + TILES * P
C_BS = C_BLK + P
C_COMP = C_BS + DEC_B
C_SELA = C_COMP + P
C_SELB = C_SELA + 1
GC_W = C_SELB + 1
C_DP = 0
C_DS = C_DP + SEQ
C_STK = C_DS + PAST + NS
C_QM = C_STK + NS
DC_W = C_QM + (DEC_B + 1) * P
H_RM = 0
H_QD = H_RM + NP_
H_KD = H_QD + NP_
H_GT = H_KD + TILES
H_G8 = H_GT + TILES
H_SL = H_G8 + DEC_B
HC_W = H_SL + 1
Q_RN, Q_HN, Q_GN, Q_DN = 0, 1, 2, 3
Q_CONV = 4
Q_LB = Q_CONV + 12
Q_QN, Q_KN = Q_LB + 2, Q_LB + 3
PH_W = Q_KN + 1
L_NM, L_NF = 0, KD
L_AL = 2 * KD
L_DT = L_AL + H
L_LAM = L_DT + H
L_LB = L_LAM + 4 * DK
L_LI, L_OL = L_LB + 1, L_LB + 2
PL_W = L_OL + 1


class Memory:
    pass


@contextmanager
def stage(nc, *names):
    with ExitStack() as ctx:
        sems = {n: ctx.enter_context(nc.semaphore(n)) for n in names}
        with nc.Block(no_gpsimd_drain=True) as block:
            yield block, sems
        for n in names:
            nc.sync.sem_clear(sems[n])
        nc.all_engine_barrier(sem_only=True)


def chained(engine, sem):
    count = [0]

    def link(instruction):
        count[0] += 1
        instruction.then_inc(sem, 1)
        engine.wait_ge(sem, count[0])

    return link


def bank(T, b, width=BANK):
    return T.ps[:, b * BANK:b * BANK + width]


def halves(T, b):
    return T.ps[:, b * BANK:(b + 2) * BANK].rearrange("p (a c) -> p a c", a=2)[:, :, 0:HALF]


def two(ap):
    return ap[:, 0:N].rearrange("p (a c) -> p a c", a=2)


def tile(ap, t):
    return ap[:, t * P:(t + 1) * P]


def wide_product(nc, T, b, weights, rhs, kn):
    for a in range(2):
        for k in range(kn):
            last = nc.tensor.matmul(bank(T, b + a)[:, 0:HALF], weights(k), rhs(k)[:, a * HALF:(a + 1) * HALF],
                                    start=(k == 0), stop=(k == kn - 1))
    return last


def project(nc, pe, T, s, n, psum_banks=(0, 2)):
    for c in range(n):
        pe.wait_ge(s["w"][c], 16)
        if c >= 2:
            pe.wait_ge(s["evicted"], c - 1)
        wide_product(nc, T, psum_banks[c % 2], lambda k: T.wr[:, c, k, :], lambda k: T.xn[:, k, :],
                     KD).then_inc(s["projected"], 1)


def load_head_weights(sp, T, s, l, h, tiles):
    for i, c in enumerate(tiles):
        sp.dma_start(T.wr[:, i], T.d["w_cm"][l, h, c]).then_inc(s["w"][i], 16)


W_SEMS = ("w0", "w1", "w2", "w3")


def norm_stage(nc, T, l, first):
    names = ("h_in", "small_in", "const_in", "squared", "summed", "scaled", "rooted", "chain_v", "chain_a",
             "zeroed", "normed", "ab_done", "a_ready", "lam_ready", "exp_done", "sp_abs", "sp_exp", "sp_in",
             "sp_ln", "b_done", "al_done")
    with stage(nc, *names) as (block, s):
        @block.sync
        def _(sp):
            if first:
                sp.dma_start(T.h[:], T.d["xs"].rearrange("m p n -> p m n")).then_inc(s["h_in"], 16)
                sp.dma_start(T.pl[:], T.d["pl"][l]).then_inc(s["small_in"], 16)
                sp.dma_start(T.wab, T.d["w_ab"][l]).then_inc(s["small_in"], 16)
                sp.dma_start(T.general[:], T.d["gc"]).then_inc(s["const_in"], 16)

        @block.scalar
        def _(act):
            if first:
                act.wait_ge(s["h_in"], 16)
            for k in range(KD):
                nc.scalar.activation(T.sq[:, k, :], T.h[:, k, :], ACT.Square).then_inc(s["squared"], 1)
            act.wait_ge(s["scaled"], 1)
            nc.scalar.activation(T.rs, T.rs, ACT.Sqrt).then_inc(s["rooted"], 1)
            if first:
                act.wait_ge(s["lam_ready"], 1)
                nc.scalar.activation(T.lam[:, 0:2], T.lam[:, 0:2], ACT.Exp).then_inc(s["exp_done"], 1)
                nc.scalar.activation(T.nea, T.pl[:, L_AL:L_AL + H], ACT.Exp).then_inc(s["al_done"], 1)
                act.wait_ge(s["a_ready"], 1)
                nc.scalar.activation(T.ga2, T.ga, ACT.Abs).then_inc(s["chain_a"], 1)
                act.wait_ge(s["chain_a"], 1)
                nc.scalar.activation(T.ga2, T.ga2, ACT.Exp, scale=-1.0).then_inc(s["sp_exp"], 1)
                act.wait_ge(s["sp_in"], 1)
                nc.scalar.activation(T.ga2, T.ga2, ACT.Ln).then_inc(s["sp_ln"], 1)
                act.wait_ge(s["ab_done"], 1)
                nc.scalar.activation(T.beta, bank(T, 2, TILES * 2 * H).rearrange("p (t c) -> p t c", c=2 * H)[:, :, H:],
                                     ACT.Sigmoid).then_inc(s["b_done"], 1)
                act.wait_ge(s["b_done"], 1)

        @block.tensor
        def _(pe):
            if first:
                pe.wait_ge(s["const_in"], 16)
            pe.wait_ge(s["squared"], KD)
            wide_product(nc, T, 0, lambda k: T.ones, lambda k: T.sq[:, k, :], KD).then_inc(s["summed"], 1)
            if first:
                pe.wait_ge(s["small_in"], 32)
                pe.wait_ge(s["zeroed"], 1)
                pe.wait_ge(s["normed"], KD)
                for t in range(TILES):
                    for k in range(KD):
                        last = nc.tensor.matmul(T.ps[:, 2 * BANK + t * 2 * H:2 * BANK + (t + 1) * 2 * H],
                                                tile(T.xn[:, k, :], t), T.wab[:, k, :],
                                                start=(k == 0), stop=(k == KD - 1))
                last.then_inc(s["ab_done"], 1)

        @block.vector
        def _(dve):
            link = chained(dve, s["chain_v"])
            if first:
                nc.vector.memset(T.xn[:, :, N:NP_], 0.0).then_inc(s["zeroed"], 1)
                link(nc.vector.memset(T.pr[:], 0.0))
            dve.wait_ge(s["summed"], 1)
            nc.vector.tensor_scalar(T.rs, halves(T, 0), 1.0 / D, EPS, ALU.mult, ALU.add).then_inc(s["scaled"], 1)
            dve.wait_ge(s["rooted"], 1)
            link(nc.vector.reciprocal(T.rs, T.rs))
            g0 = L_NM if first else L_NF
            if first:
                dve.wait_ge(s["small_in"], 32)
            for k in range(KD):
                nc.vector.scalar_tensor_tensor(out=two(T.xn[:, k, :]), in0=two(T.h[:, k, :]),
                                               scalar=T.pl[:, g0 + k:g0 + k + 1], in1=T.rs,
                                               op0=ALU.mult, op1=ALU.mult).then_inc(s["normed"], 1)
            if first:
                lp = T.pl[:, L_LAM:L_LAM + 4 * DK].rearrange("p (a b d) -> p a b d", a=2, b=2)
                link(nc.vector.tensor_tensor(T.lprod, lp[:, :, 0, :], lp[:, :, 1, :], ALU.mult))
                nc.vector.tensor_reduce(T.lam[:, 0:2], T.lprod, AX_X, ALU.add).then_inc(s["lam_ready"], 1)
                dve.wait_ge(s["exp_done"], 1)
                link(nc.vector.tensor_tensor(T.lam[:, 2:3], T.lam[:, 1:2], T.lam[:, 0:1], ALU.subtract))
                link(nc.vector.tensor_tensor(T.lam[:, 2:3], T.lam[:, 2:3], T.pl[:, L_LI:L_LI + 1], ALU.subtract))
                link(nc.vector.scalar_tensor_tensor(out=T.lam[:, 3:4], in0=T.general[:, C_SELB:C_SELB + 1],
                                                    scalar=T.lam[:, 2:3], in1=T.general[:, C_SELA:C_SELA + 1],
                                                    op0=ALU.mult, op1=ALU.add))
                dve.wait_ge(s["ab_done"], 1)
                ab = bank(T, 2, TILES * 2 * H).rearrange("p (t c) -> p t c", c=2 * H)
                nc.vector.tensor_tensor(T.ga, ab[:, :, 0:H],
                                        T.pl[:, L_DT:L_DT + H].unsqueeze(1).to_broadcast([P, TILES, H]),
                                        ALU.add).then_inc(s["a_ready"], 1)
                dve.wait_ge(s["sp_exp"], 1)
                nc.vector.tensor_scalar(T.ga2, T.ga2, 1.0, None, ALU.add).then_inc(s["sp_in"], 1)
                dve.wait_ge(s["sp_ln"], 1)
                link(nc.vector.scalar_tensor_tensor(out=T.ga, in0=T.ga, scalar=0.0, in1=T.ga2,
                                                    op0=ALU.max, op1=ALU.add))
                dve.wait_ge(s["al_done"], 1)
                link(nc.vector.scalar_tensor_tensor(out=T.logg, in0=T.ga, scalar=-1.0,
                                                    in1=T.nea.unsqueeze(1).to_broadcast([P, TILES, H]),
                                                    op0=ALU.mult, op1=ALU.mult))


def values_stage(nc, T, l, h):
    with stage(nc, "w_in", "vproj", "vcopied", "v_out", "small_in") as (block, s):
        @block.sync
        def _(sp):
            sp.dma_start(T.wtm, T.d["w_tm"][l, h]).then_inc(s["w_in"], 16)
            sp.dma_start(T.hc[:], T.d["hc"][h]).then_inc(s["small_in"], 16)
            sp.dma_start(T.ph[:], T.d["ph"][l, h]).then_inc(s["small_in"], 16)
            sp.wait_ge(s["vcopied"], TILES)
            sp.dma_start(T.d["v_prompt"][l, h].rearrange("(t p) d -> p t d", p=P),
                         T.vt[:, 0:4, 2 * P:3 * P]).then_inc(s["v_out"], 16)
            sp.dma_start(T.d["v_sample"][l, h], T.vt[0:NS, 4, 2 * P:3 * P]).then_inc(s["v_out"], 16)
            sp.wait_ge(s["v_out"], 32)
            sp.wait_ge(s["small_in"], 32)

        @block.tensor
        def _(pe):
            pe.wait_ge(s["w_in"], 16)
            for t in range(TILES):
                for k in range(KD):
                    last = nc.tensor.matmul(bank(T, t)[:, 0:3 * P], tile(T.xn[:, k, :], t), T.wtm[:, k, :],
                                            start=(k == 0), stop=(k == KD - 1))
                last.then_inc(s["vproj"], 1)

        @block.scalar
        def _(act):
            for t in range(TILES):
                act.wait_ge(s["vproj"], t + 1)
                nc.scalar.copy(T.vt[:, t, :], bank(T, t)[:, 0:3 * P]).then_inc(s["vcopied"], 1)


def pe_state_products(nc, pe, T, s, values):
    pe.wait_ge(s["keys_ready"], 1)
    for t in range(4):
        last = nc.tensor.matmul(T.ps[:, t * P:(t + 1) * P], T.kt[:, t, :], values(t), start=True, stop=True)
    last.then_inc(s["u_prompt"], 1)
    pe_sample_state(nc, pe, T, s)


def pe_sample_state(nc, pe, T, s):
    pe.wait_ge(s["vx_ready"], 1)
    for a in range(2):
        last = nc.tensor.matmul(bank(T, 2 + a), T.kt[0:NS, 4, :],
                                T.vx[0:NS, 4 * a:4 * a + 4, :], start=True, stop=True)
    last.then_inc(s["u_sample"], 1)


def pe_outputs(nc, pe, T, s, values, q_prompt, q_sample):
    for t in range(4):
        o = T.ps[:, 4 * BANK + t * P:4 * BANK + (t + 1) * P]
        nc.tensor.matmul(o, values(t), tile(T.sc, t), start=True, stop=(t == 0))
        if t:
            nc.tensor.matmul(o, T.st[:, t, :], tile(q_prompt, t), start=False, stop=True)
    nc.tensor.matmul(bank(T, 5, P), values(4), tile(T.sc, 4), start=True, stop=False)
    for b in range(DEC_B):
        last = nc.tensor.matmul(bank(T, 5)[:, b * DEC_T:(b + 1) * DEC_T], T.s_in[:, b, :],
                                q_sample[:, SEQ + b * DEC_T:SEQ + (b + 1) * DEC_T],
                                start=False, stop=(b == DEC_B - 1))
    last.then_inc(s["o_ready"], 1)


def dve_spread_values(nc, T, s, values):
    nc.vector.tensor_tensor(T.vx[0:NS], values.unsqueeze(1).to_broadcast([NS, DEC_B, P]),
                            T.general[0:NS, C_BS:C_BS + DEC_B].unsqueeze(2).to_broadcast([NS, DEC_B, P]),
                            ALU.mult).then_inc(s["vx_ready"], 1)


def dve_prompt_states(nc, dve, T, s, link, decay):
    dve.wait_ge(s["u_prompt"], 1)
    link(nc.vector.tensor_copy(T.st[:, 1, :], T.ps[:, 0:P]))
    for t in range(1, 4):
        op = nc.vector.scalar_tensor_tensor(out=T.st[:, t + 1, :], in0=T.st[:, t, :], scalar=decay[:, t:t + 1],
                                            in1=T.ps[:, t * P:(t + 1) * P], op0=ALU.mult, op1=ALU.add)
        if t < 3:
            link(op)
    op.then_inc(s["st_ready"], 1)


def dve_sample_states(nc, dve, T, s, link, decay):
    dve.wait_ge(s["s_loaded"], 16)
    link(nc.vector.tensor_tensor(T.s_new[:], T.s_in[:], decay.unsqueeze(2).to_broadcast([P, DEC_B, P]), ALU.mult))
    dve.wait_ge(s["u_sample"], 1)
    nc.vector.tensor_tensor(T.s_new[:], T.s_new[:],
                            T.ps[:, 2 * BANK:4 * BANK].rearrange("p (s v) -> p s v", s=DEC_B),
                            ALU.add).then_inc(s["s_ready"], 1)


def sp_states(sp, T, s, l, h, prompt, sample):
    sp.wait_ge(s["st_ready"], 1)
    sp.dma_start(prompt[l, h], T.st[:, 4, :]).then_inc(s["states_out"], 16)
    sp.wait_ge(s["s_ready"], 1)
    sp.dma_start(sample[l, :, h].rearrange("s k v -> k s v"), T.s_new[:]).then_inc(s["states_out"], 16)
    sp.wait_ge(s["states_out"], 32)


def act_finish(nc, act, T, s):
    act.wait_ge(s["o_ready"], 1)
    nc.scalar.activation(T.wk[:, 1, 0:N], bank(T, 4, N), ACT.Square).then_inc(s["o_squared"], 1)
    act.wait_ge(s["o_mean"], 1)
    nc.scalar.activation(T.rs, T.rs, ACT.Sqrt).then_inc(s["o_root"], 1)


def pe_finish(nc, pe, T, s):
    pe.wait_ge(s["o_squared"], 1)
    wide_product(nc, T, 6, lambda k: T.ones, lambda k: T.wk[:, 1, :], 1).then_inc(s["o_summed"], 1)


def dve_finish(nc, dve, T, s, link, gain, slot, gate):
    dve.wait_ge(s["o_summed"], 1)
    nc.vector.tensor_scalar(T.rs, halves(T, 6), 1.0 / P, EPS, ALU.mult, ALU.add).then_inc(s["o_mean"], 1)
    dve.wait_ge(s["o_root"], 1)
    link(nc.vector.reciprocal(T.rs, T.rs))
    out = T.br[:, slot, :].rearrange("p a n -> p (a n)")
    link(nc.vector.scalar_tensor_tensor(out=two(out), in0=two(bank(T, 4, N)), scalar=gain, in1=T.rs,
                                        op0=ALU.mult, op1=ALU.mult))
    if gate is not None:
        link(nc.vector.tensor_tensor(out, out, gate[:, 0:N], ALU.mult))


FINISH = ("o_ready", "o_squared", "o_summed", "o_mean", "o_root", "chain_v")
STATES = ("keys_ready", "u_prompt", "u_sample", "vx_ready", "st_ready", "s_ready", "s_loaded", "states_out")


def load_sample_state(sp, T, s, l, h, state):
    sp.dma_start(T.s_in[:], state[l, :, h].rearrange("s k v -> k s v")).then_inc(s["s_loaded"], 16)


def retention_stage(nc, T, l, h, slot):
    q, k, g = T.pr[:, 0, :], T.pr[:, 1, :], T.pr[:, 2, :]
    qd = T.wk[:, 2, :]
    with stage(nc, *W_SEMS, "projected", "evicted", "scored", "turned", "sc_ready", *FINISH, *STATES) as (block, s):
        s["w"] = [s["w0"], s["w1"], s["w2"], s["w3"]]

        @block.sync
        def _(sp):
            load_head_weights(sp, T, s, l, h, (0, 1, 2))
            load_sample_state(sp, T, s, l, h, T.d["state_ret"])
            sp_states(sp, T, s, l, h, T.d["ret_prompt"], T.d["ret_sample"])

        @block.tensor
        def _(pe):
            project(nc, pe, T, s, 3)
            pe.wait_ge(s["evicted"], 2)
            for t in range(TILES):
                last = nc.tensor.matmul(tile(bank(T, 4, NP_), t), tile(k, t), tile(q, t), start=True, stop=True)
            last.then_inc(s["scored"], 1)
            for t in range(TILES):
                last = nc.tensor.transpose(tile(bank(T, 6, NP_), t), tile(k, t), T.ident)
            last.then_inc(s["turned"], 1)
            pe.wait_ge(s["evicted"], 3)
            pe_state_products(nc, pe, T, s, lambda t: T.vt[:, t, 0:P])
            pe.wait_ge(s["sc_ready"], 1)
            pe.wait_ge(s["st_ready"], 1)
            pe.wait_ge(s["s_loaded"], 16)
            pe_outputs(nc, pe, T, s, lambda t: T.vt[:, t, 0:P], qd, qd)
            pe_finish(nc, pe, T, s)

        @block.scalar
        def _(act):
            for c, (dst, func) in enumerate(((q, ACT.Copy), (k, ACT.Copy), (g, ACT.Silu))):
                act.wait_ge(s["projected"], c + 1)
                nc.scalar.activation(two(dst), halves(T, 2 * (c % 2)), func).then_inc(s["evicted"], 1)
            act_finish(nc, act, T, s)

        @block.vector
        def _(dve):
            link = chained(dve, s["chain_v"])
            dve_spread_values(nc, T, s, T.vt[0:NS, 4, 0:P])
            dve.wait_ge(s["turned"], 1)
            nc.vector.tensor_tensor(T.kt[:], bank(T, 6, NP_).rearrange("p (t k) -> p t k", t=TILES),
                                    T.hc[:, H_KD:H_KD + TILES].unsqueeze(2).to_broadcast([P, TILES, P]),
                                    ALU.mult).then_inc(s["keys_ready"], 1)
            link(nc.vector.tensor_tensor(qd, q, T.hc[:, H_QD:H_QD + NP_], ALU.mult))
            nc.vector.tensor_tensor(T.sc, bank(T, 4, NP_), T.hc[:, H_RM:H_RM + NP_], ALU.mult).then_inc(s["sc_ready"], 1)
            dve_prompt_states(nc, dve, T, s, link, T.hc[:, H_GT:H_GT + TILES])
            dve_sample_states(nc, dve, T, s, link, T.hc[:, H_G8:H_G8 + DEC_B])
            dve_finish(nc, dve, T, s, link, T.ph[:, Q_RN:Q_RN + 1], slot, g)


def hgrn_stage(nc, T, l, h, slot):
    q, f, g, sneg = (T.pr[:, i, :] for i in range(4))
    qf = [T.wk[:, 2 + r, :] for r in range(LEVELS + 1)]
    ke = [T.wk[:, 10 + r, :] for r in range(LEVELS + 1)]
    fd = T.wk[:, 1, :]
    masked = T.masked
    vt = lambda t: T.vt[:, t, P:2 * P]
    with stage(nc, *W_SEMS, "projected", "evicted", "lb_in", "lb_exp", "level_v", "level_a", "scored", "masked_",
               "summed_", "turned", "sc_ready", *FINISH, *STATES) as (block, s):
        s["w"] = [s["w0"], s["w1"], s["w2"], s["w3"]]

        def blocks(ap, r):
            return ap.rearrange("p (n two b) -> p n two b", two=2, b=1 << r)

        @block.sync
        def _(sp):
            load_head_weights(sp, T, s, l, h, (3, 4, 5))
            load_sample_state(sp, T, s, l, h, T.d["state_hgrn"])
            sp_states(sp, T, s, l, h, T.d["hgrn_prompt"], T.d["hgrn_sample"])

        @block.tensor
        def _(pe):
            project(nc, pe, T, s, 3)
            pe.wait_ge(s["evicted"], 4)
            pe.wait_ge(s["level_v"], LEVELS + 1)
            pe.wait_ge(s["level_a"], LEVELS)
            for t in range(TILES):
                n = 1 + (LEVELS if t < 4 else 3)
                b = 2 * (t % 2)
                if t >= 2:
                    pe.wait_ge(s["masked_"], t - 1)
                for i in range(n):
                    lhs, rhs = (ke[0], q) if i == 0 else (ke[i - 1], qf[i - 1])
                    last = nc.tensor.matmul(T.ps[:, b * BANK + i * P:b * BANK + (i + 1) * P],
                                            tile(lhs, t), tile(rhs, t), start=True, stop=True)
                last.then_inc(s["scored"], 1)
            for t in range(TILES):
                last = nc.tensor.transpose(tile(bank(T, 6, NP_), t), tile(ke[LEVELS if t < 4 else 3], t), T.ident)
            last.then_inc(s["turned"], 1)
            pe.wait_ge(s["masked_"], TILES)
            pe_state_products(nc, pe, T, s, vt)
            pe.wait_ge(s["sc_ready"], TILES)
            pe.wait_ge(s["st_ready"], 1)
            pe.wait_ge(s["s_loaded"], 16)
            pe_outputs(nc, pe, T, s, vt, qf[LEVELS], qf[3])
            pe_finish(nc, pe, T, s)

        @block.scalar
        def _(act):
            act.wait_ge(s["lb_in"], 1)
            nc.scalar.activation(T.lb[:, 0:2], T.lb[:, 0:2], ACT.Exp).then_inc(s["lb_exp"], 1)
            act.wait_ge(s["projected"], 1)
            nc.scalar.activation(two(q), halves(T, 0), ACT.Copy, scale=K_SCALE).then_inc(s["evicted"], 1)
            act.wait_ge(s["projected"], 2)
            nc.scalar.activation(two(f), halves(T, 2), ACT.Sigmoid).then_inc(s["evicted"], 1)
            act.wait_ge(s["evicted"], 2)
            nc.scalar.activation(two(sneg), halves(T, 2), ACT.Sigmoid, scale=-1.0).then_inc(s["evicted"], 1)
            act.wait_ge(s["projected"], 3)
            nc.scalar.activation(two(g), halves(T, 0), ACT.Silu).then_inc(s["evicted"], 1)
            for r in range(LEVELS):
                act.wait_ge(s["level_v"], r + 1)
                if r:
                    act.wait_ge(s["level_a"], r)
                nc.scalar.copy(blocks(qf[r + 1], r)[:, :, 0, :], blocks(qf[r], r)[:, :, 0, :])
                nc.scalar.copy(blocks(ke[r + 1], r)[:, :, 1, :], blocks(ke[r], r)[:, :, 1, :]).then_inc(s["level_a"], 1)
            act_finish(nc, act, T, s)

        @block.vector
        def _(dve):
            link = chained(dve, s["chain_v"])
            dve_spread_values(nc, T, s, T.vt[0:NS, 4, P:2 * P])
            lg, lb = T.ph[:, Q_LB:Q_LB + 2], T.lb
            link(nc.vector.tensor_reduce(lb[:, 2:3], lg, AX_X, ALU.max))
            nc.vector.tensor_scalar(lb[:, 0:2], lg, lb[:, 2:3], None, ALU.subtract).then_inc(s["lb_in"], 1)
            dve.wait_ge(s["lb_exp"], 1)
            link(nc.vector.tensor_reduce(lb[:, 2:3], lb[:, 0:2], AX_X, ALU.add))
            link(nc.vector.reciprocal(lb[:, 2:3], lb[:, 2:3]))
            link(nc.vector.tensor_scalar(lb[:, 0:2], lb[:, 0:2], lb[:, 2:3], None, ALU.mult))
            link(nc.vector.tensor_tensor(lb[:, 1:2], lb[:, 0:1], lb[:, 1:2], ALU.add))
            link(nc.vector.tensor_tensor(lb[:, 1:2], lb[:, 1:2], lb[:, 0:1], ALU.subtract))
            link(nc.vector.tensor_tensor(lb[:, 1:2], lb[:, 1:2], T.pl[:, L_LB:L_LB + 1], ALU.mult))
            link(nc.vector.tensor_scalar(lb[:, 3:4], lb[:, 1:2], -1.0, 1.0, ALU.mult, ALU.add))
            dve.wait_ge(s["evicted"], 3)
            link(nc.vector.tensor_scalar(fd, f, lb[:, 3:4], lb[:, 1:2], ALU.mult, ALU.add))
            link(nc.vector.tensor_scalar(ke[0], sneg, lb[:, 3:4], None, ALU.mult))
            nc.vector.tensor_tensor(qf[0], q, fd, ALU.mult).then_inc(s["level_v"], 1)
            tot = fd
            at = 0
            for r in range(LEVELS):
                nb = NP_ >> (r + 1)
                pair = tot.rearrange("p (n two) -> p n two", two=2)
                if r:
                    dve.wait_ge(s["level_a"], r)
                else:
                    dve.wait_ge(s["level_v"], 1)
                wide = lambda c: pair[:, :, c].unsqueeze(2).to_broadcast([P, nb, 1 << r])
                nxt = T.tot[:, at:at + nb]
                link(nc.vector.tensor_tensor(nxt, pair[:, :, 0], pair[:, :, 1], ALU.mult))
                link(nc.vector.tensor_tensor(blocks(qf[r + 1], r)[:, :, 1, :], blocks(qf[r], r)[:, :, 1, :],
                                             wide(0), ALU.mult))
                link(nc.vector.tensor_tensor(blocks(ke[r + 1], r)[:, :, 0, :], blocks(ke[r], r)[:, :, 0, :],
                                             wide(1), ALU.mult))
                dve.sem_inc(s["level_v"], 1)
                tot = nxt
                if r == 2:
                    tot8 = T.tot[:, at + SEQ // 8:at + SEQ // 8 + DEC_B]
                at += nb
            for t in range(TILES):
                n = 1 + (LEVELS if t < 4 else 3)
                b = 2 * (t % 2)
                dve.wait_ge(s["scored"], t + 1)
                nc.vector.tensor_tensor(masked[:, 0:n * P], T.ps[:, b * BANK:b * BANK + n * P],
                                        T.general[:, C_MSK:C_MSK + n * P], ALU.mult).then_inc(s["masked_"], 1)
                dve.wait_ge(s["masked_"], t + 1)
                link(nc.vector.tensor_reduce(tile(T.sc, t), masked[:, 0:n * P].rearrange("p (m i) -> p i m", m=n),
                                             AX_X, ALU.add))
                dve.sem_inc(s["sc_ready"], 1)
            dve.wait_ge(s["turned"], 1)
            nc.vector.tensor_copy(T.kt[:], bank(T, 6, NP_).rearrange("p (t k) -> p t k", t=TILES)
                                  ).then_inc(s["keys_ready"], 1)
            dve_prompt_states(nc, dve, T, s, link, tot)
            dve_sample_states(nc, dve, T, s, link, tot8)
            dve_finish(nc, dve, T, s, link, T.ph[:, Q_HN:Q_HN + 1], slot, g)


def gdn_stage(nc, T, l, h, slot):
    q, k, v, g = (T.pr[:, i, :] for i in range(4))
    w = lambda i: T.wk[:, i, :]
    xp = [w(2), w(3), w(4)]
    sq = [w(5), w(6)]
    lgb, btb = w(7), w(8)
    dec, ec, bmat = w(9), w(10), w(11)
    boff, rr, rt, wz = w(12), w(13), w(14), w(15)
    qe, bv, delta, xr, kss = w(16), w(2), w(3), w(4), w(5)
    mask = lambda i: T.general[:, C_MSK + i * P:C_MSK + (i + 1) * P]
    tiled = lambda ap, n=TILES: ap[:, 0:n * P].rearrange("p (t i) -> p t i", t=n)
    col, ecol, tcol, kcol, becol = (T.cols[:, i * TILES:(i + 1) * TILES] for i in range(5))
    d8 = T.cols[:, 5 * TILES:5 * TILES + DEC_B]
    names = ("projected", "evicted", "copied", "hist_in", "conv_done", "silu_done", "sq_done", "ss_done", "ss_eps",
             "ss_root", "qk_ready", "lgb_ready", "cum_done", "col_done", "dec_in", "dec_exp", "exp_done", "scored",
             "betab_done", "b_ready", "turned", "vt_ready", "r1_ready", "rt_turned", "rt_ready", "boff_ready",
             "w_done", "w_out", "z_done", "level_done", "kt_turned", "ks_done", "x_ready", "delta_done",
             "delta_ready", "u_done", "st_step", "kss_done", "kss_copied", "kss_turned", "sc_ready", "conv_out",
             "small_done", "cols_done", "ec_done")
    with stage(nc, *W_SEMS, *names, *FINISH, *STATES) as (block, s):
        s["w"] = [s["w0"], s["w1"], s["w2"], s["w3"]]

        def hist(c):
            return xp[c][:, SEQ + 3:SEQ + 3 + DEC_B * (DEC_T + 3)].rearrange("p (s t) -> p s t", s=DEC_B)

        @block.sync
        def _(sp):
            load_head_weights(sp, T, s, l, h, (6, 7, 8, 9))
            for c in range(3):
                sp.dma_start(hist(c)[:, :, 0:3], T.d["conv_in"][l, h, c]).then_inc(s["hist_in"], 16)
            load_sample_state(sp, T, s, l, h, T.d["state_gdn"])
            sp.wait_ge(s["hist_in"], 48)
            sp.wait_ge(s["copied"], 9)
            for c in range(3):
                sp.dma_start(T.d["conv_prompt"][l, h, c], xp[c][:, SEQ:SEQ + 3]).then_inc(s["conv_out"], 16)
                sp.dma_start(T.d["conv_sample"][l, h, c], hist(c)[:, :, DEC_T:DEC_T + 3]).then_inc(s["conv_out"], 16)
            sp.wait_ge(s["conv_out"], 96)
            sp_states(sp, T, s, l, h, T.d["gdn_prompt"], T.d["gdn_sample"])

        @block.tensor
        def _(pe):
            project(nc, pe, T, s, 4)
            pe.wait_ge(s["lgb_ready"], 1)
            ut = lambda t: T.general[:, C_UT + t * P:C_UT + (t + 1) * P]
            for t in range(TILES):
                last = nc.tensor.matmul(tile(bank(T, 4, NP_), t), tile(lgb, t), ut(t), start=True, stop=True)
            last.then_inc(s["cum_done"], 1)
            one = lambda c: bank(T, 6)[:, c:c + 1]
            for t in range(TILES):
                nc.tensor.matmul(one(t), ut(t), T.lgh[:, t, :], start=True, stop=True)
                total = T.ones if t < 4 else T.general[:, C_BLK:C_BLK + P]
                nc.tensor.matmul(one(TILES + t), total, T.lgh[:, t, :], start=True, stop=True)
            nc.tensor.matmul(bank(T, 6)[:, 2 * TILES:2 * TILES + DEC_B], tile(lgb, 4), T.general[:, C_BS:C_BS + DEC_B],
                             start=True, stop=True).then_inc(s["col_done"], 1)
            pe.wait_ge(s["evicted"], 4)
            for c in range(2):
                pe.wait_ge(s["sq_done"], c + 1)
                wide_product(nc, T, 2 * c, lambda kk: T.ones, lambda kk: sq[c], 1).then_inc(s["ss_done"], 1)
            pe.wait_ge(s["exp_done"], 1)
            for t in range(TILES):
                last = nc.tensor.matmul(tile(bank(T, 4, NP_), t), tile(btb, t), T.ident, start=True, stop=True)
            last.then_inc(s["betab_done"], 1)
            pe.wait_ge(s["qk_ready"], 2)
            for i, rhs in enumerate((k, q)):
                for t in range(TILES):
                    last = nc.tensor.matmul(tile(bank(T, 2 * i, NP_), t), tile(k, t), tile(rhs, t), start=True, stop=True)
                last.then_inc(s["scored"], 1)
            pe.wait_ge(s["cols_done"], 1)
            for t in range(TILES):
                last = nc.tensor.transpose(tile(bank(T, 6, NP_), t), tile(v, t), T.ident)
            last.then_inc(s["turned"], 1)
            pe.wait_ge(s["r1_ready"], 1)
            for t in range(TILES):
                last = nc.tensor.transpose(tile(bank(T, 4, NP_), t), tile(rr, t), T.ident)
            last.then_inc(s["rt_turned"], 1)
            for r in range(1, LEVELS):
                n = TILES if r < 3 else 4
                pe.wait_ge(s["boff_ready"], r)
                pe.wait_ge(s["rt_ready"], r)
                for t in range(n):
                    last = nc.tensor.matmul(tile(bank(T, 0, NP_), t), tile(boff, t), tile(rt, t), start=True, stop=True)
                last.then_inc(s["w_done"], 1)
                pe.wait_ge(s["w_out"], r)
                for t in range(n):
                    nc.tensor.matmul(tile(bank(T, 2, NP_), t), tile(wz, t), tile(rr, t), start=True, stop=True)
                for t in range(n):
                    last = nc.tensor.matmul(tile(bank(T, 4, NP_), t), tile(rr, t), tile(wz, t), start=True, stop=True)
                last.then_inc(s["z_done"], 1)
            pe.wait_ge(s["vt_ready"], 1)
            for t in range(TILES):
                last = nc.tensor.transpose(tile(bank(T, 6, NP_), t), tile(k, t), T.ident)
            last.then_inc(s["kt_turned"], 1)
            pe.wait_ge(s["s_loaded"], 16)
            pe.wait_ge(s["level_done"], 1)
            for b in range(DEC_B):
                last = nc.tensor.matmul(bank(T, 4)[:, b * DEC_T:(b + 1) * DEC_T], T.s_in[:, b, :],
                                        k[:, SEQ + b * DEC_T:SEQ + (b + 1) * DEC_T], start=True, stop=True)
            last.then_inc(s["kss_done"], 1)
            pe.wait_ge(s["kss_copied"], 1)
            nc.tensor.transpose(bank(T, 5, P), kss[:, 0:P], T.ident).then_inc(s["kss_turned"], 1)
            pe.wait_ge(s["keys_ready"], 1)
            for t in range(4):
                if t:
                    pe.wait_ge(s["st_step"], t)
                    nc.tensor.matmul(bank(T, 0, P), tile(k, t), T.st[:, t, :], start=True, stop=True).then_inc(s["ks_done"], 1)
                pe.wait_ge(s["x_ready"], t + 1)
                nc.tensor.matmul(bank(T, 1, P), tile(rr, t), tile(xr, t), start=True, stop=True).then_inc(s["delta_done"], 1)
                pe.wait_ge(s["delta_ready"], t + 1)
                nc.tensor.matmul(bank(T, 6, P), T.kt[:, t, :], tile(delta, t), start=True, stop=True).then_inc(s["u_done"], 1)
            pe.wait_ge(s["x_ready"], 5)
            nc.tensor.matmul(bank(T, 1, P), tile(rr, 4), tile(xr, 4), start=True, stop=True).then_inc(s["delta_done"], 1)
            pe_sample_state(nc, pe, T, s)
            pe.wait_ge(s["sc_ready"], 1)
            pe.wait_ge(s["st_ready"], 1)
            pe_outputs(nc, pe, T, s, lambda t: tile(delta, t), qe, qe)
            pe_finish(nc, pe, T, s)

        @block.scalar
        def _(act):
            for c in range(3):
                act.wait_ge(s["projected"], c + 1)
                b = 2 * (c % 2)
                nc.scalar.copy(xp[c][:, 3:3 + HALF], bank(T, b)[:, 0:HALF]).then_inc(s["copied"], 1)
                nc.scalar.copy(xp[c][:, 3 + HALF:3 + SEQ], bank(T, b + 1)[:, 0:SEQ - HALF]).then_inc(s["copied"], 1)
                nc.scalar.copy(hist(c)[:, :, 3:3 + DEC_T],
                               bank(T, b + 1)[:, SEQ - HALF:HALF].rearrange("p (s t) -> p s t", s=DEC_B)
                               ).then_inc(s["copied"], 1)
                act.wait_ge(s["copied"], 3 * c + 3)
                act.sem_inc(s["evicted"], 1)
            act.wait_ge(s["projected"], 4)
            nc.scalar.activation(two(g), halves(T, 2), ACT.Silu).then_inc(s["evicted"], 1)
            for c, dst in enumerate((q, k, v)):
                act.wait_ge(s["conv_done"], c + 1)
                nc.scalar.activation(dst[:, 0:N], dst[:, 0:N], ACT.Silu).then_inc(s["silu_done"], 1)
            act.wait_ge(s["silu_done"], 3)
            for c, src in enumerate((q, k)):
                nc.scalar.activation(sq[c][:, 0:N], src[:, 0:N], ACT.Square).then_inc(s["sq_done"], 1)
            for c in range(2):
                act.wait_ge(s["ss_eps"], c + 1)
                nc.scalar.activation(sq[c][:, 0:N], sq[c][:, 0:N], ACT.Sqrt).then_inc(s["ss_root"], 1)
            act.wait_ge(s["cum_done"], 1)
            nc.scalar.activation(ec, bank(T, 4, NP_), ACT.Exp).then_inc(s["ec_done"], 1)
            act.wait_ge(s["dec_in"], 1)
            nc.scalar.activation(dec, dec, ACT.Exp).then_inc(s["dec_exp"], 1)
            act.wait_ge(s["small_done"], 1)
            nc.scalar.activation(ecol, col, ACT.Exp)
            nc.scalar.activation(kcol, kcol, ACT.Exp)
            nc.scalar.activation(tcol, tcol, ACT.Exp)
            nc.scalar.activation(d8, d8, ACT.Exp).then_inc(s["exp_done"], 1)
            act.wait_ge(s["rt_turned"], 1)
            nc.scalar.copy(rt, bank(T, 4, NP_)).then_inc(s["rt_ready"], 1)
            for r in range(1, LEVELS):
                n = TILES if r < 3 else 4
                act.wait_ge(s["w_done"], r)
                nc.scalar.copy(wz[:, 0:n * P], bank(T, 0, n * P)).then_inc(s["w_out"], 1)
            act.wait_ge(s["kss_done"], 1)
            nc.scalar.copy(kss[:, 0:NS], bank(T, 4)[:, 0:NS]).then_inc(s["kss_copied"], 1)
            for t in range(TILES):
                act.wait_ge(s["delta_done"], t + 1)
                nc.scalar.copy(tile(delta, t), bank(T, 1, P)).then_inc(s["delta_ready"], 1)
            act_finish(nc, act, T, s)

        @block.vector
        def _(dve):
            link = chained(dve, s["chain_v"])
            wide = lambda ap: ap.unsqueeze(2).to_broadcast([P, TILES, P])
            link(nc.vector.tensor_copy(T.lgh, T.logg[:, :, bass.ds(h, 1)]))
            link(nc.vector.tensor_copy(T.bth, T.beta[:, :, bass.ds(h, 1)]))
            nc.vector.tensor_copy(tiled(btb), wide(T.bth[:, :, 0]))
            nc.vector.tensor_copy(tiled(lgb), wide(T.lgh[:, :, 0])).then_inc(s["lgb_ready"], 1)
            for c in range(3):
                link(nc.vector.memset(xp[c][:, 0:3], 0.0))
            dve.wait_ge(s["hist_in"], 48)
            for c, dst in enumerate((q, k, v)):
                dve.wait_ge(s["copied"], 3 * c + 3)
                tap = lambda j: T.ph[:, Q_CONV + 4 * c + j:Q_CONV + 4 * c + j + 1]
                ds = dst[:, SEQ:N].rearrange("p (s t) -> p s t", s=DEC_B)
                nc.vector.tensor_scalar(dst[:, 0:SEQ], xp[c][:, 0:SEQ], tap(0), None, ALU.mult)
                link(nc.vector.tensor_scalar(ds, hist(c)[:, :, 0:DEC_T], tap(0), None, ALU.mult))
                for j in range(1, 4):
                    nc.vector.scalar_tensor_tensor(out=dst[:, 0:SEQ], in0=xp[c][:, j:j + SEQ], scalar=tap(j),
                                                   in1=dst[:, 0:SEQ], op0=ALU.mult, op1=ALU.add)
                    link(nc.vector.scalar_tensor_tensor(out=ds, in0=hist(c)[:, :, j:j + DEC_T], scalar=tap(j),
                                                        in1=ds, op0=ALU.mult, op1=ALU.add))
                dve.sem_inc(s["conv_done"], 1)
            for c, dst in enumerate((q, k)):
                dve.wait_ge(s["ss_done"], c + 1)
                nc.vector.tensor_scalar(two(sq[c]), halves(T, 2 * c), EPS, None, ALU.add).then_inc(s["ss_eps"], 1)
            for c, dst in enumerate((q, k)):
                dve.wait_ge(s["ss_root"], c + 1)
                link(nc.vector.reciprocal(sq[c][:, 0:N], sq[c][:, 0:N]))
                nc.vector.scalar_tensor_tensor(out=dst[:, 0:N], in0=dst[:, 0:N], scalar=K_SCALE if c == 0 else 1.0,
                                               in1=sq[c][:, 0:N], op0=ALU.mult, op1=ALU.mult).then_inc(s["qk_ready"], 1)
            dve.wait_ge(s["cum_done"], 1)
            dve.wait_ge(s["col_done"], 1)
            link(nc.vector.tensor_copy(col, bank(T, 6)[:, 0:TILES]))
            link(nc.vector.tensor_copy(tcol, bank(T, 6)[:, TILES:2 * TILES]))
            link(nc.vector.tensor_copy(d8, bank(T, 6)[:, 2 * TILES:2 * TILES + DEC_B]))
            dve.sem_inc(s["cols_done"], 1)
            link(nc.vector.tensor_tensor(kcol, tcol, col, ALU.subtract))
            dve.sem_inc(s["small_done"], 1)
            dve.wait_ge(s["ec_done"], 1)
            for t in range(TILES):
                last = nc.vector.tensor_scalar(tile(dec, t), tile(bank(T, 4, NP_), t), col[:, t:t + 1], 0.0,
                                               ALU.subtract, ALU.min)
            last.then_inc(s["dec_in"], 1)
            dve.wait_ge(s["dec_exp"], 1)
            link(nc.vector.tensor_tensor(dec, dec, T.general[:, C_UT:C_UT + NP_], ALU.mult))
            dve.wait_ge(s["exp_done"], 1)
            dve.wait_ge(s["betab_done"], 1)
            dve.wait_ge(s["scored"], 1)
            link(nc.vector.tensor_tensor(bmat, bank(T, 0, NP_), dec, ALU.mult))
            link(nc.vector.tensor_tensor(bmat, bmat, bank(T, 4, NP_), ALU.mult))
            dve.wait_ge(s["scored"], 2)
            link(nc.vector.tensor_tensor(T.sc, bank(T, 2, NP_), dec, ALU.mult))
            dve.sem_inc(s["sc_ready"], 1)
            spread = lambda i, n=TILES: mask(i).unsqueeze(1).to_broadcast([P, n, P])
            link(nc.vector.tensor_tensor(tiled(rr), tiled(bmat), spread(1), ALU.mult))
            link(nc.vector.scalar_tensor_tensor(out=tiled(rr), in0=tiled(rr), scalar=-1.0, in1=spread(0),
                                                op0=ALU.mult, op1=ALU.add))
            dve.sem_inc(s["r1_ready"], 1)
            dve.wait_ge(s["turned"], 1)
            dve.wait_ge(s["conv_out"], 96)
            nc.vector.tensor_tensor(tiled(bv), bank(T, 6, NP_).rearrange("p (t i) -> p t i", t=TILES),
                                    wide(T.bth[:, :, 0]), ALU.mult).then_inc(s["vt_ready"], 1)
            link(nc.vector.tensor_tensor(qe, q, ec, ALU.mult))
            link(nc.vector.scalar_tensor_tensor(out=becol, in0=ecol, scalar=-1.0, in1=T.bth[:, :, 0],
                                                op0=ALU.mult, op1=ALU.mult))
            link(nc.vector.memset(kss, 0.0))
            for r in range(1, LEVELS):
                n = TILES if r < 3 else 4
                nc.vector.tensor_tensor(tiled(boff, n), tiled(bmat, n), spread(1 + r, n), ALU.mult
                                        ).then_inc(s["boff_ready"], 1)
                dve.wait_ge(s["z_done"], r)
                link(nc.vector.tensor_tensor(rr[:, 0:n * P], rr[:, 0:n * P], bank(T, 2, n * P), ALU.subtract))
                link(nc.vector.tensor_tensor(rt[:, 0:n * P], rt[:, 0:n * P], bank(T, 4, n * P), ALU.subtract))
                dve.sem_inc(s["rt_ready"], 1)
                if r == LEVELS - 1:
                    dve.sem_inc(s["level_done"], 1)
            dve.wait_ge(s["kt_turned"], 1)
            nc.vector.tensor_tensor(T.kt[:], bank(T, 6, NP_).rearrange("p (t i) -> p t i", t=TILES), wide(kcol),
                                    ALU.mult).then_inc(s["keys_ready"], 1)
            dve.wait_ge(s["keys_ready"], 1)
            for t in range(4):
                if t == 0:
                    nc.vector.tensor_copy(tile(xr, 0), tile(bv, 0)).then_inc(s["x_ready"], 1)
                else:
                    dve.wait_ge(s["ks_done"], t)
                    nc.vector.scalar_tensor_tensor(out=tile(xr, t), in0=bank(T, 0, P), scalar=becol[:, t:t + 1],
                                                   in1=tile(bv, t), op0=ALU.mult, op1=ALU.add).then_inc(s["x_ready"], 1)
                dve.wait_ge(s["u_done"], t + 1)
                if t == 0:
                    nc.vector.tensor_copy(T.st[:, 1, :], bank(T, 6, P)).then_inc(s["st_step"], 1)
                else:
                    nc.vector.scalar_tensor_tensor(out=T.st[:, t + 1, :], in0=T.st[:, t, :], scalar=tcol[:, t:t + 1],
                                                   in1=bank(T, 6, P), op0=ALU.mult, op1=ALU.add).then_inc(s["st_step"], 1)
                dve.wait_ge(s["st_step"], t + 1)
            dve.sem_inc(s["st_ready"], 1)
            dve.wait_ge(s["kss_turned"], 1)
            nc.vector.scalar_tensor_tensor(out=tile(xr, 4), in0=bank(T, 5, P), scalar=becol[:, 4:5],
                                           in1=tile(bv, 4), op0=ALU.mult, op1=ALU.add).then_inc(s["x_ready"], 1)
            dve.wait_ge(s["delta_ready"], 5)
            dve_spread_values(nc, T, s, delta[0:NS, 4 * P:5 * P])
            dve_sample_states(nc, dve, T, s, link, d8)
            dve_finish(nc, dve, T, s, link, T.ph[:, Q_GN:Q_GN + 1], slot, g)



def attention_stage(nc, T, l, h, slot):
    q, k = T.pr[:, 0, :], T.pr[:, 1, :]
    w = lambda i: T.wk[:, i, :]
    sq = [w(2), w(3)]
    score = [w(2), w(3)]
    prob = [w(4), w(5)]
    diag = [w(6)[:, 0:P], w(6)[:, P:2 * P]]
    at = w(7)
    qm = T.wk[:, 8:10, :].rearrange("p a b -> p (a b)")[:, 0:(DEC_B + 1) * P]
    kc = T.wk[:, 10:14, :].rearrange("p a b -> p (a b)")[:, 0:DEC_B * PAST]
    vc = T.wk[:, 14:18, :].rearrange("p a b -> p (a b)")[:, 0:DEC_B * PAST]
    mx, sm = T.cols[:, 0:2], T.cols[:, 2:4]
    vt = lambda t: T.vt[:, t, 2 * P:3 * P]
    dc = T.dc
    names = ("projected", "evicted", "dc_in", "pt_in", "kv_in", "sq_done", "ss_done", "ss_eps", "ss_root", "qk_ready",
             "k_out", "scored", "biased", "exp_in", "exped", "diag_ready", "turned", "at_ready", "o_tile",
             "qm_ready", "s_scored", "s_turned", "s_at")
    rounds = [(t, c) for t in range(4) for c in range(2)]
    with stage(nc, *W_SEMS, *names, *FINISH) as (block, s):
        s["w"] = [s["w0"], s["w1"], s["w2"], s["w3"]]

        @block.sync
        def _(sp):
            sp.dma_start(T.pt[0:1, :], T.d["page_table"]).then_inc(s["pt_in"], 16)
            load_head_weights(sp, T, s, l, h, (10, 11))
            sp.dma_start(dc, T.d["dc"]).then_inc(s["dc_in"], 16)
            sp.wait_ge(s["pt_in"], 16)
            with sp.Fori(0, DEC_B * PAGES) as i:
                page = sp.value_load(T.pt[0:1, bass.ds(i, 1)], min_val=0, max_val=N_PHYS - 1)
                sp.dma_start(kc[:, bass.ds(i * PAGE, PAGE)], T.d["cache_k"][l, page, h]).then_inc(s["kv_in"], 16)
                sp.dma_start(vc[:, bass.ds(i * PAGE, PAGE)], T.d["cache_v"][l, page, h]).then_inc(s["kv_in"], 16)
            sp.wait_ge(s["qk_ready"], 2)
            sp.dma_start(T.d["k_out"][l, h], k[:, 0:N]).then_inc(s["k_out"], 16)
            sp.wait_ge(s["k_out"], 16)

        @block.tensor
        def _(pe):
            project(nc, pe, T, s, 2)
            for c in range(2):
                pe.wait_ge(s["sq_done"], c + 1)
                wide_product(nc, T, 4 + 2 * c, lambda kk: T.general[:, C_COMP:C_COMP + P], lambda kk: sq[c],
                             1).then_inc(s["ss_done"], 1)
            pe.wait_ge(s["qk_ready"], 2)

            def scores(t, c):
                if t:
                    pe.wait_ge(s["biased"], 2 * (t - 1) + c + 1)
                rows = slice(c * DK, (c + 1) * DK)
                nc.tensor.matmul(bank(T, c)[:, 0:(t + 1) * P], tile(q, t)[rows], k[rows, 0:(t + 1) * P],
                                 start=True, stop=True).then_inc(s["scored"], 1)

            scores(0, 0)
            scores(0, 1)
            for t in range(4):
                pe.wait_ge(s["diag_ready"], 2 * (t + 1))
                for i in range(t + 1):
                    for c in range(2):
                        last = nc.tensor.matmul(tile(bank(T, 2), i), tile(prob[c], i), diag[c],
                                                start=(c == 0), stop=(c == 1))
                last.then_inc(s["turned"], 1)
                if t < 3:
                    scores(t + 1, 0)
                    scores(t + 1, 1)
                pe.wait_ge(s["at_ready"], t + 1)
                for i in range(t + 1):
                    last = nc.tensor.matmul(tile(bank(T, 4), t), vt(i), tile(at, i), start=(i == 0), stop=(i == t))
                last.then_inc(s["o_tile"], 1)
            pe.wait_ge(s["qm_ready"], 1)
            pe.wait_ge(s["kv_in"], 32 * DEC_B * PAGES)
            new = bank(T, 0)[:, PAST:PAST + NS]
            pe.wait_ge(s["biased"], 8)
            nc.tensor.matmul(new, qm[:, DEC_B * P:(DEC_B + 1) * P], k[:, SEQ:N], start=True, stop=True)
            for b in range(DEC_B):
                last = nc.tensor.matmul(bank(T, 0)[:, 0:PAST], tile(qm, b), kc[:, b * PAST:(b + 1) * PAST],
                                        start=(b == 0), stop=(b == DEC_B - 1))
            last.then_inc(s["s_scored"], 1)
            pe.wait_ge(s["diag_ready"], 9)
            for i in range(PAGES):
                nc.tensor.matmul(bank(T, 2)[:, i * NS:(i + 1) * NS], tile(prob[0], i), diag[0][:, 0:NS],
                                 start=True, stop=True)
            nc.tensor.matmul(bank(T, 2)[0:NS, PAGES * NS:(PAGES + 1) * NS], prob[0][:, PAST:PAST + NS],
                             diag[0][:, 0:NS], start=True, stop=True).then_inc(s["s_turned"], 1)
            pe.wait_ge(s["s_at"], 2)
            o = bank(T, 5)
            nc.tensor.matmul(o[:, 0:NS], T.vt[0:NS, 4, 2 * P:3 * P], at[0:NS, PAGES * NS:(PAGES + 1) * NS],
                             start=True, stop=False)
            for b in range(DEC_B):
                for i in range(PAGES):
                    last = nc.tensor.matmul(o[:, b * DEC_T:(b + 1) * DEC_T], tile(vc, b * PAGES + i),
                                            at[:, i * NS + b * DEC_T:i * NS + (b + 1) * DEC_T], start=False,
                                            stop=(b == DEC_B - 1 and i == PAGES - 1))
            last.then_inc(s["o_ready"], 1)
            pe_finish(nc, pe, T, s)

        @block.scalar
        def _(act):
            for c, dst in enumerate((q, k)):
                act.wait_ge(s["projected"], c + 1)
                nc.scalar.copy(two(dst), halves(T, 2 * c)).then_inc(s["evicted"], 1)
            for c in range(2):
                nc.scalar.activation(two(sq[c]), halves(T, 2 * c), ACT.Square).then_inc(s["sq_done"], 1)
            for c in range(2):
                act.wait_ge(s["ss_eps"], c + 1)
                nc.scalar.activation(sq[c][:, 0:N], sq[c][:, 0:N], ACT.Sqrt).then_inc(s["ss_root"], 1)
            for i, (t, c) in enumerate(rounds):
                act.wait_ge(s["exp_in"], i + 1)
                if t:
                    act.wait_ge(s["turned"], t)
                nc.scalar.activation(prob[c][:, 0:(t + 1) * P], score[c][:, 0:(t + 1) * P], ACT.Exp,
                                     bias=mx[:, c:c + 1], scale=S_SCALE, accum_out=sm[:, c:c + 1]).then_inc(s["exped"], 1)
                if c == 1:
                    act.wait_ge(s["turned"], t + 1)
                    if t:
                        act.wait_ge(s["o_tile"], t)
                    nc.scalar.copy(at[:, 0:(t + 1) * P], bank(T, 2)[:, 0:(t + 1) * P]).then_inc(s["at_ready"], 1)
            act.wait_ge(s["exp_in"], 9)
            nc.scalar.activation(prob[0][:, 0:PAST + NS], score[0][:, 0:PAST + NS], ACT.Exp, bias=mx[:, 0:1],
                                 scale=S_SCALE, accum_out=sm[:, 0:1]).then_inc(s["exped"], 1)
            act.wait_ge(s["s_turned"], 1)
            act.wait_ge(s["o_tile"], 4)
            nc.scalar.copy(at[:, 0:PAGES * NS], bank(T, 2)[:, 0:PAGES * NS]).then_inc(s["s_at"], 1)
            nc.scalar.copy(at[0:NS, PAGES * NS:(PAGES + 1) * NS],
                           bank(T, 2)[0:NS, PAGES * NS:(PAGES + 1) * NS]).then_inc(s["s_at"], 1)
            act_finish(nc, act, T, s)

        @block.vector
        def _(dve):
            link = chained(dve, s["chain_v"])
            for c in range(2):
                dve.wait_ge(s["ss_done"], c + 1)
                nc.vector.tensor_scalar(two(sq[c]), halves(T, 4 + 2 * c), 1.0 / DK, EPS, ALU.mult,
                                        ALU.add).then_inc(s["ss_eps"], 1)
            for c, dst in enumerate((q, k)):
                dve.wait_ge(s["ss_root"], c + 1)
                link(nc.vector.reciprocal(sq[c][:, 0:N], sq[c][:, 0:N]))
                nc.vector.scalar_tensor_tensor(out=dst[:, 0:N], in0=dst[:, 0:N],
                                               scalar=T.ph[:, Q_QN + c:Q_QN + c + 1], in1=sq[c][:, 0:N],
                                               op0=ALU.mult, op1=ALU.mult).then_inc(s["qk_ready"], 1)
            dve.wait_ge(s["qk_ready"], 2)
            dve.wait_ge(s["dc_in"], 16)
            slope = T.hc[:, H_SL:H_SL + 1]

            def softmax_input(i, c, dist, src, n):
                if i >= 2:
                    dve.wait_ge(s["exped"], min(i, 8) - 1 if i < 8 else 8)
                nc.vector.scalar_tensor_tensor(out=score[c][:, 0:n], in0=dist, scalar=slope, in1=src,
                                               op0=ALU.mult, op1=ALU.add).then_inc(s["biased"], 1)
                dve.wait_ge(s["biased"], i + 1)
                link(nc.vector.tensor_reduce(mx[:, c:c + 1], score[c][:, 0:n], AX_X, ALU.max))
                nc.vector.tensor_scalar(mx[:, c:c + 1], mx[:, c:c + 1], -S_SCALE, None, ALU.mult).then_inc(s["exp_in"], 1)

            for t in range(4):
                n = (t + 1) * P
                for c in range(2):
                    i = 2 * t + c
                    dve.wait_ge(s["scored"], i + 1)
                    softmax_input(i, c, dc[:, C_DP + SEQ - n:C_DP + SEQ], bank(T, c)[:, 0:n], n)
                for c in range(2):
                    i = 2 * t + c
                    dve.wait_ge(s["exped"], i + 1)
                    if t:
                        dve.wait_ge(s["turned"], t)
                    link(nc.vector.reciprocal(sm[:, c:c + 1], sm[:, c:c + 1]))
                    if c:
                        link(nc.vector.tensor_scalar(sm[:, 1:2], sm[:, 1:2], T.lam[:, 2:3], None, ALU.mult))
                    nc.vector.tensor_scalar(diag[c], T.ident, sm[:, c:c + 1], None, ALU.mult
                                            ).then_inc(s["diag_ready"], 1)
            nc.vector.tensor_tensor(qm.rearrange("p (a t) -> p a t", t=NS),
                                    q[:, SEQ:N].unsqueeze(1).to_broadcast([P, 2 * (DEC_B + 1), NS]),
                                    dc[:, C_QM:C_QM + (DEC_B + 1) * P].rearrange("p (a t) -> p a t", t=NS),
                                    ALU.mult).then_inc(s["qm_ready"], 1)
            dve.wait_ge(s["s_scored"], 1)
            softmax_input(8, 0, dc[:, C_DS:C_DS + PAST + NS], bank(T, 0)[:, 0:PAST + NS], PAST + NS)
            dve.wait_ge(s["exped"], 9)
            dve.wait_ge(s["turned"], 4)
            link(nc.vector.reciprocal(sm[:, 0:1], sm[:, 0:1]))
            link(nc.vector.tensor_scalar(sm[:, 0:1], sm[:, 0:1], T.lam[:, 3:4], None, ALU.mult))
            nc.vector.tensor_scalar(diag[0][:, 0:NS], dc[:, C_STK:C_STK + NS], sm[:, 0:1], None, ALU.mult
                                    ).then_inc(s["diag_ready"], 1)
            link(nc.vector.tensor_tensor(T.cols[:, 4:5], T.ph[:, Q_DN:Q_DN + 1], T.pl[:, L_OL:L_OL + 1], ALU.mult))
            dve_finish(nc, dve, T, s, link, T.cols[:, 4:5], slot, None)


def merge_stage(nc, T, l):
    with stage(nc, "w_even", "w_odd", "w_free", "gated", "sig_done", "added", "chain_v") as (block, s):
        w_in = (s["w_even"], s["w_odd"])

        @block.sync
        def _(sp):
            with sp.Fori(0, KD) as m:
                for b in range(4):
                    sp.wait_ge(s["w_free"], 4 * m + b + 1)
                    sp.dma_start(T.wm[:, b % 2], T.d["w_merge"][l, m, b]).then_inc(w_in[b % 2], 16)

        @block.tensor
        def _(pe):
            pe.sem_inc(s["w_free"], 2)
            with pe.Fori(0, KD) as m:
                for b in range(4):
                    i = b % 2
                    pe.wait_ge(w_in[i], 32 * m + 16 * (b // 2) + 16)
                    pe.wait_ge(s["added"], 4 * m + b + 1)
                    wide_product(nc, T, 4 * i, lambda k: T.wm[:, i, k, :], lambda k: T.xn[:, k, :], KD
                                 ).then_inc(s["gated"], 1)
                    wide_product(nc, T, 4 * i + 2, lambda k: T.wm[:, i, KD + k, :],
                                 lambda k: T.br[:, 4 * b + k, :], 4).then_inc(s["w_free"], 1)

        @block.scalar
        def _(act):
            with act.Fori(0, KD) as m:
                for b in range(4):
                    i = b % 2
                    act.wait_ge(s["gated"], 4 * m + b + 1)
                    act.wait_ge(s["added"], 4 * m + b + 1)
                    nc.scalar.activation(T.sg[i], halves(T, 4 * i), ACT.Sigmoid).then_inc(s["sig_done"], 1)

        @block.vector
        def _(dve):
            dve.sem_inc(s["added"], 2)
            with dve.Fori(0, KD) as m:
                for b in range(4):
                    i = b % 2
                    dve.wait_ge(s["sig_done"], 4 * m + b + 1)
                    dve.wait_ge(s["w_free"], 4 * m + b + 3)
                    if b == 0:
                        dve.wait_ge(s["added"], 4 * m + 2)
                        nc.vector.tensor_tensor(T.ma, T.sg[i], halves(T, 4 * i + 2), ALU.mult).then_inc(s["added"], 1)
                    else:
                        nc.vector.tensor_tensor(T.sg[i], T.sg[i], halves(T, 4 * i + 2), ALU.mult
                                                ).then_inc(s["chain_v"], 1)
                        dve.wait_ge(s["chain_v"], 3 * m + b)
                        dve.wait_ge(s["added"], 4 * m + b + 2)
                        out = T.ma if b < 3 else two(T.mt[:, bass.ds(m, 1), :].rearrange("p a n -> p (a n)"))
                        nc.vector.tensor_tensor(out, T.ma, T.sg[i], ALU.add).then_inc(s["added"], 1)


def out_stage(nc, T, l):
    with stage(nc, "w_even", "w_odd", "h_in", "produced", "added", "h_out") as (block, s):
        w_in = (s["w_even"], s["w_odd"])

        @block.sync
        def _(sp):
            sp.dma_start(T.h[:], T.d["xs"].rearrange("m p n -> p m n")).then_inc(s["h_in"], 16)
            with sp.Fori(0, KD // 2) as g:
                for i in range(2):
                    sp.wait_ge(s["produced"], 2 * g + i + 1)
                    sp.dma_start(T.wm[:, i, 0:KD, :], T.d["w_out"][l, 2 * g + i]).then_inc(w_in[i], 16)
            sp.wait_ge(s["added"], KD + 2)
            sp.dma_start(T.d["xs"].rearrange("m p n -> p m n"), T.h[:]).then_inc(s["h_out"], 16)
            sp.wait_ge(s["h_out"], 16)

        @block.tensor
        def _(pe):
            pe.sem_inc(s["produced"], 2)
            with pe.Fori(0, KD // 2) as g:
                for i in range(2):
                    pe.wait_ge(w_in[i], 16 * g + 16)
                    pe.wait_ge(s["added"], 2 * g + i + 1)
                    wide_product(nc, T, 2 * i, lambda k: T.wm[:, i, k, :], lambda k: T.mt[:, k, :], KD
                                 ).then_inc(s["produced"], 1)

        @block.vector
        def _(dve):
            dve.sem_inc(s["added"], 2)
            dve.wait_ge(s["h_in"], 16)
            with dve.Fori(0, KD // 2) as g:
                for i in range(2):
                    dve.wait_ge(s["produced"], 2 * g + i + 3)
                    row = two(T.h[:, bass.ds(2 * g + i, 1), :].rearrange("p a n -> p (a n)"))
                    nc.vector.tensor_tensor(row, row, halves(T, 2 * i), ALU.add).then_inc(s["added"], 1)


def key_scores_stage(nc, T, l):
    with stage(nc, "w_even", "w_odd", "keys_in", "w_free", "q_done", "q_out", "scored", "kept",
               "zeroed") as (block, s):
        w_in = (s["w_even"], s["w_odd"])

        @block.sync
        def _(sp):
            sp.dma_start(T.keys, T.d["keys"][l]).then_inc(s["keys_in"], 16)
            with sp.Fori(0, PH_HEADS) as g:
                for i in range(2):
                    sp.wait_ge(s["q_done"], 2 * g + i + 1)
                    sp.dma_start(T.wm2[:, i], T.d["w_query"][l, 2 * g + i]).then_inc(w_in[i], 16)

        @block.tensor
        def _(pe):
            pe.sem_inc(s["q_done"], 2)
            pe.wait_ge(s["keys_in"], 16)
            with pe.Fori(0, PH_HEADS) as g:
                for i in range(2):
                    pe.wait_ge(w_in[i], 16 * g + 16)
                    pe.wait_ge(s["q_out"], 2 * g + i + 1)
                    wide_product(nc, T, 2 * i, lambda k: T.wm2[:, i, k, :], lambda k: T.xn[:, k, :], KD
                                 ).then_inc(s["q_done"], 1)
                    pe.wait_ge(s["q_out"], 2 * g + i + 3)
                    pe.wait_ge(s["kept"], 2 * g + i + 1)
                    for t in range(TILES):
                        last = nc.tensor.matmul(tile(bank(T, 4 + 2 * i, NP_), t), tile(T.qt[i], t),
                                                T.keys[:, bass.ds(2 * g + i, 1), :].rearrange("p a n -> p (a n)"),
                                                start=True, stop=True)
                    last.then_inc(s["scored"], 1)

        @block.scalar
        def _(act):
            act.wait_ge(s["zeroed"], 1)
            act.sem_inc(s["q_out"], 2)
            with act.Fori(0, PH_HEADS) as g:
                for i in range(2):
                    act.wait_ge(s["q_done"], 2 * g + i + 3)
                    act.wait_ge(s["kept"], 2 * g + i + 1)
                    nc.scalar.copy(two(T.qt[i]), halves(T, 2 * i)).then_inc(s["q_out"], 1)

        @block.vector
        def _(dve):
            for i in range(2):
                last = nc.vector.memset(T.qt[i], 0.0)
            last.then_inc(s["zeroed"], 1)
            dve.sem_inc(s["kept"], 2)
            with dve.Fori(0, PH_HEADS) as g:
                for i in range(2):
                    dve.wait_ge(s["scored"], 2 * g + i + 1)
                    nc.vector.tensor_copy(T.scr[:, :, bass.ds(2 * g + i, 1), :],
                                          bank(T, 4 + 2 * i, NP_).rearrange("p (t a k) -> p t a k", t=TILES, a=1)
                                          ).then_inc(s["kept"], 1)


def retrieval_stage(nc, T, l):
    LOW = -3.0e38
    KK = TOPK * TOPK
    with stage(nc, "chain_v", "exp_in", "exped", "found", "turned", "split") as (block, s):
        S2 = 2 * PH_HEADS

        @block.vector
        def _(dve):
            count = [0]
            STEPS = 31

            def link(instruction, t):
                count[0] += 1
                instruction.then_inc(s["chain_v"], 1)
                dve.wait_ge(s["chain_v"], STEPS * t + count[0])

            def best(t, values, idx, scores):
                rows = range(scores.shape[1])
                v = nc.vector
                for r in range(2):
                    part = slice(8 * r, 8 * r + 8)
                    v.memset(T.spare, 0.0)
                    for j in rows:
                        last = v.max(values[:, j, part], scores[:, j, :])
                    link(last, t)
                    v.memset(T.spare, 0.0)
                    for j in rows:
                        last = v.max_index(idx[:, j, part], values[:, j, part], scores[:, j, :])
                    link(last, t)
                    if r == 0:
                        v.memset(T.spare, 0.0)
                        for j in rows:
                            last = v.match_replace(scores[:, j, :], values[:, j, part], scores[:, j, :], LOW)
                        link(last, t)

            with dve.Fori(0, TILES) as t:
                count[0] = 0
                link(nc.vector.tensor_copy(T.x1, T.scr[:, bass.ds(t, 1)].rearrange("p a h k -> p (a h) k")), t)
                best(t, T.t1, T.i1u, T.x1)
                link(nc.vector.tensor_copy(T.i1f, T.i1u), t)
                side = T.t1.rearrange("p (h z) a -> p h z a", z=2)
                link(nc.vector.tensor_tensor(
                    T.cand.rearrange("p h (a b) -> p h a b", a=TOPK),
                    side[:, :, 0, :].unsqueeze(3).to_broadcast([P, PH_HEADS, TOPK, TOPK]),
                    side[:, :, 1, :].unsqueeze(2).to_broadcast([P, PH_HEADS, TOPK, TOPK]), ALU.add), t)
                best(t, T.t2, T.posu, T.cand)
                nc.vector.tensor_tensor(T.gw, T.t2, T.t2[:, :, 0:1].to_broadcast([P, PH_HEADS, TOPK]),
                                        ALU.subtract).then_inc(s["exp_in"], 1)
                link(nc.vector.tensor_scalar(T.pau, T.posu, 4, None, ALU.logical_shift_right), t)
                link(nc.vector.tensor_scalar(T.pbu, T.posu, 15, None, ALU.bitwise_and), t)
                link(nc.vector.tensor_copy(T.paf, T.pau), t)
                link(nc.vector.tensor_copy(T.pbf, T.pbu), t)
                sidei = T.i1f.rearrange("p (h z) a -> p h z a", z=2)
                iota = T.iota[:, 0:TOPK].unsqueeze(1).to_broadcast([P, P, TOPK])
                for z, place in enumerate((T.paf, T.pbf)):
                    eq = T.eq
                    link(nc.vector.tensor_tensor(eq, place.rearrange("p h k -> p (h k)").unsqueeze(2).to_broadcast(
                        [P, P, TOPK]), iota, ALU.is_equal), t)
                    eq4 = eq.rearrange("p (h k) a -> p h k a", h=PH_HEADS)
                    link(nc.vector.tensor_tensor(eq4, eq4, sidei[:, :, z, :].unsqueeze(2).to_broadcast(
                        [P, PH_HEADS, TOPK, TOPK]), ALU.mult), t)
                    link(nc.vector.tensor_reduce(T.found[:, z, :], eq, AX_X, ALU.add), t)
                dve.wait_ge(s["exped"], t + 1)
                link(nc.vector.tensor_reduce(T.gs, T.gw, AX_X, ALU.add), t)
                link(nc.vector.reciprocal(T.gs, T.gs), t)
                link(nc.vector.tensor_tensor(T.found[:, 2, :].rearrange("p (h k) -> p h k", h=PH_HEADS), T.gw,
                                             T.gs.unsqueeze(2).to_broadcast([P, PH_HEADS, TOPK]), ALU.mult), t)
                dve.sem_inc(s["found"], 1)
                dve.wait_ge(s["turned"], t + 1)
                cols = bass.ds(t * P, P)
                nc.vector.tensor_copy(T.idx[:, 0, cols], bank(T, 0)[:, 0:P])
                nc.vector.tensor_copy(T.idx[:, 1, cols], bank(T, 0)[:, P:2 * P])
                link(nc.vector.tensor_copy(T.gp[:, 0, :], bank(T, 0)[:, 2 * P:3 * P]), t)
                link(nc.vector.tensor_tensor(T.gr, bank(T, 0)[:, 2 * P:3 * P], T.gp[:, 0, :], ALU.subtract), t)
                link(nc.vector.tensor_copy(T.gp[:, 1, :], T.gr), t)
                link(nc.vector.tensor_tensor(T.gr, T.gr, T.gp[:, 1, :], ALU.subtract), t)
                link(nc.vector.tensor_copy(T.gp[:, 2, :], T.gr), t)
                nc.vector.tensor_copy(T.idx[:, 2:5, cols], T.gp).then_inc(s["split"], 1)
                dve.wait_ge(s["split"], t + 1)
                assert count[0] == STEPS

        @block.scalar
        def _(act):
            with act.Fori(0, TILES) as t:
                act.wait_ge(s["exp_in"], t + 1)
                nc.scalar.activation(T.gw, T.gw, ACT.Exp).then_inc(s["exped"], 1)

        @block.tensor
        def _(pe):
            with pe.Fori(0, TILES) as t:
                pe.wait_ge(s["found"], t + 1)
                for i in range(3):
                    last = nc.tensor.transpose(tile(bank(T, 0), i), T.found[:, i, :], T.ident)
                last.then_inc(s["turned"], 1)


def coefficient_stage(nc, T, l, hf):
    STEPS = N // GT
    with stage(nc, "iota_ready", "ids_ready", "first_ready", "second_ready", "summed", "kept") as (block, s):
        @block.vector
        def _(dve):
            nc.vector.tensor_copy(T.iota_h, T.iota[:, bass.ds(hf * HJ, HJ)]).then_inc(s["iota_ready"], 1)
            dve.wait_ge(s["iota_ready"], 1)
            dve.sem_inc(s["summed"], 1)
            dve.sem_inc(s["second_ready"], 1)
            with dve.Fori(0, STEPS) as g:
                dve.wait_ge(s["second_ready"], g + 1)
                nc.vector.tensor_copy(T.ids, T.idx[:, :, bass.ds(g * GT, GT)]).then_inc(s["ids_ready"], 1)
                dve.wait_ge(s["ids_ready"], g + 1)
                dve.wait_ge(s["summed"], g + 1)
                for n in range(GT):
                    last = nc.vector.tensor_scalar(T.oh1[:, n, :], T.iota_b, T.ids[:, 0, n:n + 1], None, ALU.is_equal)
                    for i in range(3):
                        last = nc.vector.tensor_scalar(T.oh2[:, n, i, :], T.iota_h, T.ids[:, 1, n:n + 1],
                                                       T.ids[:, 2 + i, n:n + 1], ALU.is_equal, ALU.mult)
                last.then_inc(s["second_ready"], 1)

        @block.tensor
        def _(pe):
            pe.sem_inc(s["kept"], 1)
            with pe.Fori(0, STEPS) as g:
                pe.wait_ge(s["second_ready"], g + 2)
                pe.wait_ge(s["kept"], g + 1)
                for n in range(GT):
                    for i in range(3):
                        last = nc.tensor.matmul(bank(T, 0)[:, n * HJ:(n + 1) * HJ], T.oh1[:, n, :], T.oh2[:, n, i, :],
                                                start=(i == 0), stop=(i == 2))
                last.then_inc(s["summed"], 1)

        @block.scalar
        def _(act):
            with act.Fori(0, STEPS) as g:
                act.wait_ge(s["summed"], g + 2)
                nc.scalar.copy(T.g[:, :, bass.ds(g * GT, GT)],
                               bank(T, 0).rearrange("p (n i) -> p i n", n=GT)).then_inc(s["kept"], 1)


def expert_in_stage(nc, T, l, hf):
    with stage(nc, "u_even", "u_odd", "dotted", "activated", "weighted") as (block, s):
        u_in = (s["u_even"], s["u_odd"])

        @block.sync
        def _(sp):
            with sp.Fori(0, HJ // 2) as j:
                for i in range(2):
                    sp.wait_ge(s["dotted"], 2 * j + i + 1)
                    sp.dma_start(T.ur[:, i], T.d["u"][l, hf, 2 * j + i]).then_inc(u_in[i], 16)

        @block.tensor
        def _(pe):
            pe.sem_inc(s["dotted"], 2)
            with pe.Fori(0, HJ // 2) as j:
                for i in range(2):
                    pe.wait_ge(u_in[i], 16 * j + 16)
                    pe.wait_ge(s["activated"], 2 * j + i + 1)
                    wide_product(nc, T, 2 * i, lambda k: T.ur[:, i, k, :], lambda k: T.xn[:, k, :], KD
                                 ).then_inc(s["dotted"], 1)

        @block.scalar
        def _(act):
            act.sem_inc(s["activated"], 2)
            with act.Fori(0, HJ // 2) as j:
                for i in range(2):
                    act.wait_ge(s["dotted"], 2 * j + i + 3)
                    act.wait_ge(s["weighted"], 2 * j + i + 1)
                    nc.scalar.activation(two(T.gelu[i]), halves(T, 2 * i), ACT.Gelu).then_inc(s["activated"], 1)

        @block.vector
        def _(dve):
            dve.sem_inc(s["weighted"], 2)
            with dve.Fori(0, HJ // 2) as j:
                for i in range(2):
                    dve.wait_ge(s["activated"], 2 * j + i + 3)
                    row = T.g[:, bass.ds(2 * j + i, 1), :].rearrange("p a n -> p (a n)")
                    nc.vector.tensor_tensor(row, row, T.gelu[i], ALU.mult).then_inc(s["weighted"], 1)


def expert_out_stage(nc, T, l, hf):
    CH = 8
    with stage(nc, "v_even", "v_odd", "v_free", "h_in", "summed", "added", "h_out") as (block, s):
        v_in = (s["v_even"], s["v_odd"])

        @block.sync
        def _(sp):
            with sp.Fori(0, KD) as m:
                for c in range(HJ // CH):
                    sp.wait_ge(s["v_free"], 8 * m + c + 1)
                    sp.dma_start(T.ur[:, c % 2], T.d["v"][l, hf, m, c]).then_inc(v_in[c % 2], 16)
                    if c == 0:
                        sp.wait_ge(s["h_out"], 16 * m + 16)
                        sp.dma_start(T.gelu[0], T.d["xs"][m]).then_inc(s["h_in"], 16)
                sp.wait_ge(s["added"], m + 2)
                sp.dma_start(T.d["xs"][m], T.gelu[0]).then_inc(s["h_out"], 16)
            sp.wait_ge(s["h_out"], 16 * KD + 16)

        @block.tensor
        def _(pe):
            pe.sem_inc(s["v_free"], 2)
            pe.sem_inc(s["h_out"], 16)
            with pe.Fori(0, KD) as m:
                pe.wait_ge(s["added"], m + 1)
                for c in range(HJ // CH):
                    pe.wait_ge(v_in[c % 2], 64 * m + 16 * (c // 2) + 16)
                    for a in range(2):
                        for j in range(CH):
                            last = nc.tensor.matmul(bank(T, a)[:, 0:HALF], T.ur[:, c % 2, j, :],
                                                    T.g[:, c * CH + j, a * HALF:(a + 1) * HALF],
                                                    start=(c == 0 and j == 0), stop=(c == 7 and j == CH - 1))
                    last.then_inc(s["v_free"], 1)
                pe.sem_inc(s["summed"], 1)

        @block.vector
        def _(dve):
            dve.sem_inc(s["added"], 1)
            with dve.Fori(0, KD) as m:
                dve.wait_ge(s["h_in"], 16 * m + 16)
                dve.wait_ge(s["v_free"], 8 * m + 10)
                nc.vector.tensor_tensor(two(T.gelu[0]), two(T.gelu[0]), halves(T, 0), ALU.add).then_inc(s["added"], 1)


def program(nc, d):
    T = Memory()
    T.d = d
    with ExitStack() as keep:
        def sb(ctx, name, shape, dt=F32):
            return ctx.enter_context(nc.sbuf_tensor(name, shape, dt))

        T.ps = keep.enter_context(nc.psum_tensor("ps", [P, 8 * BANK], F32))
        T.xn = sb(keep, "xn", [P, KD, NP_])
        T.general = sb(keep, "gc", [P, GC_W])
        T.pl = sb(keep, "pl", [P, PL_W])
        T.ident = T.general[:, C_MSK:C_MSK + P]
        T.ones = T.general[:, C_ONES:C_ONES + P]
        with stage(nc, "x_in") as (block, s):
            @block.sync
            def _(sp):
                sp.dma_start(d["xs"], d["x"]).then_inc(s["x_in"], 16)
                sp.wait_ge(s["x_in"], 16)
        with nc.Fori(0, DEPTH) as l:
            with ExitStack() as ctx:
                T.pr = sb(ctx, "pr", [P, 4, NP_])
                T.hc = sb(ctx, "hc", [P, HC_W])
                T.ph = sb(ctx, "ph", [P, PH_W])
                T.vt = sb(ctx, "vt", [P, TILES, 3 * P])
                T.br = sb(ctx, "br", [P, 16, N])
                T.st = sb(ctx, "st", [P, 5, P])
                T.s_in = sb(ctx, "s_in", [P, DEC_B, P])
                T.s_new = sb(ctx, "s_new", [P, DEC_B, P])
                T.kt = sb(ctx, "kt", [P, TILES, P])
                T.cols = sb(ctx, "cols", [P, 40])
                small = sb(ctx, "small", [P, 256])
                T.logg = small[:, 0:20].rearrange("p (t c) -> p t c", t=TILES)
                T.beta = small[:, 20:40].rearrange("p (t c) -> p t c", t=TILES)
                T.ga = small[:, 40:60].rearrange("p (t c) -> p t c", t=TILES)
                T.ga2 = small[:, 60:80].rearrange("p (t c) -> p t c", t=TILES)
                T.nea = small[:, 80:84]
                T.lam = small[:, 84:88]
                T.lb = small[:, 88:92]
                T.lgh = small[:, 96:101].unsqueeze(2)
                T.bth = small[:, 104:109].unsqueeze(2)
                T.lprod = small[:, 128:256].rearrange("p (a d) -> p a d", a=2)
                rs = sb(ctx, "rs", [P, N])
                T.rs = two(rs[:])
                T.tot = sb(ctx, "tot", [P, NP_])[:]
                T.pt = sb(ctx, "pt", [P, DEC_B * PAGES], I32)
                with ExitStack() as sub:
                    T.wr = sb(sub, "wr", [P, 4, KD, P])
                    T.wk = sb(sub, "wk", [P, 20, NP_])
                    flat = T.wk.rearrange("p a b -> p (a b)")
                    T.wtm = T.wr.rearrange("p a k c -> p (a k c)")[:, 0:KD * 3 * P].rearrange("p (k c) -> p k c", k=KD)
                    T.h = flat[:, 0:KD * N].rearrange("p (k n) -> p k n", k=KD)
                    T.sq = flat[:, KD * N:2 * KD * N].rearrange("p (k n) -> p k n", k=KD)
                    T.wab = flat[:, 2 * KD * N:2 * KD * N + 8 * KD].rearrange("p (k c) -> p k c", k=KD)
                    T.sc = T.wk[:, 0, :]
                    T.masked = flat[:, 18 * NP_:18 * NP_ + 8 * P]
                    T.vx = T.wr.rearrange("p a k c -> p (a k c)")[:, 3 * KD * P:].rearrange("p (s v) -> p s v", s=DEC_B)
                    T.dc = T.wr.rearrange("p a k c -> p (a k c)")[:, 2 * KD * P:2 * KD * P + DC_W]
                    norm_stage(nc, T, l, True)
                    with nc.Fori(0, H) as h:
                        values_stage(nc, T, l, h)
                        retention_stage(nc, T, l, h, br_slot(0, h))
                        hgrn_stage(nc, T, l, h, br_slot(1, h))
                        gdn_stage(nc, T, l, h, br_slot(2, h))
                        attention_stage(nc, T, l, h, br_slot(3, h))
                with ExitStack() as sub:
                    T.wm = sb(sub, "wm", [P, 2, 12, P])
                    T.mt = sb(sub, "mt", [P, KD, N])
                    sg = sb(sub, "sg", [P, 3, N])
                    T.sg = [two(sg[:, i, :]) for i in range(2)]
                    T.ma = two(sg[:, 2, :])
                    merge_stage(nc, T, l)
                    T.h = sb(sub, "h2", [P, KD, N])
                    out_stage(nc, T, l)
                    T.sq = T.mt
                    norm_stage(nc, T, l, False)
            with ExitStack() as ctx:
                T.idx = sb(ctx, "idx", [P, 5, NP_], BF16)
                T.iota = sb(ctx, "iota", [P, P])
                T.iota_b = sb(ctx, "iota_b", [P, P], BF16)[:]
                T.iota_h = sb(ctx, "iota_h", [P, HJ], BF16)[:]
                with ExitStack() as sub:
                    T.keys = sb(sub, "keys", [P, 2 * PH_HEADS, P])[:]
                    T.wm2 = sb(sub, "wm2", [P, 2, KD, P])
                    qt = sb(sub, "qt", [P, 2, NP_])
                    T.qt = [qt[:, i, :] for i in range(2)]
                    T.scr = sb(sub, "scr", [P, TILES, 2 * PH_HEADS, NKEY])
                    T.x1 = sb(sub, "x1", [P, 2 * PH_HEADS, NKEY])[:]
                    T.t1 = sb(sub, "t1", [P, 2 * PH_HEADS, TOPK])[:]
                    T.i1u = sb(sub, "i1u", [P, 2 * PH_HEADS, TOPK], U32)[:]
                    T.i1f = sb(sub, "i1f", [P, 2 * PH_HEADS, TOPK])[:]
                    T.cand = sb(sub, "cand", [P, PH_HEADS, TOPK * TOPK])[:]
                    T.t2 = sb(sub, "t2", [P, PH_HEADS, TOPK])[:]
                    T.posu = sb(sub, "posu", [P, PH_HEADS, TOPK], U32)[:]
                    T.pau = sb(sub, "pau", [P, PH_HEADS, TOPK], U32)[:]
                    T.pbu = sb(sub, "pbu", [P, PH_HEADS, TOPK], U32)[:]
                    T.paf = sb(sub, "paf", [P, PH_HEADS, TOPK])[:]
                    T.pbf = sb(sub, "pbf", [P, PH_HEADS, TOPK])[:]
                    T.eq = sb(sub, "eq", [P, P, TOPK])[:]
                    T.gw = sb(sub, "gw", [P, PH_HEADS, TOPK])[:]
                    T.gs = sb(sub, "gs", [P, PH_HEADS])[:]
                    T.found = sb(sub, "found", [P, 3, P])[:]
                    T.gp = sb(sub, "gp", [P, 3, P], BF16)[:]
                    T.spare = sb(sub, "spare", [P, 1])[:]
                    T.gr = sb(sub, "gr", [P, P])[:]
                    iota_stage(nc, T)
                    key_scores_stage(nc, T, l)
                    retrieval_stage(nc, T, l)
                with ExitStack() as sub:
                    T.g = sb(sub, "g", [P, HJ, N])
                    T.ur = sb(sub, "ur", [P, 2, KD, P])
                    T.oh1 = sb(sub, "oh1", [P, GT, P], BF16)
                    T.oh2 = sb(sub, "oh2", [P, GT, 3, HJ], BF16)
                    T.ids = sb(sub, "ids", [P, 5, GT])[:]
                    gelu = sb(sub, "gelu", [P, 2, N])
                    T.gelu = [gelu[:, i, :] for i in range(2)]
                    with nc.Fori(0, 2) as hf:
                        coefficient_stage(nc, T, l, hf)
                        expert_in_stage(nc, T, l, hf)
                        expert_out_stage(nc, T, l, hf)
        with stage(nc, "y_out") as (block, s):
            @block.sync
            def _(sp):
                sp.dma_start(d["y"], d["xs"]).then_inc(s["y_out"], 16)
                sp.wait_ge(s["y_out"], 16)


def iota_stage(nc, T):
    with stage(nc, "counted", "cast") as (block, s):
        @block.gpsimd
        def _(pool):
            nc.gpsimd.iota(T.iota[:], pattern=[[1, P]], base=0, channel_multiplier=0,
                           allow_small_or_imprecise_dtypes=True).then_inc(s["counted"], 1)

        @block.vector
        def _(dve):
            dve.wait_ge(s["counted"], 1)
            nc.vector.tensor_copy(T.iota_b, T.iota[:]).then_inc(s["cast"], 1)
            dve.wait_ge(s["cast"], 1)


def br_slot(b, h):
    return bass.ds(4 * b + h, 1)


def constants():
    f = np.float32
    p = np.arange(P)
    key, qry = p[:, None], p[None, :]
    gc = np.zeros((P, GC_W), f)
    gc[:, C_MSK:C_MSK + P] = np.eye(P)
    for r in range(LEVELS):
        m = 1 << r
        pair = (key // (2 * m) == qry // (2 * m)) & (key // m % 2 == 0) & (qry // m % 2 == 1)
        gc[:, C_MSK + (1 + r) * P:C_MSK + (2 + r) * P] = pair
    gc[:, C_ONES:C_ONES + P] = 1
    causal = key <= qry
    same = key // DEC_T == qry // DEC_T
    for t in range(TILES):
        gc[:, C_UT + t * P:C_UT + (t + 1) * P] = causal if t < 4 else causal & same
    gc[:, C_BLK:C_BLK + P] = same
    gc[:, C_BS:C_BS + DEC_B] = key // DEC_T == np.arange(DEC_B)[None, :]
    gc[:, C_COMP:C_COMP + P] = key // DK == qry // DK
    gc[:, C_SELA] = p < DK
    gc[:, C_SELB] = p >= DK
    dc = np.zeros((P, DC_W), f)
    x = np.arange(SEQ)[None, :]
    dist = p[:, None] + (SEQ - P) - x
    dc[:, C_DP:C_DP + SEQ] = np.where(dist >= 0, dist, FAR)
    tok = p % NS
    pos = tok % DEC_T
    dc[:, C_DS:C_DS + PAST] = PAST + pos[:, None] - np.arange(PAST)[None, :]
    new = np.arange(NS)[None, :]
    gap = pos[:, None] - new % DEC_T
    ok = (tok[:, None] // DEC_T == new // DEC_T) & (gap >= 0)
    dc[:, C_DS + PAST:C_DS + PAST + NS] = np.where(ok, gap, FAR)
    dc[:, C_STK:C_STK + NS] = tok[:, None] == new
    qm = np.zeros((P, DEC_B + 1, 2, NS))
    for c in range(2):
        qm[c * DK:(c + 1) * DK, DEC_B, c, :] = 1
        for b in range(DEC_B):
            qm[c * DK:(c + 1) * DK, b, c, b * DEC_T:(b + 1) * DEC_T] = 1
    dc[:, C_QM:] = qm.reshape(P, -1)
    hc = np.zeros((H, P, HC_W), np.float64)
    for h in range(H):
        lg = np.log1p(-np.exp2(-5.0 - h))
        gap = qry - key
        decay = np.where(gap >= 0, np.exp(np.maximum(gap, 0) * lg), 0.0) * K_SCALE
        for t in range(TILES):
            c = slice(t * P, (t + 1) * P)
            hc[h, :, H_RM:][:, c] = decay if t < 4 else decay * same
            at = p if t < 4 else p % DEC_T
            hc[h, :, H_QD:][:, c] = np.exp((at + 1) * lg)[None, :]
            hc[h, :, H_KD + t] = np.exp(((P if t < 4 else DEC_T) - 1 - at) * lg) * K_SCALE
            hc[h, :, H_GT + t] = np.exp(P * lg)
        hc[h, :, H_G8:H_G8 + DEC_B] = np.exp(DEC_T * lg)
        hc[h, :, H_SL] = -(2.0 ** (-8.0 * (h + 1) / H)) / S_SCALE
    layer = np.zeros((DEPTH, 3), f)
    for l in range(DEPTH):
        li = 0.8 - 0.6 * np.exp(-0.3 * l)
        layer[l] = (float(l > 0), li, 1.0 - li)
    return gc, dc, hc.astype(f), layer


def lay_out(i):
    c = np.ascontiguousarray
    i = {k: np.asarray(v) for k, v in i.items()}
    gc, dc, hc, layer = constants()
    a = {"gc": gc, "dc": dc, "hc": hc}
    x = np.concatenate([i["x_prompt"].reshape(SEQ, D), i["x_sample"].reshape(NS, D)])
    a["x"] = c(x.T.reshape(KD, P, N))
    w = i["w_in"]
    kt = lambda m: m.reshape(m.shape[0], KD, P, -1).transpose(0, 2, 1, 3)
    at = lambda o, h: slice(o + h * P, o + (h + 1) * P)
    rq, rk, rv, rg, hq, hf, hi, hg, gq, gk, gv, gg = (j * 512 for j in range(12))
    ga = 12 * 512
    dq = ga + 2 * H
    dk, dv = dq + 512, dq + 1024
    gate = dq + 1536
    cols = (rq, rk, rg, hq, hf, hg, gq, gk, gv, gg, dq, dk)
    a["w_cm"] = c(np.stack([np.stack([kt(w[:, :, at(o, h)]) for o in cols], 1) for h in range(H)], 1))
    a["w_tm"] = c(np.stack([kt(np.concatenate([w[:, :, at(o, h)] for o in (rv, hi, dv)], 2)) for h in range(H)], 1))
    a["w_ab"] = c(kt(w[:, :, ga:ga + 2 * H]))
    wg = w[:, :, gate:].reshape(DEPTH, KD, P, 4, KD, P).transpose(0, 4, 3, 2, 1, 5)
    wb = i["w_branch"].reshape(DEPTH, 4, 4, P, KD, P).transpose(0, 4, 1, 3, 2, 5)
    a["w_merge"] = c(np.concatenate([wg, wb], 4))
    a["w_out"] = c(i["w_out"].reshape(DEPTH, KD, P, KD, P).transpose(0, 3, 2, 1, 4))
    a["w_query"] = c(i["peer_wq"].reshape(DEPTH, KD, P, 2 * PH_HEADS, P).transpose(0, 3, 2, 1, 4))
    a["keys"] = c(i["peer_keys"].reshape(DEPTH, 2 * PH_HEADS, NKEY, P).transpose(0, 3, 1, 2))
    u = i["peer_u"].reshape(DEPTH, NKEY, 2, HJ, KD, P)
    a["u"] = c(u.transpose(0, 2, 3, 5, 4, 1))
    v = i["peer_v"].reshape(DEPTH, NKEY, 2, 8, 8, KD, P)
    a["v"] = c(v.transpose(0, 2, 5, 3, 1, 4, 6))
    rep = lambda m: np.repeat(m[:, None, :], P, 1)
    fk = lambda m: m.reshape(DEPTH, KD, P).transpose(0, 2, 1)
    a["pl"] = c(np.concatenate([fk(i["norm_mix"]), fk(i["norm_ffn"]), rep(i["gdn_a_log"]), rep(i["gdn_dt_bias"]),
                                rep(i["diff_lambda"].reshape(DEPTH, -1)), rep(layer)], 2))
    ph = np.zeros((DEPTH, H, P, PH_W), np.float32)
    for n, name in enumerate(("ret_norm", "hgrn_norm", "gdn_norm", "diff_norm")):
        ph[..., n] = i[name].reshape(DEPTH, H, P)
    taps = i["gdn_conv"].reshape(DEPTH, 4, 3, H, P).transpose(0, 3, 4, 2, 1)
    ph[..., Q_CONV:Q_CONV + 12] = taps.reshape(DEPTH, H, P, 12)
    ph[..., Q_LB:Q_LB + 2] = i["hgrn_lb_logits"].reshape(DEPTH, H, P).transpose(1, 2, 0)[None]
    ph[..., Q_QN] = np.tile(i["diff_q_norm"], (1, 2))[:, None, :]
    ph[..., Q_KN] = np.tile(i["diff_k_norm"], (1, 2))[:, None, :]
    a["ph"] = ph
    a["conv_in"] = c(i["state_gdn_conv"].reshape(DEPTH, DEC_B, 3, 3, H, P).transpose(0, 4, 3, 5, 1, 2))
    for n in ("state_ret", "state_hgrn", "state_gdn"):
        a[n] = c(i[n])
    a["cache_k"] = c(i["cache_k"].reshape(DEPTH, N_PHYS, PAGE, H, P).transpose(0, 1, 3, 4, 2))
    a["cache_v"] = c(i["cache_v"].transpose(0, 1, 3, 2, 4))
    a["page_table"] = c(i["page_table"].reshape(1, -1).astype(np.int32))
    return a


_OUTS = {
    "y": (KD, P, N),
    "ret_prompt": (DEPTH, H, P, P), "ret_sample": (DEPTH, DEC_B, H, P, P),
    "hgrn_prompt": (DEPTH, H, P, P), "hgrn_sample": (DEPTH, DEC_B, H, P, P),
    "gdn_prompt": (DEPTH, H, P, P), "gdn_sample": (DEPTH, DEC_B, H, P, P),
    "conv_prompt": (DEPTH, H, 3, P, 3), "conv_sample": (DEPTH, H, 3, P, DEC_B, 3),
    "k_out": (DEPTH, H, P, N), "v_prompt": (DEPTH, H, SEQ, P), "v_sample": (DEPTH, H, NS, P),
}


def kernel(**inputs):
    import concourse.bacc as _bacc
    from concourse.bass_utils import run_bass_kernel_spmd as _run

    nc = _bacc.Bacc("TRN2", target_bir_lowering=False, num_devices=1)
    arrays = lay_out(inputs)
    d = {}
    for name, a in arrays.items():
        d[name] = nc.dram_tensor(f"in_{name}", a.shape, mybir.dt.from_np(a.dtype), kind="ExternalInput").ap()
    for name, shape in _OUTS.items():
        d[name] = nc.dram_tensor(f"out_{name}", shape, F32, kind="ExternalOutput").ap()
    d["xs"] = nc.dram_tensor("residual", (KD, P, N), F32, kind="Internal").ap()
    program(nc, d)
    r = _run(nc, [{f"in_{n}": a for n, a in arrays.items()}], core_ids=[0])
    o = {n: r.results[0][f"out_{n}"] for n in _OUTS}
    y = o["y"].reshape(D, N).T
    conv_p = o["conv_prompt"].transpose(0, 4, 2, 1, 3).reshape(DEPTH, 1, 3, 3 * 512)
    conv_s = o["conv_sample"].transpose(0, 4, 5, 2, 1, 3).reshape(DEPTH, DEC_B, 3, 3 * 512)
    k = o["k_out"].transpose(0, 3, 1, 2)
    return (y[:SEQ].reshape(1, SEQ, D), y[SEQ:].reshape(DEC_B, DEC_T, D),
            o["ret_prompt"][:, None], o["ret_sample"], o["hgrn_prompt"][:, None], o["hgrn_sample"],
            o["gdn_prompt"][:, None], o["gdn_sample"], conv_p, conv_s,
            k[:, :SEQ].reshape(DEPTH, 1, SEQ, H, 2, DK),
            o["v_prompt"].transpose(0, 2, 1, 3)[:, None],
            k[:, SEQ:].reshape(DEPTH, DEC_B, DEC_T, H, 2, DK),
            o["v_sample"].transpose(0, 2, 1, 3).reshape(DEPTH, DEC_B, DEC_T, H, P))
```

```python
from contextlib import ExitStack, contextmanager

import numpy as np
import concourse.bass as bass
from concourse import mybir

F32 = mybir.dt.float32
F32R = mybir.dt.float32r
F16 = mybir.dt.float16
U32 = mybir.dt.uint32
I32 = mybir.dt.int32
ALU = mybir.AluOpType
ACT = mybir.ActivationFunctionType
AX_X = mybir.AxisListType.X

P = 128
D = 1024
KD = D // P
DEPTH = 2
SEQ = 512
DEC_B, DEC_T = 8, 8
NS = DEC_B * DEC_T
N = SEQ + NS
TILES = 5
NP_ = TILES * P
HALF = N // 2
H = 4
LEVELS = 7
W_HEAD = 12
PAGES = 2
PAGE = 128
PAST = PAGES * PAGE
N_PHYS = DEC_B * PAGES + DEC_B * PAGES // 4
DK = 64
EPS = 1e-6
K_SCALE = float(P) ** -0.5
S_SCALE = float(DK) ** -0.5
PH_HEADS = 8
TOPK = 16
NKEY = 128
FAR = 1e30
BANK = 512
PARTS = 4
PART = NKEY // PARTS
GT = N // PART
G_SCALE = 4096.0

C_MSK = 0
C_ONES = C_MSK + (1 + LEVELS) * P
C_UT = C_ONES + P
C_BLK = C_UT + TILES * P
C_BS = C_BLK + P
C_COMP = C_BS + DEC_B
C_SELA = C_COMP + P
C_SELB = C_SELA + 1
GC_W = C_SELB + 1
C_DP = 0
C_DS = C_DP + SEQ
C_STK = C_DS + PAST + NS
C_QM = C_STK + NS
DC_W = C_QM + (DEC_B + 1) * P
H_RM = 0
H_QD = H_RM + NP_
H_KD = H_QD + NP_
H_GT = H_KD + TILES
H_G8 = H_GT + TILES
H_SL = H_G8 + DEC_B
HC_W = H_SL + 1
Q_RN, Q_HN, Q_GN, Q_DN = 0, 1, 2, 3
Q_CONV = 4
Q_LB = Q_CONV + 12
Q_QN, Q_KN = Q_LB + 2, Q_LB + 3
PH_W = Q_KN + 1
L_NM, L_NF = 0, KD
L_AL = 2 * KD
L_DT = L_AL + H
L_LAM = L_DT + H
L_LB = L_LAM + 4 * DK
L_LI, L_OL = L_LB + 1, L_LB + 2
PL_W = L_OL + 1


class Memory:
    pass


@contextmanager
def stage(nc, *names):
    with ExitStack() as ctx:
        sems = {n: ctx.enter_context(nc.semaphore(n)) for n in names}
        with nc.Block(no_gpsimd_drain=True) as block:
            yield block, sems
        for n in names:
            nc.sync.sem_clear(sems[n])
        nc.all_engine_barrier(sem_only=True)


def chained(engine, sem):
    count = [0]

    def link(instruction):
        count[0] += 1
        instruction.then_inc(sem, 1)
        engine.wait_ge(sem, count[0])

    return link


def bank(T, b, width=BANK):
    return T.ps[:, b * BANK:b * BANK + width]


def halves(T, b):
    return T.ps[:, b * BANK:(b + 2) * BANK].rearrange("p (a c) -> p a c", a=2)[:, :, 0:HALF]


def two(ap):
    return ap[:, 0:N].rearrange("p (a c) -> p a c", a=2)


def tile(ap, t):
    return ap[:, t * P:(t + 1) * P]


def wide_product(nc, T, b, weights, rhs, kn):
    for a in range(2):
        for k in range(kn):
            last = nc.tensor.matmul(bank(T, b + a)[:, 0:HALF], weights(k), rhs(k)[:, a * HALF:(a + 1) * HALF],
                                    start=(k == 0), stop=(k == kn - 1))
    return last



def pe_ahead(nc, pe, T, s, u, b, banks=1):
    c, a = divmod(u, 2)
    if a == 0:
        pe.wait_ge(s["w"][c % 4], 16 * (c // 4 + 1))
    if u >= banks:
        pe.wait_ge(s["taken"], u - banks + 1)
    for k in range(KD):
        last = nc.tensor.matmul(bank(T, b)[:, 0:HALF], T.wr[:, c % 4, k, :], T.xn[:, k, a * HALF:(a + 1) * HALF],
                                start=(k == 0), stop=(k == KD - 1))
    last.then_inc(s["ahead"], 1)


def act_take(nc, act, T, s, u, b, dst, func=ACT.Copy, scale=1.0, dst_minus=None):
    cols = slice(u % 2 * HALF, (u % 2 + 1) * HALF)
    act.wait_ge(s["ahead"], u + 1)
    if dst_minus is not None:
        nc.scalar.activation(dst_minus[:, cols], bank(T, b)[:, 0:HALF], func, scale=-scale)
    nc.scalar.activation(dst[:, cols], bank(T, b)[:, 0:HALF], func, scale=scale).then_inc(s["taken"], 1)


def load_ahead(sp, T, s, l, h, tiles):
    for c, column in enumerate(tiles):
        if c >= 4:
            sp.wait_ge(s["ahead"], 2 * (c - 4) + 2)
        sp.dma_start(T.wr[:, c % 4], T.d["w_cm"][l, h, column]).then_inc(s["w"][c % 4], 16)


def pe_value_tile(nc, T, t, b):
    for k in range(KD):
        last = nc.tensor.matmul(bank(T, b)[:, 0:2 * P], tile(T.xn[:, k, :], t), T.wtm[:, k, :],
                                start=(k == 0), stop=(k == KD - 1))
    return last


RET_TILES, HGRN_TILES, GDN_TILES, ATT_TILES = (0, 1, 2), (3, 4, 5), (6, 7, 8, 9), (10, 11, 12)
AHEAD = ("ahead", "taken")
W_SEMS = ("w0", "w1", "w2", "w3")


def norm_stage(nc, T, l, first):
    names = ("h_in", "small_in", "const_in", "squared", "summed", "scaled", "rooted", "chain_v", "chain_a",
             "zeroed", "normed", "ab_done", "a_ready", "lam_ready", "exp_done", "sp_abs", "sp_exp", "sp_in",
             "sp_ln", "b_done", "al_done", "dc_in")
    with stage(nc, *names) as (block, s):
        @block.sync
        def _(sp):
            if first:
                sp.dma_start(T.h[:], T.d["xs"].rearrange("m p n -> p m n")).then_inc(s["h_in"], 16)
                sp.dma_start(T.pl[:], T.d["pl"][l]).then_inc(s["small_in"], 16)
                sp.dma_start(T.wab, T.d["w_ab"][l]).then_inc(s["small_in"], 16)
                sp.dma_start(T.general[:], T.d["gc"]).then_inc(s["const_in"], 16)
                sp.dma_start(T.dc, T.d["dc"]).then_inc(s["dc_in"], 16)
                sp.wait_ge(s["dc_in"], 16)

        @block.scalar
        def _(act):
            if first:
                act.wait_ge(s["h_in"], 16)
            for k in range(KD):
                nc.scalar.activation(T.sq[:, k, :], T.h[:, k, :], ACT.Square).then_inc(s["squared"], 1)
            act.wait_ge(s["scaled"], 1)
            nc.scalar.activation(T.rs, T.rs, ACT.Sqrt).then_inc(s["rooted"], 1)
            if first:
                act.wait_ge(s["lam_ready"], 1)
                nc.scalar.activation(T.lam[:, 0:2], T.lam[:, 0:2], ACT.Exp).then_inc(s["exp_done"], 1)
                nc.scalar.activation(T.nea, T.pl[:, L_AL:L_AL + H], ACT.Exp).then_inc(s["al_done"], 1)
                act.wait_ge(s["a_ready"], 1)
                nc.scalar.activation(T.ga2, T.ga, ACT.Abs).then_inc(s["chain_a"], 1)
                act.wait_ge(s["chain_a"], 1)
                nc.scalar.activation(T.ga2, T.ga2, ACT.Exp, scale=-1.0).then_inc(s["sp_exp"], 1)
                act.wait_ge(s["sp_in"], 1)
                nc.scalar.activation(T.ga2, T.ga2, ACT.Ln).then_inc(s["sp_ln"], 1)
                act.wait_ge(s["ab_done"], 1)
                nc.scalar.activation(T.beta, bank(T, 2, TILES * 2 * H).rearrange("p (t c) -> p t c", c=2 * H)[:, :, H:],
                                     ACT.Sigmoid).then_inc(s["b_done"], 1)
                act.wait_ge(s["b_done"], 1)

        @block.tensor
        def _(pe):
            if first:
                pe.wait_ge(s["const_in"], 16)
            pe.wait_ge(s["squared"], KD)
            wide_product(nc, T, 0, lambda k: T.ones, lambda k: T.sq[:, k, :], KD).then_inc(s["summed"], 1)
            if first:
                pe.wait_ge(s["small_in"], 32)
                pe.wait_ge(s["zeroed"], 1)
                pe.wait_ge(s["normed"], KD)
                for t in range(TILES):
                    for k in range(KD):
                        last = nc.tensor.matmul(T.ps[:, 2 * BANK + t * 2 * H:2 * BANK + (t + 1) * 2 * H],
                                                tile(T.xn[:, k, :], t), T.wab[:, k, :],
                                                start=(k == 0), stop=(k == KD - 1))
                last.then_inc(s["ab_done"], 1)

        @block.vector
        def _(dve):
            link = chained(dve, s["chain_v"])
            if first:
                nc.vector.memset(T.xn[:, :, N:NP_], 0.0).then_inc(s["zeroed"], 1)
                link(nc.vector.memset(T.pr[:], 0.0))
            dve.wait_ge(s["summed"], 1)
            nc.vector.tensor_scalar(T.rs, halves(T, 0), 1.0 / D, EPS, ALU.mult, ALU.add).then_inc(s["scaled"], 1)
            dve.wait_ge(s["rooted"], 1)
            link(nc.vector.reciprocal(T.rs, T.rs))
            g0 = L_NM if first else L_NF
            if first:
                dve.wait_ge(s["small_in"], 32)
            for k in range(KD):
                nc.vector.scalar_tensor_tensor(out=two(T.xn[:, k, :]), in0=two(T.h[:, k, :]),
                                               scalar=T.pl[:, g0 + k:g0 + k + 1], in1=T.rs,
                                               op0=ALU.mult, op1=ALU.mult).then_inc(s["normed"], 1)
            if first:
                lp = T.pl[:, L_LAM:L_LAM + 4 * DK].rearrange("p (a b d) -> p a b d", a=2, b=2)
                link(nc.vector.tensor_tensor(T.lprod, lp[:, :, 0, :], lp[:, :, 1, :], ALU.mult))
                nc.vector.tensor_reduce(T.lam[:, 0:2], T.lprod, AX_X, ALU.add).then_inc(s["lam_ready"], 1)
                dve.wait_ge(s["exp_done"], 1)
                link(nc.vector.tensor_tensor(T.lam[:, 2:3], T.lam[:, 1:2], T.lam[:, 0:1], ALU.subtract))
                link(nc.vector.tensor_tensor(T.lam[:, 2:3], T.lam[:, 2:3], T.pl[:, L_LI:L_LI + 1], ALU.subtract))
                link(nc.vector.scalar_tensor_tensor(out=T.lam[:, 3:4], in0=T.general[:, C_SELB:C_SELB + 1],
                                                    scalar=T.lam[:, 2:3], in1=T.general[:, C_SELA:C_SELA + 1],
                                                    op0=ALU.mult, op1=ALU.add))
                dve.wait_ge(s["ab_done"], 1)
                ab = bank(T, 2, TILES * 2 * H).rearrange("p (t c) -> p t c", c=2 * H)
                nc.vector.tensor_tensor(T.ga, ab[:, :, 0:H],
                                        T.pl[:, L_DT:L_DT + H].unsqueeze(1).to_broadcast([P, TILES, H]),
                                        ALU.add).then_inc(s["a_ready"], 1)
                dve.wait_ge(s["sp_exp"], 1)
                nc.vector.tensor_scalar(T.ga2, T.ga2, 1.0, None, ALU.add).then_inc(s["sp_in"], 1)
                dve.wait_ge(s["sp_ln"], 1)
                link(nc.vector.scalar_tensor_tensor(out=T.ga, in0=T.ga, scalar=0.0, in1=T.ga2,
                                                    op0=ALU.max, op1=ALU.add))
                dve.wait_ge(s["al_done"], 1)
                link(nc.vector.scalar_tensor_tensor(out=T.logg, in0=T.ga, scalar=-1.0,
                                                    in1=T.nea.unsqueeze(1).to_broadcast([P, TILES, H]),
                                                    op0=ALU.mult, op1=ALU.mult))


def first_head_stage(nc, T, l):
    with stage(nc, *W_SEMS, *AHEAD, "values_in", "valued", "copied") as (block, s):
        s["w"] = [s["w0"], s["w1"], s["w2"], s["w3"]]

        @block.sync
        def _(sp):
            load_ahead(sp, T, s, l, 0, RET_TILES)
            sp.wait_ge(s["ahead"], 4)
            sp.dma_start(T.wtm, T.d["w_tm"][l, 0]).then_inc(s["values_in"], 16)

        @block.tensor
        def _(pe):
            for u in range(6):
                pe_ahead(nc, pe, T, s, u, u % 2, banks=2)
            pe.wait_ge(s["values_in"], 16)
            for t in range(TILES):
                pe_value_tile(nc, T, t, 2 + t).then_inc(s["valued"], 1)

        @block.scalar
        def _(act):
            for u in range(6):
                act_take(nc, act, T, s, u, u % 2, T.ret[u // 2], ACT.Silu if u >= 4 else ACT.Copy)
            for t in range(TILES):
                act.wait_ge(s["valued"], t + 1)
                nc.scalar.copy(T.vt[:, t, 0:2 * P], bank(T, 2 + t)[:, 0:2 * P]).then_inc(s["copied"], 1)


def pe_state_products(nc, pe, T, s, values):
    pe.wait_ge(s["keys_ready"], 1)
    for t in range(4):
        last = nc.tensor.matmul(T.ps[:, t * P:(t + 1) * P], T.kt[:, t, :], values(t), start=True, stop=True)
    last.then_inc(s["u_prompt"], 1)
    pe_sample_state(nc, pe, T, s)


def pe_sample_state(nc, pe, T, s):
    pe.wait_ge(s["vx_ready"], 1)
    for a in range(2):
        last = nc.tensor.matmul(bank(T, 2 + a), T.kt[0:NS, 4, :],
                                T.vx[0:NS, 4 * a:4 * a + 4, :], start=True, stop=True)
    last.then_inc(s["u_sample"], 1)


def pe_outputs(nc, pe, T, s, values, q_prompt, q_sample):
    for t in range(4):
        o = T.ps[:, 4 * BANK + t * P:4 * BANK + (t + 1) * P]
        nc.tensor.matmul(o, values(t), tile(T.sc, t), start=True, stop=(t == 0))
        if t:
            nc.tensor.matmul(o, T.st[:, t, :], tile(q_prompt, t), start=False, stop=True)
    nc.tensor.matmul(bank(T, 5, P), values(4), tile(T.sc, 4), start=True, stop=False)
    for b in range(DEC_B):
        last = nc.tensor.matmul(bank(T, 5)[:, b * DEC_T:(b + 1) * DEC_T], T.s_in[:, b, :],
                                q_sample[:, SEQ + b * DEC_T:SEQ + (b + 1) * DEC_T],
                                start=False, stop=(b == DEC_B - 1))
    last.then_inc(s["o_ready"], 1)


def dve_spread_values(nc, T, s, values):
    nc.vector.tensor_tensor(T.vx[0:NS], values.unsqueeze(1).to_broadcast([NS, DEC_B, P]),
                            T.general[0:NS, C_BS:C_BS + DEC_B].unsqueeze(2).to_broadcast([NS, DEC_B, P]),
                            ALU.mult).then_inc(s["vx_ready"], 1)


def dve_prompt_states(nc, dve, T, s, link, decay):
    dve.wait_ge(s["u_prompt"], 1)
    link(nc.vector.tensor_copy(T.st[:, 1, :], T.ps[:, 0:P]))
    for t in range(1, 4):
        op = nc.vector.scalar_tensor_tensor(out=T.st[:, t + 1, :], in0=T.st[:, t, :], scalar=decay[:, t:t + 1],
                                            in1=T.ps[:, t * P:(t + 1) * P], op0=ALU.mult, op1=ALU.add)
        if t < 3:
            link(op)
    op.then_inc(s["st_ready"], 1)


def dve_sample_states(nc, dve, T, s, link, decay):
    dve.wait_ge(s["s_loaded"], 16)
    link(nc.vector.tensor_tensor(T.s_new[:], T.s_in[:], decay.unsqueeze(2).to_broadcast([P, DEC_B, P]), ALU.mult))
    dve.wait_ge(s["u_sample"], 1)
    nc.vector.tensor_tensor(T.s_new[:], T.s_new[:],
                            T.ps[:, 2 * BANK:4 * BANK].rearrange("p (s v) -> p s v", s=DEC_B),
                            ALU.add).then_inc(s["s_ready"], 1)


def sp_states(sp, T, s, l, h, prompt, sample):
    sp.wait_ge(s["st_ready"], 1)
    sp.dma_start(prompt[l, h], T.st[:, 4, :]).then_inc(s["states_out"], 16)
    sp.wait_ge(s["s_ready"], 1)
    sp.dma_start(sample[l, :, h].rearrange("s k v -> k s v"), T.s_new[:]).then_inc(s["states_out"], 16)
    sp.wait_ge(s["states_out"], 32)


def act_square(nc, act, T, s):
    act.wait_ge(s["o_ready"], 1)
    nc.scalar.activation(T.wk[:, 1, 0:N], bank(T, 4, N), ACT.Square).then_inc(s["o_squared"], 1)


def act_root(nc, act, T, s):
    act.wait_ge(s["o_mean"], 1)
    nc.scalar.activation(T.rs, T.rs, ACT.Sqrt).then_inc(s["o_root"], 1)


def pe_finish(nc, pe, T, s):
    pe.wait_ge(s["o_squared"], 1)
    wide_product(nc, T, 6, lambda k: T.ones, lambda k: T.wk[:, 1, :], 1).then_inc(s["o_summed"], 1)


def dve_finish(nc, dve, T, s, link, gain, slot, gate):
    dve.wait_ge(s["o_summed"], 1)
    nc.vector.tensor_scalar(T.rs, halves(T, 6), 1.0 / P, EPS, ALU.mult, ALU.add).then_inc(s["o_mean"], 1)
    dve.wait_ge(s["o_root"], 1)
    link(nc.vector.reciprocal(T.rs, T.rs))
    out = T.br[:, slot, :].rearrange("p a n -> p (a n)")
    link(nc.vector.scalar_tensor_tensor(out=two(out), in0=two(bank(T, 4, N)), scalar=gain, in1=T.rs,
                                        op0=ALU.mult, op1=ALU.mult))
    if gate is not None:
        link(nc.vector.tensor_tensor(out, out, gate[:, 0:N], ALU.mult))


FINISH = ("o_ready", "o_squared", "o_summed", "o_mean", "o_root", "chain_v")
STATES = ("keys_ready", "u_prompt", "u_sample", "vx_ready", "st_ready", "s_ready", "s_loaded", "states_out")


def load_sample_state(sp, T, s, l, h, state):
    sp.dma_start(T.s_in[:], state[l, :, h].rearrange("s k v -> k s v")).then_inc(s["s_loaded"], 16)


def retention_stage(nc, T, l, h, slot):
    q, k, g = T.ret
    hq, hf, hg, hneg = T.hgrn
    qd = T.wk[:, 2, :]
    with stage(nc, *W_SEMS, *AHEAD, "small_in", "scored", "turned", "sc_ready", *FINISH, *STATES) as (block, s):
        s["w"] = [s["w0"], s["w1"], s["w2"], s["w3"]]

        @block.sync
        def _(sp):
            sp.dma_start(T.hc[:], T.d["hc"][h]).then_inc(s["small_in"], 16)
            sp.dma_start(T.ph[:], T.d["ph"][l, h]).then_inc(s["small_in"], 16)
            load_ahead(sp, T, s, l, h, HGRN_TILES)
            load_sample_state(sp, T, s, l, h, T.d["state_ret"])
            sp_states(sp, T, s, l, h, T.d["ret_prompt"], T.d["ret_sample"])

        @block.tensor
        def _(pe):
            for t in range(TILES):
                last = nc.tensor.matmul(tile(bank(T, 4, NP_), t), tile(k, t), tile(q, t), start=True, stop=True)
            last.then_inc(s["scored"], 1)
            for t in range(TILES):
                last = nc.tensor.transpose(tile(bank(T, 6, NP_), t), tile(k, t), T.ident)
            last.then_inc(s["turned"], 1)
            pe_state_products(nc, pe, T, s, lambda t: T.vt[:, t, 0:P])
            pe_ahead(nc, pe, T, s, 0, 1)
            pe_ahead(nc, pe, T, s, 1, 1)
            pe.wait_ge(s["sc_ready"], 1)
            pe.wait_ge(s["st_ready"], 1)
            pe.wait_ge(s["s_loaded"], 16)
            pe_outputs(nc, pe, T, s, lambda t: T.vt[:, t, 0:P], qd, qd)
            pe_ahead(nc, pe, T, s, 2, 1)
            pe_finish(nc, pe, T, s)
            for u in range(3, 6):
                pe_ahead(nc, pe, T, s, u, 1)

        @block.scalar
        def _(act):
            def take(u):
                if u < 2:
                    act_take(nc, act, T, s, u, 1, hq, scale=K_SCALE)
                elif u < 4:
                    act_take(nc, act, T, s, u, 1, hf, ACT.Sigmoid, dst_minus=hneg)
                else:
                    act_take(nc, act, T, s, u, 1, hg, ACT.Silu)

            take(0)
            take(1)
            act_square(nc, act, T, s)
            take(2)
            act_root(nc, act, T, s)
            for u in range(3, 6):
                take(u)

        @block.vector
        def _(dve):
            link = chained(dve, s["chain_v"])
            dve_spread_values(nc, T, s, T.vt[0:NS, 4, 0:P])
            dve.wait_ge(s["small_in"], 32)
            dve.wait_ge(s["turned"], 1)
            nc.vector.tensor_tensor(T.kt[:], bank(T, 6, NP_).rearrange("p (t k) -> p t k", t=TILES),
                                    T.hc[:, H_KD:H_KD + TILES].unsqueeze(2).to_broadcast([P, TILES, P]),
                                    ALU.mult).then_inc(s["keys_ready"], 1)
            link(nc.vector.tensor_tensor(qd, q, T.hc[:, H_QD:H_QD + NP_], ALU.mult))
            nc.vector.tensor_tensor(T.sc, bank(T, 4, NP_), T.hc[:, H_RM:H_RM + NP_], ALU.mult).then_inc(s["sc_ready"], 1)
            dve_prompt_states(nc, dve, T, s, link, T.hc[:, H_GT:H_GT + TILES])
            dve_sample_states(nc, dve, T, s, link, T.hc[:, H_G8:H_G8 + DEC_B])
            dve_finish(nc, dve, T, s, link, T.ph[:, Q_RN:Q_RN + 1], slot, g)


def history(ap):
    return ap[:, SEQ + 3:SEQ + 3 + DEC_B * (DEC_T + 3)].rearrange("p (s t) -> p s t", s=DEC_B)


def act_take_gdn(nc, act, T, s, u, b):
    c, a = divmod(u, 2)
    if c == 3:
        act_take(nc, act, T, s, u, b, T.gdn_gate, ACT.Silu)
        return
    xp = T.conv[c]
    act.wait_ge(s["ahead"], u + 1)
    if a == 0:
        nc.scalar.copy(xp[:, 3:3 + HALF], bank(T, b)[:, 0:HALF]).then_inc(s["taken"], 1)
    else:
        nc.scalar.copy(xp[:, 3 + HALF:3 + SEQ], bank(T, b)[:, 0:SEQ - HALF])
        nc.scalar.copy(history(xp)[:, :, 3:3 + DEC_T],
                       bank(T, b)[:, SEQ - HALF:HALF].rearrange("p (s t) -> p s t", s=DEC_B)).then_inc(s["taken"], 1)


def hgrn_stage(nc, T, l, h, slot):
    q, f, g, sneg = T.hgrn
    qf = [T.wk[:, 2 + r, :] for r in range(LEVELS + 1)]
    ke = [T.wk[:, 10 + r, :] for r in range(LEVELS + 1)]
    fd = T.wk[:, 1, :]
    masked = T.masked
    vt = lambda t: T.vt[:, t, P:2 * P]
    with stage(nc, *W_SEMS, *AHEAD, "lb_in", "lb_exp", "level_v", "level_a", "scored", "masked_",
               "summed_", "turned", "sc_ready", *FINISH, *STATES) as (block, s):
        s["w"] = [s["w0"], s["w1"], s["w2"], s["w3"]]

        def blocks(ap, r):
            return ap.rearrange("p (n two b) -> p n two b", two=2, b=1 << r)

        @block.sync
        def _(sp):
            load_ahead(sp, T, s, l, h, GDN_TILES)
            load_sample_state(sp, T, s, l, h, T.d["state_hgrn"])
            sp_states(sp, T, s, l, h, T.d["hgrn_prompt"], T.d["hgrn_sample"])

        @block.tensor
        def _(pe):
            for u in range(4):
                pe_ahead(nc, pe, T, s, u, 4 + u % 2, banks=2)
            pe.wait_ge(s["level_v"], LEVELS + 1)
            pe.wait_ge(s["level_a"], LEVELS)
            for t in range(TILES):
                n = 1 + (LEVELS if t < 4 else 3)
                b = 2 * (t % 2)
                if t >= 2:
                    pe.wait_ge(s["masked_"], t - 1)
                for i in range(n):
                    lhs, rhs = (ke[0], q) if i == 0 else (ke[i - 1], qf[i - 1])
                    last = nc.tensor.matmul(T.ps[:, b * BANK + i * P:b * BANK + (i + 1) * P],
                                            tile(lhs, t), tile(rhs, t), start=True, stop=True)
                last.then_inc(s["scored"], 1)
            for t in range(TILES):
                last = nc.tensor.transpose(tile(bank(T, 6, NP_), t), tile(ke[LEVELS if t < 4 else 3], t), T.ident)
            last.then_inc(s["turned"], 1)
            pe.wait_ge(s["masked_"], TILES)
            pe_state_products(nc, pe, T, s, vt)
            pe_ahead(nc, pe, T, s, 4, 1)
            pe.wait_ge(s["sc_ready"], TILES)
            pe.wait_ge(s["st_ready"], 1)
            pe.wait_ge(s["s_loaded"], 16)
            pe_outputs(nc, pe, T, s, vt, qf[LEVELS], qf[3])
            pe_ahead(nc, pe, T, s, 5, 1)
            pe_finish(nc, pe, T, s)
            pe_ahead(nc, pe, T, s, 6, 1)
            pe_ahead(nc, pe, T, s, 7, 1)

        @block.scalar
        def _(act):
            act.wait_ge(s["lb_in"], 1)
            nc.scalar.activation(T.lb[:, 0:2], T.lb[:, 0:2], ACT.Exp).then_inc(s["lb_exp"], 1)
            take = lambda u: act_take_gdn(nc, act, T, s, u, 4 + u % 2 if u < 4 else 1)
            for r in range(LEVELS):
                act.wait_ge(s["level_v"], r + 1)
                if r:
                    act.wait_ge(s["level_a"], r)
                nc.scalar.copy(blocks(qf[r + 1], r)[:, :, 0, :], blocks(qf[r], r)[:, :, 0, :])
                nc.scalar.copy(blocks(ke[r + 1], r)[:, :, 1, :], blocks(ke[r], r)[:, :, 1, :]).then_inc(s["level_a"], 1)
                if r == 4:
                    take(0)
            for u in range(1, 5):
                take(u)
            act_square(nc, act, T, s)
            take(5)
            act_root(nc, act, T, s)
            take(6)
            take(7)

        @block.vector
        def _(dve):
            link = chained(dve, s["chain_v"])
            dve_spread_values(nc, T, s, T.vt[0:NS, 4, P:2 * P])
            lg, lb = T.ph[:, Q_LB:Q_LB + 2], T.lb
            link(nc.vector.tensor_reduce(lb[:, 2:3], lg, AX_X, ALU.max))
            nc.vector.tensor_scalar(lb[:, 0:2], lg, lb[:, 2:3], None, ALU.subtract).then_inc(s["lb_in"], 1)
            dve.wait_ge(s["lb_exp"], 1)
            link(nc.vector.tensor_reduce(lb[:, 2:3], lb[:, 0:2], AX_X, ALU.add))
            link(nc.vector.reciprocal(lb[:, 2:3], lb[:, 2:3]))
            link(nc.vector.tensor_scalar(lb[:, 0:2], lb[:, 0:2], lb[:, 2:3], None, ALU.mult))
            link(nc.vector.tensor_tensor(lb[:, 1:2], lb[:, 0:1], lb[:, 1:2], ALU.add))
            link(nc.vector.tensor_tensor(lb[:, 1:2], lb[:, 1:2], lb[:, 0:1], ALU.subtract))
            link(nc.vector.tensor_tensor(lb[:, 1:2], lb[:, 1:2], T.pl[:, L_LB:L_LB + 1], ALU.mult))
            link(nc.vector.tensor_scalar(lb[:, 3:4], lb[:, 1:2], -1.0, 1.0, ALU.mult, ALU.add))
            link(nc.vector.tensor_scalar(fd, f, lb[:, 3:4], lb[:, 1:2], ALU.mult, ALU.add))
            link(nc.vector.tensor_scalar(ke[0], sneg, lb[:, 3:4], None, ALU.mult))
            nc.vector.tensor_tensor(qf[0], q, fd, ALU.mult).then_inc(s["level_v"], 1)
            tot = fd
            at = 0
            for r in range(LEVELS):
                nb = NP_ >> (r + 1)
                pair = tot.rearrange("p (n two) -> p n two", two=2)
                if r:
                    dve.wait_ge(s["level_a"], r)
                else:
                    dve.wait_ge(s["level_v"], 1)
                wide = lambda c: pair[:, :, c].unsqueeze(2).to_broadcast([P, nb, 1 << r])
                nxt = T.tot[:, at:at + nb]
                link(nc.vector.tensor_tensor(nxt, pair[:, :, 0], pair[:, :, 1], ALU.mult))
                link(nc.vector.tensor_tensor(blocks(qf[r + 1], r)[:, :, 1, :], blocks(qf[r], r)[:, :, 1, :],
                                             wide(0), ALU.mult))
                link(nc.vector.tensor_tensor(blocks(ke[r + 1], r)[:, :, 0, :], blocks(ke[r], r)[:, :, 0, :],
                                             wide(1), ALU.mult))
                dve.sem_inc(s["level_v"], 1)
                tot = nxt
                if r == 2:
                    tot8 = T.tot[:, at + SEQ // 8:at + SEQ // 8 + DEC_B]
                at += nb
            for t in range(TILES):
                n = 1 + (LEVELS if t < 4 else 3)
                b = 2 * (t % 2)
                dve.wait_ge(s["scored"], t + 1)
                nc.vector.tensor_tensor(masked[:, 0:n * P], T.ps[:, b * BANK:b * BANK + n * P],
                                        T.general[:, C_MSK:C_MSK + n * P], ALU.mult).then_inc(s["masked_"], 1)
                dve.wait_ge(s["masked_"], t + 1)
                link(nc.vector.tensor_reduce(tile(T.sc, t), masked[:, 0:n * P].rearrange("p (m i) -> p i m", m=n),
                                             AX_X, ALU.add))
                dve.sem_inc(s["sc_ready"], 1)
            dve.wait_ge(s["turned"], 1)
            nc.vector.tensor_copy(T.kt[:], bank(T, 6, NP_).rearrange("p (t k) -> p t k", t=TILES)
                                  ).then_inc(s["keys_ready"], 1)
            dve_prompt_states(nc, dve, T, s, link, tot)
            dve_sample_states(nc, dve, T, s, link, tot8)
            dve_finish(nc, dve, T, s, link, T.ph[:, Q_HN:Q_HN + 1], slot, g)


def gdn_stage(nc, T, l, h, slot, more):
    q, k, v = T.gdn
    g = T.gdn_gate
    w = lambda i: T.wk[:, i, :]
    xp = T.conv
    sq = [w(5), w(6)]
    lgb, btb = w(7), w(8)
    dec, ec, bmat = w(9), w(10), w(11)
    boff, rr, rt, wz = w(12), w(13), w(14), w(15)
    qe, bv, delta, xr, kss = w(16), w(2), w(3), w(4), w(5)
    mask = lambda i: T.general[:, C_MSK + i * P:C_MSK + (i + 1) * P]
    tiled = lambda ap, n=TILES: ap[:, 0:n * P].rearrange("p (t i) -> p t i", t=n)
    col, ecol, tcol, kcol, becol = (T.cols[:, i * TILES:(i + 1) * TILES] for i in range(5))
    d8 = T.cols[:, 5 * TILES:5 * TILES + DEC_B]
    names = ("hist_in", "conv_done", "silu_done", "sq_done", "ss_done", "ss_eps",
             "ss_root", "qk_ready", "lgb_ready", "cum_done", "col_done", "dec_in", "dec_exp", "exp_done", "scored",
             "betab_done", "b_ready", "turned", "vt_ready", "r1_ready", "rt_turned", "rt_ready", "boff_ready",
             "w_done", "w_out", "z_done", "level_done", "kt_turned", "ks_done", "x_ready", "delta_done",
             "delta_ready", "u_done", "st_step", "kss_done", "kss_copied", "kss_turned", "sc_ready", "conv_out",
             "small_done", "cols_done", "ec_done")
    with stage(nc, *W_SEMS, *AHEAD, *names, *FINISH, *STATES) as (block, s):
        s["w"] = [s["w0"], s["w1"], s["w2"], s["w3"]]

        hist = lambda c: history(xp[c])

        @block.sync
        def _(sp):
            for c in range(3):
                sp.dma_start(hist(c)[:, :, 0:3], T.d["conv_in"][l, h, c]).then_inc(s["hist_in"], 16)
            load_ahead(sp, T, s, l, h, ATT_TILES)
            load_sample_state(sp, T, s, l, h, T.d["state_gdn"])
            sp.wait_ge(s["hist_in"], 48)
            for c in range(3):
                sp.dma_start(T.d["conv_prompt"][l, h, c], xp[c][:, SEQ:SEQ + 3]).then_inc(s["conv_out"], 16)
                sp.dma_start(T.d["conv_sample"][l, h, c], hist(c)[:, :, DEC_T:DEC_T + 3]).then_inc(s["conv_out"], 16)
            if more:
                for c, column in enumerate(RET_TILES, 3):
                    if c >= 4:
                        sp.wait_ge(s["ahead"], 2 * (c - 4) + 2)
                    sp.dma_start(T.wr[:, c % 4], T.d["w_cm"][l, h + 1, column]).then_inc(s["w"][c % 4], 16)
            sp.wait_ge(s["conv_out"], 96)
            sp_states(sp, T, s, l, h, T.d["gdn_prompt"], T.d["gdn_sample"])

        @block.tensor
        def _(pe):
            ahead = lambda u, b, banks=1: pe_ahead(nc, pe, T, s, u, b, banks)
            pe.wait_ge(s["lgb_ready"], 1)
            ut = lambda t: T.general[:, C_UT + t * P:C_UT + (t + 1) * P]
            for t in range(TILES):
                last = nc.tensor.matmul(tile(bank(T, 4, NP_), t), tile(lgb, t), ut(t), start=True, stop=True)
            last.then_inc(s["cum_done"], 1)
            one = lambda c: bank(T, 6)[:, c:c + 1]
            for t in range(TILES):
                nc.tensor.matmul(one(t), ut(t), T.lgh[:, t, :], start=True, stop=True)
                total = T.ones if t < 4 else T.general[:, C_BLK:C_BLK + P]
                nc.tensor.matmul(one(TILES + t), total, T.lgh[:, t, :], start=True, stop=True)
            nc.tensor.matmul(bank(T, 6)[:, 2 * TILES:2 * TILES + DEC_B], tile(lgb, 4), T.general[:, C_BS:C_BS + DEC_B],
                             start=True, stop=True).then_inc(s["col_done"], 1)
            ahead(0, 7)
            ahead(1, 7)
            ahead(2, 7)
            for c in range(2):
                pe.wait_ge(s["sq_done"], c + 1)
                wide_product(nc, T, 2 * c, lambda kk: T.ones, lambda kk: sq[c], 1).then_inc(s["ss_done"], 1)
            pe.wait_ge(s["exp_done"], 1)
            for t in range(TILES):
                last = nc.tensor.matmul(tile(bank(T, 4, NP_), t), tile(btb, t), T.ident, start=True, stop=True)
            last.then_inc(s["betab_done"], 1)
            ahead(3, 7)
            pe.wait_ge(s["qk_ready"], 2)
            for i, rhs in enumerate((k, q)):
                for t in range(TILES):
                    last = nc.tensor.matmul(tile(bank(T, 2 * i, NP_), t), tile(k, t), tile(rhs, t), start=True, stop=True)
                last.then_inc(s["scored"], 1)
            pe.wait_ge(s["cols_done"], 1)
            pe.wait_ge(s["taken"], 4)
            for t in range(TILES):
                last = nc.tensor.transpose(tile(bank(T, 6, NP_), t), tile(v, t), T.ident)
            last.then_inc(s["turned"], 1)
            pe.wait_ge(s["r1_ready"], 1)
            for t in range(TILES):
                last = nc.tensor.transpose(tile(bank(T, 4, NP_), t), tile(rr, t), T.ident)
            last.then_inc(s["rt_turned"], 1)
            for r in range(1, LEVELS):
                n = TILES if r < 3 else 4
                pe.wait_ge(s["boff_ready"], r)
                pe.wait_ge(s["rt_ready"], r)
                for t in range(n):
                    last = nc.tensor.matmul(tile(bank(T, 0, NP_), t), tile(boff, t), tile(rt, t), start=True, stop=True)
                last.then_inc(s["w_done"], 1)
                pe.wait_ge(s["w_out"], r)
                for t in range(n):
                    nc.tensor.matmul(tile(bank(T, 2, NP_), t), tile(wz, t), tile(rr, t), start=True, stop=True)
                for t in range(n):
                    last = nc.tensor.matmul(tile(bank(T, 4, NP_), t), tile(rr, t), tile(wz, t), start=True, stop=True)
                last.then_inc(s["z_done"], 1)
                if r == 1:
                    pe.wait_ge(s["vt_ready"], 1)
                    pe.wait_ge(s["w"][2], 16)
                if r < 3:
                    for t in range(4) if r == 1 else (4,):
                        for kk in range(KD):
                            last = nc.tensor.matmul(bank(T, 5 + r)[:, t % 4 * P:(t % 4 + 1) * P],
                                                    tile(T.xn[:, kk, :], t), T.wr[:, 2, kk, :],
                                                    start=(kk == 0), stop=(kk == KD - 1))
                    last.then_inc(s["ahead"], 1)
                elif more and r < 6:
                    ahead(3 + r, 7)
            pe.wait_ge(s["taken"], 9 if more else 6)
            for t in range(TILES):
                last = nc.tensor.transpose(tile(bank(T, 6, NP_), t), tile(k, t), T.ident)
            last.then_inc(s["kt_turned"], 1)
            pe.wait_ge(s["s_loaded"], 16)
            pe.wait_ge(s["level_done"], 1)
            for b in range(DEC_B):
                last = nc.tensor.matmul(bank(T, 4)[:, b * DEC_T:(b + 1) * DEC_T], T.s_in[:, b, :],
                                        k[:, SEQ + b * DEC_T:SEQ + (b + 1) * DEC_T], start=True, stop=True)
            last.then_inc(s["kss_done"], 1)
            pe.wait_ge(s["kss_copied"], 1)
            nc.tensor.transpose(bank(T, 5, P), kss[:, 0:P], T.ident).then_inc(s["kss_turned"], 1)
            pe.wait_ge(s["keys_ready"], 1)
            for t in range(4):
                if t:
                    pe.wait_ge(s["st_step"], t)
                    nc.tensor.matmul(bank(T, 0, P), tile(k, t), T.st[:, t, :], start=True, stop=True).then_inc(s["ks_done"], 1)
                pe.wait_ge(s["x_ready"], t + 1)
                nc.tensor.matmul(bank(T, 1, P), tile(rr, t), tile(xr, t), start=True, stop=True).then_inc(s["delta_done"], 1)
                pe.wait_ge(s["delta_ready"], t + 1)
                nc.tensor.matmul(bank(T, 6, P), T.kt[:, t, :], tile(delta, t), start=True, stop=True).then_inc(s["u_done"], 1)
                if more and t == 1:
                    ahead(9, 7)
            pe.wait_ge(s["x_ready"], 5)
            nc.tensor.matmul(bank(T, 1, P), tile(rr, 4), tile(xr, 4), start=True, stop=True).then_inc(s["delta_done"], 1)
            pe_sample_state(nc, pe, T, s)
            pe.wait_ge(s["sc_ready"], 1)
            pe.wait_ge(s["st_ready"], 1)
            pe_outputs(nc, pe, T, s, lambda t: tile(delta, t), qe, qe)
            if more:
                ahead(10, 0)
            pe_finish(nc, pe, T, s)
            if more:
                ahead(11, 0)

        @block.scalar
        def _(act):
            def take(u):
                if u < 4:
                    act_take(nc, act, T, s, u, 7, T.att[u // 2])
                else:
                    act_take(nc, act, T, s, u, 7 if u < 10 else 0, T.ret[u // 2 - 3],
                             ACT.Silu if u >= 10 else ACT.Copy)

            take(0)
            for c, dst in enumerate((q, k, v)):
                act.wait_ge(s["conv_done"], c + 1)
                nc.scalar.activation(dst[:, 0:N], dst[:, 0:N], ACT.Silu).then_inc(s["silu_done"], 1)
                if c < 2:
                    take(c + 1)
            act.wait_ge(s["silu_done"], 3)
            for c, src in enumerate((q, k)):
                nc.scalar.activation(sq[c][:, 0:N], src[:, 0:N], ACT.Square).then_inc(s["sq_done"], 1)
            for c in range(2):
                act.wait_ge(s["ss_eps"], c + 1)
                nc.scalar.activation(sq[c][:, 0:N], sq[c][:, 0:N], ACT.Sqrt).then_inc(s["ss_root"], 1)
            act.wait_ge(s["cum_done"], 1)
            nc.scalar.activation(ec, bank(T, 4, NP_), ACT.Exp).then_inc(s["ec_done"], 1)
            act.wait_ge(s["dec_in"], 1)
            nc.scalar.activation(dec, dec, ACT.Exp).then_inc(s["dec_exp"], 1)
            act.wait_ge(s["small_done"], 1)
            nc.scalar.activation(ecol, col, ACT.Exp)
            nc.scalar.activation(kcol, kcol, ACT.Exp)
            nc.scalar.activation(tcol, tcol, ACT.Exp)
            nc.scalar.activation(d8, d8, ACT.Exp).then_inc(s["exp_done"], 1)
            take(3)
            act.wait_ge(s["rt_turned"], 1)
            nc.scalar.copy(rt, bank(T, 4, NP_)).then_inc(s["rt_ready"], 1)
            for r in range(1, LEVELS):
                n = TILES if r < 3 else 4
                act.wait_ge(s["w_done"], r)
                nc.scalar.copy(wz[:, 0:n * P], bank(T, 0, n * P)).then_inc(s["w_out"], 1)
                if r < 3:
                    act.wait_ge(s["ahead"], r + 4)
                    tiles = range(4) if r == 1 else range(4, 5)
                    for t in tiles:
                        last = nc.scalar.copy(T.vt[:, t, 2 * P:3 * P], bank(T, 5 + r)[:, t % 4 * P:(t % 4 + 1) * P])
                    last.then_inc(s["taken"], 1)
                elif more and r < 6:
                    if r == 3:
                        act.wait_ge(s["conv_out"], 96)
                    take(3 + r)
            act.wait_ge(s["kss_done"], 1)
            nc.scalar.copy(kss[:, 0:NS], bank(T, 4)[:, 0:NS]).then_inc(s["kss_copied"], 1)
            for t in range(TILES):
                act.wait_ge(s["delta_done"], t + 1)
                nc.scalar.copy(tile(delta, t), bank(T, 1, P)).then_inc(s["delta_ready"], 1)
                if more and t == 1:
                    take(9)
            act_square(nc, act, T, s)
            if more:
                take(10)
            act_root(nc, act, T, s)
            if more:
                take(11)

        @block.vector
        def _(dve):
            link = chained(dve, s["chain_v"])
            wide = lambda ap: ap.unsqueeze(2).to_broadcast([P, TILES, P])
            link(nc.vector.tensor_copy(T.lgh, T.logg[:, :, bass.ds(h, 1)]))
            link(nc.vector.tensor_copy(T.bth, T.beta[:, :, bass.ds(h, 1)]))
            nc.vector.tensor_copy(tiled(btb), wide(T.bth[:, :, 0]))
            nc.vector.tensor_copy(tiled(lgb), wide(T.lgh[:, :, 0])).then_inc(s["lgb_ready"], 1)
            for c in range(3):
                link(nc.vector.memset(xp[c][:, 0:3], 0.0))
            dve.wait_ge(s["hist_in"], 48)
            for c, dst in enumerate((q, k, v)):
                tap = lambda j: T.ph[:, Q_CONV + 4 * c + j:Q_CONV + 4 * c + j + 1]
                ds = dst[:, SEQ:N].rearrange("p (s t) -> p s t", s=DEC_B)
                nc.vector.tensor_scalar(dst[:, 0:SEQ], xp[c][:, 0:SEQ], tap(0), None, ALU.mult)
                link(nc.vector.tensor_scalar(ds, hist(c)[:, :, 0:DEC_T], tap(0), None, ALU.mult))
                for j in range(1, 4):
                    nc.vector.scalar_tensor_tensor(out=dst[:, 0:SEQ], in0=xp[c][:, j:j + SEQ], scalar=tap(j),
                                                   in1=dst[:, 0:SEQ], op0=ALU.mult, op1=ALU.add)
                    link(nc.vector.scalar_tensor_tensor(out=ds, in0=hist(c)[:, :, j:j + DEC_T], scalar=tap(j),
                                                        in1=ds, op0=ALU.mult, op1=ALU.add))
                dve.sem_inc(s["conv_done"], 1)
            for c, dst in enumerate((q, k)):
                dve.wait_ge(s["ss_done"], c + 1)
                nc.vector.tensor_scalar(two(sq[c]), halves(T, 2 * c), EPS, None, ALU.add).then_inc(s["ss_eps"], 1)
            for c, dst in enumerate((q, k)):
                dve.wait_ge(s["ss_root"], c + 1)
                link(nc.vector.reciprocal(sq[c][:, 0:N], sq[c][:, 0:N]))
                nc.vector.scalar_tensor_tensor(out=dst[:, 0:N], in0=dst[:, 0:N], scalar=K_SCALE if c == 0 else 1.0,
                                               in1=sq[c][:, 0:N], op0=ALU.mult, op1=ALU.mult).then_inc(s["qk_ready"], 1)
            dve.wait_ge(s["cum_done"], 1)
            dve.wait_ge(s["col_done"], 1)
            link(nc.vector.tensor_copy(col, bank(T, 6)[:, 0:TILES]))
            link(nc.vector.tensor_copy(tcol, bank(T, 6)[:, TILES:2 * TILES]))
            link(nc.vector.tensor_copy(d8, bank(T, 6)[:, 2 * TILES:2 * TILES + DEC_B]))
            dve.sem_inc(s["cols_done"], 1)
            link(nc.vector.tensor_tensor(kcol, tcol, col, ALU.subtract))
            dve.sem_inc(s["small_done"], 1)
            dve.wait_ge(s["ec_done"], 1)
            for t in range(TILES):
                last = nc.vector.tensor_scalar(tile(dec, t), tile(bank(T, 4, NP_), t), col[:, t:t + 1], 0.0,
                                               ALU.subtract, ALU.min)
            last.then_inc(s["dec_in"], 1)
            dve.wait_ge(s["dec_exp"], 1)
            link(nc.vector.tensor_tensor(dec, dec, T.general[:, C_UT:C_UT + NP_], ALU.mult))
            dve.wait_ge(s["exp_done"], 1)
            dve.wait_ge(s["betab_done"], 1)
            dve.wait_ge(s["scored"], 1)
            link(nc.vector.tensor_tensor(bmat, bank(T, 0, NP_), dec, ALU.mult))
            link(nc.vector.tensor_tensor(bmat, bmat, bank(T, 4, NP_), ALU.mult))
            dve.wait_ge(s["scored"], 2)
            link(nc.vector.tensor_tensor(T.sc, bank(T, 2, NP_), dec, ALU.mult))
            dve.sem_inc(s["sc_ready"], 1)
            spread = lambda i, n=TILES: mask(i).unsqueeze(1).to_broadcast([P, n, P])
            link(nc.vector.tensor_tensor(tiled(rr), tiled(bmat), spread(1), ALU.mult))
            link(nc.vector.scalar_tensor_tensor(out=tiled(rr), in0=tiled(rr), scalar=-1.0, in1=spread(0),
                                                op0=ALU.mult, op1=ALU.add))
            dve.sem_inc(s["r1_ready"], 1)
            dve.wait_ge(s["turned"], 1)
            nc.vector.tensor_tensor(tiled(bv), bank(T, 6, NP_).rearrange("p (t i) -> p t i", t=TILES),
                                    wide(T.bth[:, :, 0]), ALU.mult).then_inc(s["vt_ready"], 1)
            link(nc.vector.tensor_tensor(qe, q, ec, ALU.mult))
            link(nc.vector.scalar_tensor_tensor(out=becol, in0=ecol, scalar=-1.0, in1=T.bth[:, :, 0],
                                                op0=ALU.mult, op1=ALU.mult))
            link(nc.vector.memset(kss, 0.0))
            for r in range(1, LEVELS):
                n = TILES if r < 3 else 4
                nc.vector.tensor_tensor(tiled(boff, n), tiled(bmat, n), spread(1 + r, n), ALU.mult
                                        ).then_inc(s["boff_ready"], 1)
                dve.wait_ge(s["z_done"], r)
                link(nc.vector.tensor_tensor(rr[:, 0:n * P], rr[:, 0:n * P], bank(T, 2, n * P), ALU.subtract))
                link(nc.vector.tensor_tensor(rt[:, 0:n * P], rt[:, 0:n * P], bank(T, 4, n * P), ALU.subtract))
                dve.sem_inc(s["rt_ready"], 1)
                if r == LEVELS - 1:
                    dve.sem_inc(s["level_done"], 1)
            dve.wait_ge(s["kt_turned"], 1)
            nc.vector.tensor_tensor(T.kt[:], bank(T, 6, NP_).rearrange("p (t i) -> p t i", t=TILES), wide(kcol),
                                    ALU.mult).then_inc(s["keys_ready"], 1)
            dve.wait_ge(s["keys_ready"], 1)
            for t in range(4):
                if t == 0:
                    nc.vector.tensor_copy(tile(xr, 0), tile(bv, 0)).then_inc(s["x_ready"], 1)
                else:
                    dve.wait_ge(s["ks_done"], t)
                    nc.vector.scalar_tensor_tensor(out=tile(xr, t), in0=bank(T, 0, P), scalar=becol[:, t:t + 1],
                                                   in1=tile(bv, t), op0=ALU.mult, op1=ALU.add).then_inc(s["x_ready"], 1)
                dve.wait_ge(s["u_done"], t + 1)
                if t == 0:
                    nc.vector.tensor_copy(T.st[:, 1, :], bank(T, 6, P)).then_inc(s["st_step"], 1)
                else:
                    nc.vector.scalar_tensor_tensor(out=T.st[:, t + 1, :], in0=T.st[:, t, :], scalar=tcol[:, t:t + 1],
                                                   in1=bank(T, 6, P), op0=ALU.mult, op1=ALU.add).then_inc(s["st_step"], 1)
                dve.wait_ge(s["st_step"], t + 1)
            dve.sem_inc(s["st_ready"], 1)
            dve.wait_ge(s["kss_turned"], 1)
            nc.vector.scalar_tensor_tensor(out=tile(xr, 4), in0=bank(T, 5, P), scalar=becol[:, 4:5],
                                           in1=tile(bv, 4), op0=ALU.mult, op1=ALU.add).then_inc(s["x_ready"], 1)
            dve.wait_ge(s["delta_ready"], 5)
            dve_spread_values(nc, T, s, delta[0:NS, 4 * P:5 * P])
            dve_sample_states(nc, dve, T, s, link, d8)
            dve_finish(nc, dve, T, s, link, T.ph[:, Q_GN:Q_GN + 1], slot, g)



def attention_stage(nc, T, l, h, slot, more):
    q, k = T.att
    w = lambda i: T.wk[:, i, :]
    sq = [w(2), w(3)]
    score = [w(2), w(3)]
    prob = [w(4), w(5)]
    diag = [w(6)[:, 0:P], w(6)[:, P:2 * P]]
    at = w(7)
    qm = T.wk[:, 8:10, :].rearrange("p a b -> p (a b)")[:, 0:(DEC_B + 1) * P]
    kc = T.wk[:, 10:14, :].rearrange("p a b -> p (a b)")[:, 0:DEC_B * PAST]
    vc = T.wk[:, 14:18, :].rearrange("p a b -> p (a b)")[:, 0:DEC_B * PAST]
    mx, sm = T.cols[:, 0:2], T.cols[:, 2:4]
    vt = lambda t: T.vt[:, t, 2 * P:3 * P]
    dc = T.dc
    names = ("values_in", "valued", "copied", "v_out", "pt_in", "kv_in", "sq_done", "ss_done", "ss_eps", "ss_root", "qk_ready",
             "k_out", "scored", "biased", "exp_in", "exped", "diag_ready", "turned", "at_ready", "o_tile",
             "qm_ready", "s_scored", "s_turned", "s_at")
    rounds = [(t, c) for t in range(4) for c in range(2)]
    with stage(nc, *names, *FINISH) as (block, s):
        @block.sync
        def _(sp):
            sp.dma_start(T.pt[0:1, :], T.d["page_table"]).then_inc(s["pt_in"], 16)
            if more:
                sp.dma_start(T.wtm, T.d["w_tm"][l, h + 1]).then_inc(s["values_in"], 16)
            sp.dma_start(T.d["v_prompt"][l, h].rearrange("(t p) d -> p t d", p=P),
                         T.vt[:, 0:4, 2 * P:3 * P]).then_inc(s["v_out"], 16)
            sp.dma_start(T.d["v_sample"][l, h], T.vt[0:NS, 4, 2 * P:3 * P]).then_inc(s["v_out"], 16)
            sp.wait_ge(s["pt_in"], 16)
            with sp.Fori(0, DEC_B * PAGES) as i:
                page = sp.value_load(T.pt[0:1, bass.ds(i, 1)], min_val=0, max_val=N_PHYS - 1)
                sp.dma_start(kc[:, bass.ds(i * PAGE, PAGE)], T.d["cache_k"][l, page, h]).then_inc(s["kv_in"], 16)
                sp.dma_start(vc[:, bass.ds(i * PAGE, PAGE)], T.d["cache_v"][l, page, h]).then_inc(s["kv_in"], 16)
            sp.wait_ge(s["qk_ready"], 2)
            sp.dma_start(T.d["k_out"][l, h], k[:, 0:N]).then_inc(s["k_out"], 16)
            sp.wait_ge(s["k_out"], 16)
            sp.wait_ge(s["v_out"], 32)

        @block.tensor
        def _(pe):
            def value_tile(t):
                if t:
                    pe.wait_ge(s["copied"], t)
                pe_value_tile(nc, T, t, 3).then_inc(s["valued"], 1)

            for c in range(2):
                pe.wait_ge(s["sq_done"], c + 1)
                wide_product(nc, T, 4 + 2 * c, lambda kk: T.general[:, C_COMP:C_COMP + P], lambda kk: sq[c],
                             1).then_inc(s["ss_done"], 1)
            if more:
                pe.wait_ge(s["values_in"], 16)
                value_tile(0)
                value_tile(1)
            pe.wait_ge(s["qk_ready"], 2)

            def scores(t, c):
                if t:
                    pe.wait_ge(s["biased"], 2 * (t - 1) + c + 1)
                rows = slice(c * DK, (c + 1) * DK)
                nc.tensor.matmul(bank(T, c)[:, 0:(t + 1) * P], tile(q, t)[rows], k[rows, 0:(t + 1) * P],
                                 start=True, stop=True).then_inc(s["scored"], 1)

            scores(0, 0)
            scores(0, 1)
            for t in range(4):
                pe.wait_ge(s["diag_ready"], 2 * (t + 1))
                for i in range(t + 1):
                    for c in range(2):
                        last = nc.tensor.matmul(tile(bank(T, 2), i), tile(prob[c], i), diag[c],
                                                start=(c == 0), stop=(c == 1))
                last.then_inc(s["turned"], 1)
                if t < 3:
                    scores(t + 1, 0)
                    scores(t + 1, 1)
                    if more:
                        value_tile(t + 2)
                pe.wait_ge(s["at_ready"], t + 1)
                for i in range(t + 1):
                    last = nc.tensor.matmul(tile(bank(T, 4), t), vt(i), tile(at, i), start=(i == 0), stop=(i == t))
                last.then_inc(s["o_tile"], 1)
            pe.wait_ge(s["qm_ready"], 1)
            pe.wait_ge(s["kv_in"], 32 * DEC_B * PAGES)
            new = bank(T, 0)[:, PAST:PAST + NS]
            pe.wait_ge(s["biased"], 8)
            nc.tensor.matmul(new, qm[:, DEC_B * P:(DEC_B + 1) * P], k[:, SEQ:N], start=True, stop=True)
            for b in range(DEC_B):
                last = nc.tensor.matmul(bank(T, 0)[:, 0:PAST], tile(qm, b), kc[:, b * PAST:(b + 1) * PAST],
                                        start=(b == 0), stop=(b == DEC_B - 1))
            last.then_inc(s["s_scored"], 1)
            pe.wait_ge(s["diag_ready"], 9)
            for i in range(PAGES):
                nc.tensor.matmul(bank(T, 2)[:, i * NS:(i + 1) * NS], tile(prob[0], i), diag[0][:, 0:NS],
                                 start=True, stop=True)
            nc.tensor.matmul(bank(T, 2)[0:NS, PAGES * NS:(PAGES + 1) * NS], prob[0][:, PAST:PAST + NS],
                             diag[0][:, 0:NS], start=True, stop=True).then_inc(s["s_turned"], 1)
            pe.wait_ge(s["s_at"], 2)
            o = bank(T, 5)
            nc.tensor.matmul(o[:, 0:NS], T.vt[0:NS, 4, 2 * P:3 * P], at[0:NS, PAGES * NS:(PAGES + 1) * NS],
                             start=True, stop=False)
            for b in range(DEC_B):
                for i in range(PAGES):
                    last = nc.tensor.matmul(o[:, b * DEC_T:(b + 1) * DEC_T], tile(vc, b * PAGES + i),
                                            at[:, i * NS + b * DEC_T:i * NS + (b + 1) * DEC_T], start=False,
                                            stop=(b == DEC_B - 1 and i == PAGES - 1))
            last.then_inc(s["o_ready"], 1)
            pe_finish(nc, pe, T, s)

        @block.scalar
        def _(act):
            def copy_values(t):
                act.wait_ge(s["valued"], t + 1)
                nc.scalar.copy(T.vt[:, t, 0:2 * P], bank(T, 3)[:, 0:2 * P]).then_inc(s["copied"], 1)

            for c, src in enumerate((q, k)):
                nc.scalar.activation(sq[c][:, 0:N], src[:, 0:N], ACT.Square).then_inc(s["sq_done"], 1)
            for c in range(2):
                act.wait_ge(s["ss_eps"], c + 1)
                nc.scalar.activation(sq[c][:, 0:N], sq[c][:, 0:N], ACT.Sqrt).then_inc(s["ss_root"], 1)
            if more:
                copy_values(0)
                copy_values(1)
            for i, (t, c) in enumerate(rounds):
                act.wait_ge(s["exp_in"], i + 1)
                if t:
                    act.wait_ge(s["turned"], t)
                nc.scalar.activation(prob[c][:, 0:(t + 1) * P], score[c][:, 0:(t + 1) * P], ACT.Exp,
                                     bias=mx[:, c:c + 1], scale=S_SCALE, accum_out=sm[:, c:c + 1]).then_inc(s["exped"], 1)
                if c == 1:
                    act.wait_ge(s["turned"], t + 1)
                    if t:
                        act.wait_ge(s["o_tile"], t)
                    nc.scalar.copy(at[:, 0:(t + 1) * P], bank(T, 2)[:, 0:(t + 1) * P]).then_inc(s["at_ready"], 1)
                    if more and t < 3:
                        copy_values(t + 2)
            act.wait_ge(s["exp_in"], 9)
            nc.scalar.activation(prob[0][:, 0:PAST + NS], score[0][:, 0:PAST + NS], ACT.Exp, bias=mx[:, 0:1],
                                 scale=S_SCALE, accum_out=sm[:, 0:1]).then_inc(s["exped"], 1)
            act.wait_ge(s["s_turned"], 1)
            act.wait_ge(s["o_tile"], 4)
            nc.scalar.copy(at[:, 0:PAGES * NS], bank(T, 2)[:, 0:PAGES * NS]).then_inc(s["s_at"], 1)
            nc.scalar.copy(at[0:NS, PAGES * NS:(PAGES + 1) * NS],
                           bank(T, 2)[0:NS, PAGES * NS:(PAGES + 1) * NS]).then_inc(s["s_at"], 1)
            act_square(nc, act, T, s)
            act_root(nc, act, T, s)

        @block.vector
        def _(dve):
            link = chained(dve, s["chain_v"])
            for c in range(2):
                dve.wait_ge(s["ss_done"], c + 1)
                nc.vector.tensor_scalar(two(sq[c]), halves(T, 4 + 2 * c), 1.0 / DK, EPS, ALU.mult,
                                        ALU.add).then_inc(s["ss_eps"], 1)
            for c, dst in enumerate((q, k)):
                dve.wait_ge(s["ss_root"], c + 1)
                link(nc.vector.reciprocal(sq[c][:, 0:N], sq[c][:, 0:N]))
                nc.vector.scalar_tensor_tensor(out=dst[:, 0:N], in0=dst[:, 0:N],
                                               scalar=T.ph[:, Q_QN + c:Q_QN + c + 1], in1=sq[c][:, 0:N],
                                               op0=ALU.mult, op1=ALU.mult).then_inc(s["qk_ready"], 1)
            dve.wait_ge(s["qk_ready"], 2)
            slope = T.hc[:, H_SL:H_SL + 1]

            def softmax_input(i, c, dist, src, n):
                if i >= 2:
                    dve.wait_ge(s["exped"], min(i, 8) - 1 if i < 8 else 8)
                nc.vector.scalar_tensor_tensor(out=score[c][:, 0:n], in0=dist, scalar=slope, in1=src,
                                               op0=ALU.mult, op1=ALU.add).then_inc(s["biased"], 1)
                dve.wait_ge(s["biased"], i + 1)
                link(nc.vector.tensor_reduce(mx[:, c:c + 1], score[c][:, 0:n], AX_X, ALU.max))
                nc.vector.tensor_scalar(mx[:, c:c + 1], mx[:, c:c + 1], -S_SCALE, None, ALU.mult).then_inc(s["exp_in"], 1)

            for t in range(4):
                n = (t + 1) * P
                for c in range(2):
                    i = 2 * t + c
                    dve.wait_ge(s["scored"], i + 1)
                    softmax_input(i, c, dc[:, C_DP + SEQ - n:C_DP + SEQ], bank(T, c)[:, 0:n], n)
                for c in range(2):
                    i = 2 * t + c
                    dve.wait_ge(s["exped"], i + 1)
                    if t:
                        dve.wait_ge(s["turned"], t)
                    link(nc.vector.reciprocal(sm[:, c:c + 1], sm[:, c:c + 1]))
                    if c:
                        link(nc.vector.tensor_scalar(sm[:, 1:2], sm[:, 1:2], T.lam[:, 2:3], None, ALU.mult))
                    nc.vector.tensor_scalar(diag[c], T.ident, sm[:, c:c + 1], None, ALU.mult
                                            ).then_inc(s["diag_ready"], 1)
            nc.vector.tensor_tensor(qm.rearrange("p (a t) -> p a t", t=NS),
                                    q[:, SEQ:N].unsqueeze(1).to_broadcast([P, 2 * (DEC_B + 1), NS]),
                                    dc[:, C_QM:C_QM + (DEC_B + 1) * P].rearrange("p (a t) -> p a t", t=NS),
                                    ALU.mult).then_inc(s["qm_ready"], 1)
            dve.wait_ge(s["s_scored"], 1)
            softmax_input(8, 0, dc[:, C_DS:C_DS + PAST + NS], bank(T, 0)[:, 0:PAST + NS], PAST + NS)
            dve.wait_ge(s["exped"], 9)
            dve.wait_ge(s["turned"], 4)
            link(nc.vector.reciprocal(sm[:, 0:1], sm[:, 0:1]))
            link(nc.vector.tensor_scalar(sm[:, 0:1], sm[:, 0:1], T.lam[:, 3:4], None, ALU.mult))
            nc.vector.tensor_scalar(diag[0][:, 0:NS], dc[:, C_STK:C_STK + NS], sm[:, 0:1], None, ALU.mult
                                    ).then_inc(s["diag_ready"], 1)
            link(nc.vector.tensor_tensor(T.cols[:, 4:5], T.ph[:, Q_DN:Q_DN + 1], T.pl[:, L_OL:L_OL + 1], ALU.mult))
            dve_finish(nc, dve, T, s, link, T.cols[:, 4:5], slot, None)


def head(nc, T, l, h, more):
    retention_stage(nc, T, l, h, br_slot(0, h))
    hgrn_stage(nc, T, l, h, br_slot(1, h))
    gdn_stage(nc, T, l, h, br_slot(2, h), more)
    attention_stage(nc, T, l, h, br_slot(3, h), more)


def merge_stage(nc, T, l):
    with stage(nc, "w_even", "w_odd", "w_free", "gated", "sig_done", "added", "chain_v") as (block, s):
        w_in = (s["w_even"], s["w_odd"])

        @block.sync
        def _(sp):
            with sp.Fori(0, KD) as m:
                for b in range(4):
                    sp.wait_ge(s["w_free"], 4 * m + b + 1)
                    sp.dma_start(T.wm[:, b % 2], T.d["w_merge"][l, m, b]).then_inc(w_in[b % 2], 16)

        @block.tensor
        def _(pe):
            pe.sem_inc(s["w_free"], 2)
            with pe.Fori(0, KD) as m:
                for b in range(4):
                    i = b % 2
                    pe.wait_ge(w_in[i], 32 * m + 16 * (b // 2) + 16)
                    pe.wait_ge(s["added"], 4 * m + b + 1)
                    wide_product(nc, T, 4 * i, lambda k: T.wm[:, i, k, :], lambda k: T.xn[:, k, :], KD
                                 ).then_inc(s["gated"], 1)
                    wide_product(nc, T, 4 * i + 2, lambda k: T.wm[:, i, KD + k, :],
                                 lambda k: T.br[:, 4 * b + k, :], 4).then_inc(s["w_free"], 1)

        @block.scalar
        def _(act):
            with act.Fori(0, KD) as m:
                for b in range(4):
                    i = b % 2
                    act.wait_ge(s["gated"], 4 * m + b + 1)
                    act.wait_ge(s["added"], 4 * m + b + 1)
                    nc.scalar.activation(T.sg[i], halves(T, 4 * i), ACT.Sigmoid).then_inc(s["sig_done"], 1)

        @block.vector
        def _(dve):
            dve.sem_inc(s["added"], 2)
            with dve.Fori(0, KD) as m:
                for b in range(4):
                    i = b % 2
                    dve.wait_ge(s["sig_done"], 4 * m + b + 1)
                    dve.wait_ge(s["w_free"], 4 * m + b + 3)
                    if b == 0:
                        dve.wait_ge(s["added"], 4 * m + 2)
                        nc.vector.tensor_tensor(T.ma, T.sg[i], halves(T, 4 * i + 2), ALU.mult).then_inc(s["added"], 1)
                    else:
                        nc.vector.tensor_tensor(T.sg[i], T.sg[i], halves(T, 4 * i + 2), ALU.mult
                                                ).then_inc(s["chain_v"], 1)
                        dve.wait_ge(s["chain_v"], 3 * m + b)
                        dve.wait_ge(s["added"], 4 * m + b + 2)
                        out = T.ma if b < 3 else two(T.mt[:, bass.ds(m, 1), :].rearrange("p a n -> p (a n)"))
                        nc.vector.tensor_tensor(out, T.ma, T.sg[i], ALU.add).then_inc(s["added"], 1)


def out_stage(nc, T, l):
    with stage(nc, "w_even", "w_odd", "h_in", "produced", "added", "h_out") as (block, s):
        w_in = (s["w_even"], s["w_odd"])

        @block.sync
        def _(sp):
            sp.dma_start(T.h[:], T.d["xs"].rearrange("m p n -> p m n")).then_inc(s["h_in"], 16)
            with sp.Fori(0, KD // 2) as g:
                for i in range(2):
                    sp.wait_ge(s["produced"], 2 * g + i + 1)
                    sp.dma_start(T.wm[:, i, 0:KD, :], T.d["w_out"][l, 2 * g + i]).then_inc(w_in[i], 16)
            sp.wait_ge(s["added"], KD + 2)
            sp.dma_start(T.d["xs"].rearrange("m p n -> p m n"), T.h[:]).then_inc(s["h_out"], 16)
            sp.wait_ge(s["h_out"], 16)

        @block.tensor
        def _(pe):
            pe.sem_inc(s["produced"], 2)
            with pe.Fori(0, KD // 2) as g:
                for i in range(2):
                    pe.wait_ge(w_in[i], 16 * g + 16)
                    pe.wait_ge(s["added"], 2 * g + i + 1)
                    wide_product(nc, T, 2 * i, lambda k: T.wm[:, i, k, :], lambda k: T.mt[:, k, :], KD
                                 ).then_inc(s["produced"], 1)

        @block.vector
        def _(dve):
            dve.sem_inc(s["added"], 2)
            dve.wait_ge(s["h_in"], 16)
            with dve.Fori(0, KD // 2) as g:
                for i in range(2):
                    dve.wait_ge(s["produced"], 2 * g + i + 3)
                    row = two(T.h[:, bass.ds(2 * g + i, 1), :].rearrange("p a n -> p (a n)"))
                    nc.vector.tensor_tensor(row, row, halves(T, 2 * i), ALU.add).then_inc(s["added"], 1)


def key_scores_stage(nc, T, l):
    with stage(nc, "w_even", "w_odd", "keys_in", "w_free", "q_done", "q_out", "scored", "kept",
               "zeroed") as (block, s):
        w_in = (s["w_even"], s["w_odd"])

        @block.sync
        def _(sp):
            sp.dma_start(T.keys, T.d["keys"][l]).then_inc(s["keys_in"], 16)
            with sp.Fori(0, PH_HEADS) as g:
                for i in range(2):
                    sp.wait_ge(s["q_done"], 2 * g + i + 1)
                    sp.dma_start(T.wm2[:, i], T.d["w_query"][l, 2 * g + i]).then_inc(w_in[i], 16)

        @block.tensor
        def _(pe):
            pe.sem_inc(s["q_done"], 2)
            pe.wait_ge(s["keys_in"], 16)
            with pe.Fori(0, PH_HEADS) as g:
                for i in range(2):
                    pe.wait_ge(w_in[i], 16 * g + 16)
                    pe.wait_ge(s["q_out"], 2 * g + i + 1)
                    wide_product(nc, T, 2 * i, lambda k: T.wm2[:, i, k, :], lambda k: T.xn[:, k, :], KD
                                 ).then_inc(s["q_done"], 1)
                    pe.wait_ge(s["q_out"], 2 * g + i + 3)
                    pe.wait_ge(s["kept"], 2 * g + i + 1)
                    for t in range(TILES):
                        last = nc.tensor.matmul(tile(bank(T, 4 + 2 * i, NP_), t), tile(T.qt[i], t),
                                                T.keys[:, bass.ds(2 * g + i, 1), :].rearrange("p a n -> p (a n)"),
                                                start=True, stop=True)
                    last.then_inc(s["scored"], 1)

        @block.scalar
        def _(act):
            act.wait_ge(s["zeroed"], 1)
            act.sem_inc(s["q_out"], 2)
            with act.Fori(0, PH_HEADS) as g:
                for i in range(2):
                    act.wait_ge(s["q_done"], 2 * g + i + 3)
                    act.wait_ge(s["kept"], 2 * g + i + 1)
                    nc.scalar.copy(two(T.qt[i]), halves(T, 2 * i)).then_inc(s["q_out"], 1)

        @block.vector
        def _(dve):
            for i in range(2):
                last = nc.vector.memset(T.qt[i], 0.0)
            last.then_inc(s["zeroed"], 1)
            dve.sem_inc(s["kept"], 2)
            with dve.Fori(0, PH_HEADS) as g:
                for i in range(2):
                    dve.wait_ge(s["scored"], 2 * g + i + 1)
                    nc.vector.tensor_copy(T.scr[:, :, bass.ds(2 * g + i, 1), :],
                                          bank(T, 4 + 2 * i, NP_).rearrange("p (t a k) -> p t a k", t=TILES, a=1)
                                          ).then_inc(s["kept"], 1)


def retrieval_stage(nc, T, l):
    LOW = -3.0e38
    STEPS = 20
    with stage(nc, "u_even", "u_odd", "dotted", "activated", "chain_v", "exp_in", "exped", "found", "turned",
               "tail") as (block, s):
        @block.sync
        def _(sp):
            sp_expert_weights(sp, T, s, T.d["u"], l, 0)

        @block.scalar
        def _(act):
            act_gelu(nc, act, T, s, 0)
            act.wait_ge(s["exp_in"], 1)
            nc.scalar.activation(T.t2[:], T.t2[:], ACT.Exp).then_inc(s["exped"], 1)

        @block.tensor
        def _(pe):
            pe.sem_inc(s["dotted"], 2)
            with pe.Fori(0, PART // 2) as j:
                for i in range(2):
                    pe_expert_dots(nc, pe, T, s, j, i)
            pe.wait_ge(s["found"], 1)
            for z in range(3):
                pe.wait_ge(s["turned"], z)
                if z:
                    pe.wait_ge(s["tail"], z)
                for t in range(TILES):
                    last = nc.tensor.transpose(tile(bank(T, 4, NP_), t), T.found[:, z, t, :], T.ident)
                last.then_inc(s["turned"], 1)

        @block.vector
        def _(dve):
            count = [0]

            def link(instruction, t):
                count[0] += 1
                instruction.then_inc(s["chain_v"], 1)
                dve.wait_ge(s["chain_v"], STEPS * t + count[0])

            def best(t, values, idx, scores):
                rows = range(scores.shape[1])
                v = nc.vector
                for r in range(2):
                    part = slice(8 * r, 8 * r + 8)
                    v.memset(T.spare, 0.0)
                    for j in rows:
                        last = v.max(values[:, j, part], scores[:, j, :])
                    link(last, t)
                    v.memset(T.spare, 0.0)
                    for j in rows:
                        last = v.max_index(idx[:, j, part], values[:, j, part], scores[:, j, :])
                    link(last, t)
                    if r == 0:
                        v.memset(T.spare, 0.0)
                        for j in rows:
                            last = v.match_replace(scores[:, j, :], values[:, j, part], scores[:, j, :], LOW)
                        link(last, t)

            with dve.Fori(0, TILES) as t:
                count[0] = 0
                link(nc.vector.tensor_copy(T.x1, T.scr[:, bass.ds(t, 1)].rearrange("p a h k -> p (a h) k")), t)
                best(t, T.t1, T.i1u, T.x1)
                nc.vector.tensor_copy(T.i1f, T.i1u)
                side = T.t1.rearrange("p (h z) a -> p h z a", z=2)
                link(nc.vector.tensor_tensor(
                    T.cand.rearrange("p h (a b) -> p h a b", a=TOPK),
                    side[:, :, 0, :].unsqueeze(3).to_broadcast([P, PH_HEADS, TOPK, TOPK]),
                    side[:, :, 1, :].unsqueeze(2).to_broadcast([P, PH_HEADS, TOPK, TOPK]), ALU.add), t)
                best(t, T.tv, T.posu, T.cand)
                nc.vector.tensor_copy(T.t2[:, bass.ds(t, 1)].rearrange("p a h k -> p (a h) k"), T.tv)
                nc.vector.tensor_scalar(T.pau, T.posu, 4, None, ALU.logical_shift_right)
                link(nc.vector.tensor_scalar(T.pbu, T.posu, 15, None, ALU.bitwise_and), t)
                nc.vector.tensor_copy(T.paf, T.pau)
                link(nc.vector.tensor_copy(T.pbf, T.pbu), t)
                sidei = T.i1f.rearrange("p (h z) a -> p h z a", z=2)
                iota = T.iota[:, 0:TOPK].unsqueeze(1).to_broadcast([P, P, TOPK])
                for z, place in enumerate((T.paf, T.pbf)):
                    eq = T.x1.rearrange("p h k -> p (h k)").rearrange("p (c a) -> p c a", a=TOPK)
                    link(nc.vector.tensor_tensor(eq, place.rearrange("p h k -> p (h k)").unsqueeze(2).to_broadcast(
                        [P, P, TOPK]), iota, ALU.is_equal), t)
                    eq4 = eq.rearrange("p (h k) a -> p h k a", h=PH_HEADS)
                    link(nc.vector.tensor_tensor(eq4, eq4, sidei[:, :, z, :].unsqueeze(2).to_broadcast(
                        [P, PH_HEADS, TOPK, TOPK]), ALU.mult), t)
                    out = T.found[:, z, bass.ds(t, 1), :].rearrange("p a c -> p (a c)")
                    if z == 0:
                        link(nc.vector.tensor_reduce(out, eq, AX_X, ALU.add), t)
                    else:
                        nc.vector.tensor_reduce(out, eq, AX_X, ALU.add).then_inc(s["chain_v"], 1)
                        dve.wait_ge(s["chain_v"], STEPS * t + STEPS)
                assert count[0] == STEPS - 1
            done = [STEPS * TILES]

            def then(instruction):
                done[0] += 1
                instruction.then_inc(s["chain_v"], 1)
                dve.wait_ge(s["chain_v"], done[0])

            t2 = T.t2.rearrange("p t h k -> p (t h) k")
            rows = [P, TILES * PH_HEADS, TOPK]
            then(nc.vector.tensor_copy(T.gs, t2[:, :, 0]))
            nc.vector.tensor_tensor(t2, t2, T.gs.unsqueeze(2).to_broadcast(rows), ALU.subtract
                                    ).then_inc(s["exp_in"], 1)
            dve.wait_ge(s["exped"], 1)
            then(nc.vector.tensor_reduce(T.gs, t2, AX_X, ALU.add))
            then(nc.vector.reciprocal(T.gs, T.gs))
            then(nc.vector.scalar_tensor_tensor(
                out=T.found[:, 2].rearrange("p t (h k) -> p (t h) k", k=TOPK), in0=t2, scalar=G_SCALE,
                in1=T.gs.unsqueeze(2).to_broadcast(rows), op0=ALU.mult, op1=ALU.mult))
            dve.sem_inc(s["found"], 1)
            for z in range(2):
                dve.wait_ge(s["turned"], z + 1)
                nc.vector.tensor_copy(T.idx[:, z, :], bank(T, 4, NP_)).then_inc(s["tail"], 1)
            dve.wait_ge(s["tail"], 2)
            dve.wait_ge(s["turned"], 3)
            then(nc.vector.tensor_copy(T.idx[:, 2, :], bank(T, 4, NP_)))
            then(nc.vector.tensor_tensor(T.idx[:, 3, :], bank(T, 4, NP_), T.idx[:, 2, :], ALU.subtract))


def sp_expert_weights(sp, T, s, table, l, part):
    with sp.Fori(0, PART // 2) as j:
        for i in range(2):
            sp.wait_ge(s["dotted"], 2 * j + i + 1)
            sp.dma_start(T.ur[:, i], table[l, part, 2 * j + i]).then_inc(s["u_odd" if i else "u_even"], 16)


def pe_expert_dots(nc, pe, T, s, j, i):
    pe.wait_ge(s["u_odd" if i else "u_even"], 16 * j + 16)
    pe.wait_ge(s["activated"], 2 * j + i + 1)
    wide_product(nc, T, 2 * i, lambda k: T.ur[:, i, k, :], lambda k: T.xn[:, k, :], KD).then_inc(s["dotted"], 1)


def act_gelu(nc, act, T, s, part):
    g = T.g[part % 2]
    act.sem_inc(s["activated"], 2)
    with act.Fori(0, PART // 2) as j:
        for i in range(2):
            act.wait_ge(s["dotted"], 2 * j + i + 3)
            nc.scalar.activation(two(g[:, bass.ds(2 * j + i, 1), :].rearrange("p a n -> p (a n)")),
                                 halves(T, 2 * i), ACT.Gelu).then_inc(s["activated"], 1)


def coefficient_stage(nc, T, l, part):
    ahead = part + 1 < PARTS
    g = T.g[part % 2]
    with stage(nc, "u_even", "u_odd", "dotted", "activated", "iota_ready", "rows_ready", "eq_ready", "summed",
               "kept") as (block, s):
        if ahead:
            @block.sync
            def _(sp):
                sp_expert_weights(sp, T, s, T.d["u"], l, part + 1)

            @block.scalar
            def _(act):
                act_gelu(nc, act, T, s, part + 1)

        @block.tensor
        def _(pe):
            pe.sem_inc(s["dotted"], 2)
            pe.sem_inc(s["kept"], 2)
            with pe.Fori(0, PART // 2) as j:
                for i in range(2):
                    if ahead:
                        pe_expert_dots(nc, pe, T, s, j, i)
                    pe.wait_ge(s["rows_ready"], 2 * j + i + 1)
                    pe.wait_ge(s["kept"], 2 * j + i + 1)
                    for n in range(GT):
                        out = bank(T, 4 + 2 * i + n // (GT // 2))[:, n % (GT // 2) * PART:][:, 0:PART]
                        for z in range(2):
                            last = nc.tensor.matmul(out, T.oh1[:, i, n, :], T.oh2[:, i, n, z, :],
                                                    start=(z == 0), stop=(z == 1))
                    last.then_inc(s["summed"], 1)

        @block.vector
        def _(dve):
            nc.vector.tensor_copy(T.iota_h, T.iota[:, part * PART:(part + 1) * PART]).then_inc(s["iota_ready"], 1)
            dve.wait_ge(s["iota_ready"], 1)
            dve.sem_inc(s["summed"], 2)

            def rows(j, i):
                cols = bass.ds((2 * j + i) * GT, GT)
                one = lambda z: T.idx[:, z, cols]
                dve.wait_ge(s["summed"], 2 * j + i + 1)
                nc.vector.tensor_tensor(T.oh1[:, i], T.iota_b.unsqueeze(1).to_broadcast([P, GT, P]),
                                        one(0).unsqueeze(2).to_broadcast([P, GT, P]), ALU.is_equal)
                nc.vector.tensor_tensor(T.eq2[:, i], T.iota_h.unsqueeze(1).to_broadcast([P, GT, PART]),
                                        one(1).unsqueeze(2).to_broadcast([P, GT, PART]), ALU.is_equal
                                        ).then_inc(s["eq_ready"], 1)
                dve.wait_ge(s["eq_ready"], 2 * j + i + 1)
                nc.vector.tensor_tensor(T.oh2[:, i], T.eq2[:, i].unsqueeze(2).to_broadcast([P, GT, 2, PART]),
                                        T.idx[:, 2:4, cols].rearrange("p z n -> p n z").unsqueeze(3).to_broadcast(
                                            [P, GT, 2, PART]), ALU.mult).then_inc(s["rows_ready"], 1)

            def weigh(j, i):
                dve.wait_ge(s["summed"], 2 * j + i + 3)
                for a in range(2):
                    dst = g[:, :, bass.ds((2 * j + i) * GT + a * (GT // 2), GT // 2)]
                    src = bank(T, 4 + 2 * i + a, GT // 2 * PART).rearrange("p (n i) -> p i n", i=PART)
                    last = nc.vector.scalar_tensor_tensor(out=dst, in0=src, scalar=1.0 / G_SCALE, in1=dst,
                                                          op0=ALU.mult, op1=ALU.mult)
                last.then_inc(s["kept"], 1)

            with dve.Fori(0, PART // 2) as j:
                for i in range(2):
                    rows(j, i)
                for i in range(2):
                    weigh(j, i)


def expert_out_stage(nc, T, l, part):
    g = T.g[part % 2]
    for group in range(2):
        with stage(nc, "v_even", "v_odd", "v_free", "v_high", "v_low", "used", "h_in", "added", "h_out",
                   "zeroed") as (block, s):
            v_in = (s["v_even"], s["v_odd"])

            @block.sync
            def _(sp):
                for m in range(4):
                    sp.dma_start(T.ht[:, m, :], T.d["xs"][4 * group + m]).then_inc(s["h_in"], 16)
                with sp.Fori(0, PART // 4) as c:
                    for i in range(2):
                        sp.wait_ge(s["v_free"], 4 * c + 2 * i + 2)
                        sp.dma_start(T.vr[:, i], T.d["v"][l, part, group, 2 * c + i]).then_inc(v_in[i], 16)
                sp.wait_ge(s["added"], 4)
                sp.dma_start(T.d["xs"][4 * group:4 * group + 4].rearrange("m p n -> p m n"), T.ht[:]
                             ).then_inc(s["h_out"], 16)
                sp.wait_ge(s["h_out"], 16)

            @block.scalar
            def _(act):
                with act.Fori(0, PART // 4) as c:
                    for i in range(4):
                        slot = i % 2
                        row = g[:, bass.ds(4 * c + i, 1), :].rearrange("p a n -> p (a n)")
                        act.wait_ge(s["used"], 4 * c + i + 1)
                        nc.scalar.copy(T.gh[:, slot, :], row)
                        if i % 2 == 0:
                            act.wait_ge(v_in[i // 2], 16 * c + 16)
                        nc.scalar.copy(T.vh[:, slot, :], T.vr[:, i // 2, i % 2, :]).then_inc(s["v_high"], 1)

            @block.vector
            def _(dve):
                with dve.Fori(0, PART // 4) as c:
                    for i in range(4):
                        slot = i % 2
                        row = g[:, bass.ds(4 * c + i, 1), :].rearrange("p a n -> p (a n)")
                        dve.wait_ge(s["v_high"], 4 * c + i + 1)
                        nc.vector.tensor_tensor(T.gl[:, slot, :], row, T.gh[:, slot, :].bitcast(F32), ALU.subtract)
                        nc.vector.tensor_tensor(T.vl[:, slot, :], T.vr[:, i // 2, i % 2, :],
                                                T.vh[:, slot, :].bitcast(F32), ALU.subtract).then_inc(s["v_low"], 1)
                        dve.wait_ge(s["v_low"], 4 * c + i + 1)
                        dve.sem_inc(s["v_free"], 1)
                dve.wait_ge(s["used"], PART + 2)
                for m in range(4):
                    if m == 0:
                        dve.wait_ge(s["h_in"], 64)
                    nc.vector.tensor_tensor(two(T.ht[:, m, :]), two(T.ht[:, m, :]), halves(T, 2 * m), ALU.add
                                            ).then_inc(s["added"], 1)

            @block.tensor
            def _(pe):
                pe.sem_inc(s["used"], 2)
                pe.sem_inc(s["v_free"], 4)
                for b in range(8):
                    nc.tensor.matmul(bank(T, b)[:, 0:HALF], T.zero[:, 0:P], T.zero[:, 0:HALF], start=True, stop=False,
                                     skip_group_check=True)
                with pe.Fori(0, PART // 4) as c:
                    for i in range(4):
                        slot = i % 2
                        pe.wait_ge(s["v_low"], 4 * c + i + 1)
                        for m in range(4):
                            cols = slice(m * P, (m + 1) * P)
                            for vp, gp in ((T.vh, T.gh), (T.vh, T.gl), (T.vl, T.gh)):
                                for a in range(2):
                                    last = nc.tensor.matmul(bank(T, 2 * m + a)[:, 0:HALF], vp[:, slot, cols],
                                                            gp[:, slot, a * HALF:(a + 1) * HALF],
                                                            start=False, stop=False, skip_group_check=True)
                        last.then_inc(s["used"], 1)


def program(nc, d):
    T = Memory()
    T.d = d
    with ExitStack() as keep:
        def sb(ctx, name, shape, dt=F32):
            return ctx.enter_context(nc.sbuf_tensor(name, shape, dt))

        T.ps = keep.enter_context(nc.psum_tensor("ps", [P, 8 * BANK], F32))
        T.xn = sb(keep, "xn", [P, KD, NP_])
        core = sb(keep, "core", [P, 2, P])
        T.ident, T.ones = core[:, 0, :], core[:, 1, :]
        with stage(nc, "x_in") as (block, s):
            @block.sync
            def _(sp):
                sp.dma_start(d["xs"], d["x"]).then_inc(s["x_in"], 16)
                sp.dma_start(T.ident, d["gc"][:, C_MSK:C_MSK + P]).then_inc(s["x_in"], 16)
                sp.dma_start(T.ones, d["gc"][:, C_ONES:C_ONES + P]).then_inc(s["x_in"], 16)
                sp.wait_ge(s["x_in"], 48)
        with nc.Fori(0, DEPTH) as l:
            with ExitStack() as ctx:
                T.general = sb(ctx, "gc", [P, GC_W])
                T.pl = sb(ctx, "pl", [P, PL_W])
                T.pr = sb(ctx, "pr", [P, 9, NP_])
                row = lambda i: T.pr[:, i, :]
                T.hgrn = [row(0), row(1), row(2), row(3)]
                T.gdn, T.gdn_gate = [row(0), row(1), row(2)], row(7)
                T.conv = T.ret = [row(4), row(5), row(6)]
                T.att = [row(8), row(3)]
                T.hc = sb(ctx, "hc", [P, HC_W])
                T.ph = sb(ctx, "ph", [P, PH_W])
                T.vt = sb(ctx, "vt", [P, TILES, 3 * P])
                T.br = sb(ctx, "br", [P, 16, N])
                T.st = sb(ctx, "st", [P, 5, P])
                T.s_in = sb(ctx, "s_in", [P, DEC_B, P])
                T.s_new = sb(ctx, "s_new", [P, DEC_B, P])
                T.kt = sb(ctx, "kt", [P, TILES, P])
                T.cols = sb(ctx, "cols", [P, 40])
                small = sb(ctx, "small", [P, 256])
                T.logg = small[:, 0:20].rearrange("p (t c) -> p t c", t=TILES)
                T.beta = small[:, 20:40].rearrange("p (t c) -> p t c", t=TILES)
                T.ga = small[:, 40:60].rearrange("p (t c) -> p t c", t=TILES)
                T.ga2 = small[:, 60:80].rearrange("p (t c) -> p t c", t=TILES)
                T.nea = small[:, 80:84]
                T.lam = small[:, 84:88]
                T.lb = small[:, 88:92]
                T.lgh = small[:, 96:101].unsqueeze(2)
                T.bth = small[:, 104:109].unsqueeze(2)
                T.lprod = small[:, 128:256].rearrange("p (a d) -> p a d", a=2)
                rs = sb(ctx, "rs", [P, N])
                T.rs = two(rs[:])
                T.tot = sb(ctx, "tot", [P, NP_])[:]
                T.pt = sb(ctx, "pt", [P, DEC_B * PAGES], I32)
                with ExitStack() as sub:
                    T.wr = sb(sub, "wr", [P, 4, KD, P])
                    T.wk = sb(sub, "wk", [P, 20, NP_])
                    flat = T.wk.rearrange("p a b -> p (a b)")
                    T.wtm = T.wr.rearrange("p a k c -> p (a k c)")[:, 0:KD * 2 * P].rearrange("p (k c) -> p k c", k=KD)
                    T.h = flat[:, 0:KD * N].rearrange("p (k n) -> p k n", k=KD)
                    T.sq = flat[:, KD * N:2 * KD * N].rearrange("p (k n) -> p k n", k=KD)
                    T.wab = flat[:, 2 * KD * N:2 * KD * N + 8 * KD].rearrange("p (k c) -> p k c", k=KD)
                    T.sc = T.wk[:, 0, :]
                    T.masked = flat[:, 18 * NP_:18 * NP_ + 8 * P]
                    T.vx = sb(sub, "vx", [P, DEC_B, P])
                    T.dc = sb(sub, "dc", [P, DC_W])[:]
                    norm_stage(nc, T, l, True)
                    first_head_stage(nc, T, l)
                    with nc.Fori(0, H - 1) as h:
                        head(nc, T, l, h, True)
                    head(nc, T, l, H - 1, False)
                with ExitStack() as sub:
                    T.wm = sb(sub, "wm", [P, 2, 12, P])
                    T.mt = sb(sub, "mt", [P, KD, N])
                    sg = sb(sub, "sg", [P, 3, N])
                    T.sg = [two(sg[:, i, :]) for i in range(2)]
                    T.ma = two(sg[:, 2, :])
                    merge_stage(nc, T, l)
                    T.h = sb(sub, "h2", [P, KD, N])
                    out_stage(nc, T, l)
                    T.sq = T.mt
                    norm_stage(nc, T, l, False)
            with ExitStack() as ctx:
                T.g = [sb(ctx, "g0", [P, PART, N])]
                T.idx = sb(ctx, "idx", [P, 4, NP_], F16)
                T.iota = sb(ctx, "iota", [P, P])
                T.iota_b = sb(ctx, "iota_b", [P, P], F16)[:]
                T.iota_h = sb(ctx, "iota_h", [P, PART], F16)[:]
                T.zero = sb(ctx, "zero", [P, HALF], F16)[:]
                iota_stage(nc, T)
                with ExitStack() as sub:
                    T.scr = sb(sub, "scr", [P, TILES, 2 * PH_HEADS, NKEY])
                    with ExitStack() as early:
                        T.keys = sb(early, "keys", [P, 2 * PH_HEADS, P])[:]
                        T.wm2 = sb(early, "wm2", [P, 2, KD, P])
                        qt = sb(early, "qt", [P, 2, NP_])
                        T.qt = [qt[:, i, :] for i in range(2)]
                        key_scores_stage(nc, T, l)
                    T.x1 = sb(sub, "x1", [P, 2 * PH_HEADS, NKEY])[:]
                    T.t1 = sb(sub, "t1", [P, 2 * PH_HEADS, TOPK])[:]
                    T.i1u = sb(sub, "i1u", [P, 2 * PH_HEADS, TOPK], U32)[:]
                    T.i1f = sb(sub, "i1f", [P, 2 * PH_HEADS, TOPK])[:]
                    T.cand = sb(sub, "cand", [P, PH_HEADS, TOPK * TOPK])[:]
                    T.posu = sb(sub, "posu", [P, PH_HEADS, TOPK], U32)[:]
                    T.pau = sb(sub, "pau", [P, PH_HEADS, TOPK], U32)[:]
                    T.pbu = sb(sub, "pbu", [P, PH_HEADS, TOPK], U32)[:]
                    T.paf = sb(sub, "paf", [P, PH_HEADS, TOPK])[:]
                    T.pbf = sb(sub, "pbf", [P, PH_HEADS, TOPK])[:]
                    T.tv = sb(sub, "tv", [P, PH_HEADS, TOPK])[:]
                    T.t2 = sb(sub, "t2", [P, TILES, PH_HEADS, TOPK])
                    T.found = sb(sub, "found", [P, 3, TILES, P])
                    T.spare = sb(sub, "spare", [P, 1])[:]
                    T.gs = sb(sub, "gs", [P, TILES * PH_HEADS])[:]
                    T.ur = sb(sub, "ur0", [P, 2, KD, P])
                    retrieval_stage(nc, T, l)
                T.g.append(sb(ctx, "g1", [P, PART, N]))
                for part in range(PARTS):
                    with ExitStack() as sub:
                        T.ur = sb(sub, f"ur{part + 1}", [P, 2, KD, P])
                        T.oh1 = sb(sub, f"oh1_{part}", [P, 2, GT, P], F16)
                        T.oh2 = sb(sub, f"oh2_{part}", [P, 2, GT, 2, PART], F16)
                        T.eq2 = sb(sub, f"eq2_{part}", [P, 2, GT, PART], F16)
                        coefficient_stage(nc, T, l, part)
                    with ExitStack() as sub:
                        T.vr = sb(sub, f"vr{part}", [P, 2, 2, 4 * P])
                        T.vh = sb(sub, f"vh{part}", [P, 2, 4 * P], F32R)
                        T.vl = sb(sub, f"vl{part}", [P, 2, 4 * P], F32R)
                        T.gh = sb(sub, f"gh{part}", [P, 2, N], F32R)
                        T.gl = sb(sub, f"gl{part}", [P, 2, N], F32R)
                        T.ht = sb(sub, f"ht{part}", [P, 4, N])
                        expert_out_stage(nc, T, l, part)
        with stage(nc, "y_out") as (block, s):
            @block.sync
            def _(sp):
                sp.dma_start(d["y"], d["xs"]).then_inc(s["y_out"], 16)
                sp.wait_ge(s["y_out"], 16)


def iota_stage(nc, T):
    with stage(nc, "counted", "zeroed", "cast") as (block, s):
        @block.gpsimd
        def _(pool):
            nc.gpsimd.iota(T.iota[:], pattern=[[1, P]], base=0, channel_multiplier=0,
                           allow_small_or_imprecise_dtypes=True).then_inc(s["counted"], 1)

        @block.vector
        def _(dve):
            nc.vector.memset(T.zero, 0.0).then_inc(s["zeroed"], 1)
            dve.wait_ge(s["zeroed"], 1)
            dve.wait_ge(s["counted"], 1)
            nc.vector.tensor_copy(T.iota_b, T.iota[:]).then_inc(s["cast"], 1)
            dve.wait_ge(s["cast"], 1)


def br_slot(b, h):
    return bass.ds(4 * b + h, 1)


def constants():
    f = np.float32
    p = np.arange(P)
    key, qry = p[:, None], p[None, :]
    gc = np.zeros((P, GC_W), f)
    gc[:, C_MSK:C_MSK + P] = np.eye(P)
    for r in range(LEVELS):
        m = 1 << r
        pair = (key // (2 * m) == qry // (2 * m)) & (key // m % 2 == 0) & (qry // m % 2 == 1)
        gc[:, C_MSK + (1 + r) * P:C_MSK + (2 + r) * P] = pair
    gc[:, C_ONES:C_ONES + P] = 1
    causal = key <= qry
    same = key // DEC_T == qry // DEC_T
    for t in range(TILES):
        gc[:, C_UT + t * P:C_UT + (t + 1) * P] = causal if t < 4 else causal & same
    gc[:, C_BLK:C_BLK + P] = same
    gc[:, C_BS:C_BS + DEC_B] = key // DEC_T == np.arange(DEC_B)[None, :]
    gc[:, C_COMP:C_COMP + P] = key // DK == qry // DK
    gc[:, C_SELA] = p < DK
    gc[:, C_SELB] = p >= DK
    dc = np.zeros((P, DC_W), f)
    x = np.arange(SEQ)[None, :]
    dist = p[:, None] + (SEQ - P) - x
    dc[:, C_DP:C_DP + SEQ] = np.where(dist >= 0, dist, FAR)
    tok = p % NS
    pos = tok % DEC_T
    dc[:, C_DS:C_DS + PAST] = PAST + pos[:, None] - np.arange(PAST)[None, :]
    new = np.arange(NS)[None, :]
    gap = pos[:, None] - new % DEC_T
    ok = (tok[:, None] // DEC_T == new // DEC_T) & (gap >= 0)
    dc[:, C_DS + PAST:C_DS + PAST + NS] = np.where(ok, gap, FAR)
    dc[:, C_STK:C_STK + NS] = tok[:, None] == new
    qm = np.zeros((P, DEC_B + 1, 2, NS))
    for c in range(2):
        qm[c * DK:(c + 1) * DK, DEC_B, c, :] = 1
        for b in range(DEC_B):
            qm[c * DK:(c + 1) * DK, b, c, b * DEC_T:(b + 1) * DEC_T] = 1
    dc[:, C_QM:] = qm.reshape(P, -1)
    hc = np.zeros((H, P, HC_W), np.float64)
    for h in range(H):
        lg = np.log1p(-np.exp2(-5.0 - h))
        gap = qry - key
        decay = np.where(gap >= 0, np.exp(np.maximum(gap, 0) * lg), 0.0) * K_SCALE
        for t in range(TILES):
            c = slice(t * P, (t + 1) * P)
            hc[h, :, H_RM:][:, c] = decay if t < 4 else decay * same
            at = p if t < 4 else p % DEC_T
            hc[h, :, H_QD:][:, c] = np.exp((at + 1) * lg)[None, :]
            hc[h, :, H_KD + t] = np.exp(((P if t < 4 else DEC_T) - 1 - at) * lg) * K_SCALE
            hc[h, :, H_GT + t] = np.exp(P * lg)
        hc[h, :, H_G8:H_G8 + DEC_B] = np.exp(DEC_T * lg)
        hc[h, :, H_SL] = -(2.0 ** (-8.0 * (h + 1) / H)) / S_SCALE
    layer = np.zeros((DEPTH, 3), f)
    for l in range(DEPTH):
        li = 0.8 - 0.6 * np.exp(-0.3 * l)
        layer[l] = (float(l > 0), li, 1.0 - li)
    return gc, dc, hc.astype(f), layer


def lay_out(i):
    c = np.ascontiguousarray
    i = {k: np.asarray(v) for k, v in i.items()}
    gc, dc, hc, layer = constants()
    a = {"gc": gc, "dc": dc, "hc": hc}
    x = np.concatenate([i["x_prompt"].reshape(SEQ, D), i["x_sample"].reshape(NS, D)])
    a["x"] = c(x.T.reshape(KD, P, N))
    w = i["w_in"]
    kt = lambda m: m.reshape(m.shape[0], KD, P, -1).transpose(0, 2, 1, 3)
    at = lambda o, h: slice(o + h * P, o + (h + 1) * P)
    rq, rk, rv, rg, hq, hf, hi, hg, gq, gk, gv, gg = (j * 512 for j in range(12))
    ga = 12 * 512
    dq = ga + 2 * H
    dk, dv = dq + 512, dq + 1024
    gate = dq + 1536
    cols = (rq, rk, rg, hq, hf, hg, gq, gk, gv, gg, dq, dk, dv)
    a["w_cm"] = c(np.stack([np.stack([kt(w[:, :, at(o, h)]) for o in cols], 1) for h in range(H)], 1))
    a["w_tm"] = c(np.stack([kt(np.concatenate([w[:, :, at(o, h)] for o in (rv, hi)], 2)) for h in range(H)], 1))
    a["w_ab"] = c(kt(w[:, :, ga:ga + 2 * H]))
    wg = w[:, :, gate:].reshape(DEPTH, KD, P, 4, KD, P).transpose(0, 4, 3, 2, 1, 5)
    wb = i["w_branch"].reshape(DEPTH, 4, 4, P, KD, P).transpose(0, 4, 1, 3, 2, 5)
    a["w_merge"] = c(np.concatenate([wg, wb], 4))
    a["w_out"] = c(i["w_out"].reshape(DEPTH, KD, P, KD, P).transpose(0, 3, 2, 1, 4))
    a["w_query"] = c(i["peer_wq"].reshape(DEPTH, KD, P, 2 * PH_HEADS, P).transpose(0, 3, 2, 1, 4))
    a["keys"] = c(i["peer_keys"].reshape(DEPTH, 2 * PH_HEADS, NKEY, P).transpose(0, 3, 1, 2))
    u = i["peer_u"].reshape(DEPTH, NKEY, PARTS, PART, KD, P)
    a["u"] = c(u.transpose(0, 2, 3, 5, 4, 1))
    v = i["peer_v"].reshape(DEPTH, NKEY, PARTS, PART // 2, 2, 2, D // 2)
    a["v"] = c(v.transpose(0, 2, 5, 3, 1, 4, 6))
    rep = lambda m: np.repeat(m[:, None, :], P, 1)
    fk = lambda m: m.reshape(DEPTH, KD, P).transpose(0, 2, 1)
    a["pl"] = c(np.concatenate([fk(i["norm_mix"]), fk(i["norm_ffn"]), rep(i["gdn_a_log"]), rep(i["gdn_dt_bias"]),
                                rep(i["diff_lambda"].reshape(DEPTH, -1)), rep(layer)], 2))
    ph = np.zeros((DEPTH, H, P, PH_W), np.float32)
    for n, name in enumerate(("ret_norm", "hgrn_norm", "gdn_norm", "diff_norm")):
        ph[..., n] = i[name].reshape(DEPTH, H, P)
    taps = i["gdn_conv"].reshape(DEPTH, 4, 3, H, P).transpose(0, 3, 4, 2, 1)
    ph[..., Q_CONV:Q_CONV + 12] = taps.reshape(DEPTH, H, P, 12)
    ph[..., Q_LB:Q_LB + 2] = i["hgrn_lb_logits"].reshape(DEPTH, H, P).transpose(1, 2, 0)[None]
    ph[..., Q_QN] = np.tile(i["diff_q_norm"], (1, 2))[:, None, :]
    ph[..., Q_KN] = np.tile(i["diff_k_norm"], (1, 2))[:, None, :]
    a["ph"] = ph
    a["conv_in"] = c(i["state_gdn_conv"].reshape(DEPTH, DEC_B, 3, 3, H, P).transpose(0, 4, 3, 5, 1, 2))
    for n in ("state_ret", "state_hgrn", "state_gdn"):
        a[n] = c(i[n])
    a["cache_k"] = c(i["cache_k"].reshape(DEPTH, N_PHYS, PAGE, H, P).transpose(0, 1, 3, 4, 2))
    a["cache_v"] = c(i["cache_v"].transpose(0, 1, 3, 2, 4))
    a["page_table"] = c(i["page_table"].reshape(1, -1).astype(np.int32))
    return a


_OUTS = {
    "y": (KD, P, N),
    "ret_prompt": (DEPTH, H, P, P), "ret_sample": (DEPTH, DEC_B, H, P, P),
    "hgrn_prompt": (DEPTH, H, P, P), "hgrn_sample": (DEPTH, DEC_B, H, P, P),
    "gdn_prompt": (DEPTH, H, P, P), "gdn_sample": (DEPTH, DEC_B, H, P, P),
    "conv_prompt": (DEPTH, H, 3, P, 3), "conv_sample": (DEPTH, H, 3, P, DEC_B, 3),
    "k_out": (DEPTH, H, P, N), "v_prompt": (DEPTH, H, SEQ, P), "v_sample": (DEPTH, H, NS, P),
}


def kernel(**inputs):
    import concourse.bacc as _bacc
    from concourse.bass_utils import run_bass_kernel_spmd as _run

    nc = _bacc.Bacc("TRN2", target_bir_lowering=False, num_devices=1)
    arrays = lay_out(inputs)
    d = {}
    for name, a in arrays.items():
        d[name] = nc.dram_tensor(f"in_{name}", a.shape, mybir.dt.from_np(a.dtype), kind="ExternalInput").ap()
    for name, shape in _OUTS.items():
        d[name] = nc.dram_tensor(f"out_{name}", shape, F32, kind="ExternalOutput").ap()
    d["xs"] = nc.dram_tensor("residual", (KD, P, N), F32, kind="Internal").ap()
    program(nc, d)
    r = _run(nc, [{f"in_{n}": a for n, a in arrays.items()}], core_ids=[0])
    o = {n: r.results[0][f"out_{n}"] for n in _OUTS}
    y = o["y"].reshape(D, N).T
    conv_p = o["conv_prompt"].transpose(0, 4, 2, 1, 3).reshape(DEPTH, 1, 3, 3 * 512)
    conv_s = o["conv_sample"].transpose(0, 4, 5, 2, 1, 3).reshape(DEPTH, DEC_B, 3, 3 * 512)
    k = o["k_out"].transpose(0, 3, 1, 2)
    return (y[:SEQ].reshape(1, SEQ, D), y[SEQ:].reshape(DEC_B, DEC_T, D),
            o["ret_prompt"][:, None], o["ret_sample"], o["hgrn_prompt"][:, None], o["hgrn_sample"],
            o["gdn_prompt"][:, None], o["gdn_sample"], conv_p, conv_s,
            k[:, :SEQ].reshape(DEPTH, 1, SEQ, H, 2, DK),
            o["v_prompt"].transpose(0, 2, 1, 3)[:, None],
            k[:, SEQ:].reshape(DEPTH, DEC_B, DEC_T, H, 2, DK),
            o["v_sample"].transpose(0, 2, 1, 3).reshape(DEPTH, DEC_B, DEC_T, H, P))
```

```python
from contextlib import ExitStack, contextmanager

import numpy as np
import concourse.bass as bass
from concourse import mybir

F32 = mybir.dt.float32
F32R = mybir.dt.float32r
F16 = mybir.dt.float16
U32 = mybir.dt.uint32
I32 = mybir.dt.int32
ALU = mybir.AluOpType
ACT = mybir.ActivationFunctionType
AX_X = mybir.AxisListType.X

P = 128
D = 1024
KD = D // P
DEPTH = 2
SEQ = 512
DEC_B, DEC_T = 8, 8
NS = DEC_B * DEC_T
N = SEQ + NS
TILES = 5
NP_ = TILES * P
HALF = N // 2
H = 4
LEVELS = 7
W_HEAD = 12
PAGES = 2
PAGE = 128
PAST = PAGES * PAGE
N_PHYS = DEC_B * PAGES + DEC_B * PAGES // 4
DK = 64
EPS = 1e-6
K_SCALE = float(P) ** -0.5
S_SCALE = float(DK) ** -0.5
PH_HEADS = 8
TOPK = 16
NKEY = 128
FAR = 1e30
BANK = 512
PARTS = 4
PART = NKEY // PARTS
GT = N // PART
GT_W = 8
G_SCALE = 4096.0

C_MSK = 0
C_ONES = C_MSK + (1 + LEVELS) * P
C_UT = C_ONES + P
C_BLK = C_UT + TILES * P
C_BS = C_BLK + P
C_COMP = C_BS + DEC_B
C_SELA = C_COMP + P
C_SELB = C_SELA + 1
GC_W = C_SELB + 1
C_DP = 0
C_DS = C_DP + SEQ
C_STK = C_DS + PAST + NS
C_QM = C_STK + NS
DC_W = C_QM + (DEC_B + 1) * P
H_RM = 0
H_QD = H_RM + NP_
H_KD = H_QD + NP_
H_GT = H_KD + TILES
H_G8 = H_GT + TILES
HC_W = H_G8 + DEC_B
Q_RN, Q_HN, Q_GN, Q_DN = 0, 1, 2, 3
Q_CONV = 4
Q_LB = Q_CONV + 12
Q_QN, Q_KN = Q_LB + 2, Q_LB + 3
Q_SL = Q_KN + 1
PH_W = Q_SL + 1
L_NM, L_NF = 0, KD
L_AL = 2 * KD
L_DT = L_AL + H
L_LAM = L_DT + H
L_LB = L_LAM + 4 * DK
L_LI, L_OL = L_LB + 1, L_LB + 2
PL_W = L_OL + 1


class Memory:
    pass


@contextmanager
def stage(nc, *names, shared=()):
    with ExitStack() as ctx:
        sems = {n: ctx.enter_context(nc.semaphore(n)) for n in names}
        sems.update(shared)
        with nc.Block(no_gpsimd_drain=True) as block:
            yield block, sems
        for n in names:
            nc.sync.sem_clear(sems[n])
        nc.all_engine_barrier(sem_only=True)


def chained(engine, sem):
    count = [0]

    def link(instruction):
        count[0] += 1
        instruction.then_inc(sem, 1)
        engine.wait_ge(sem, count[0])

    return link


def bank(T, b, width=BANK):
    return T.ps[:, b * BANK:b * BANK + width]


def halves(T, b):
    return T.ps[:, b * BANK:(b + 2) * BANK].rearrange("p (a c) -> p a c", a=2)[:, :, 0:HALF]


def two(ap):
    return ap[:, 0:N].rearrange("p (a c) -> p a c", a=2)


def tile(ap, t):
    return ap[:, t * P:(t + 1) * P]


def wide_product(nc, T, b, weights, rhs, kn):
    for a in range(2):
        for k in range(kn):
            last = nc.tensor.matmul(bank(T, b + a)[:, 0:HALF], weights(k), rhs(k)[:, a * HALF:(a + 1) * HALF],
                                    start=(k == 0), stop=(k == kn - 1))
    return last


HGRN_SLOTS = ((2, 0), (3, 0), (0, 1))
GDN_SLOTS = ((1, 0), (0, 1), (2, 1), (3, 1))
ATT_SLOTS = ((1, 0), (0, 1), (2, 1), (3, 1), (2, 2), (3, 2))
FIRST_SLOTS = ((0, 1), (1, 1), (2, 1))


def pe_ahead(nc, pe, T, s, slots, u, b, banks=1):
    c, a = divmod(u, 2)
    slot, loads = slots[c]
    if a == 0 and loads:
        pe.wait_ge(s["w"][slot], 16 * loads)
    if u >= banks:
        pe.wait_ge(s["taken"], u - banks + 1)
    for k in range(KD):
        last = nc.tensor.matmul(bank(T, b)[:, 0:HALF], T.wr[:, slot, k, :], T.xn[:, k, a * HALF:(a + 1) * HALF],
                                start=(k == 0), stop=(k == KD - 1))
    last.then_inc(s["ahead"], 1)


def load_tile(sp, T, s, l, h, column, slot, after=0):
    if after:
        sp.wait_ge(s["ahead"], after)
    sp.dma_start(T.wr[:, slot], T.d["w_cm"][l, h, column]).then_inc(s["w"][slot], 16)


def act_take(nc, act, T, s, u, b, dst, func=ACT.Copy, scale=1.0, dst_minus=None):
    cols = slice(u % 2 * HALF, (u % 2 + 1) * HALF)
    act.wait_ge(s["ahead"], u + 1)
    if dst_minus is not None:
        nc.scalar.activation(dst_minus[:, cols], bank(T, b)[:, 0:HALF], func, scale=-scale)
    nc.scalar.activation(dst[:, cols], bank(T, b)[:, 0:HALF], func, scale=scale).then_inc(s["taken"], 1)


def pe_value_tile(nc, T, t, b):
    for k in range(KD):
        last = nc.tensor.matmul(bank(T, b)[:, 0:2 * P], tile(T.xn[:, k, :], t), T.wtm[:, k, :],
                                start=(k == 0), stop=(k == KD - 1))
    return last


RET_W, HGRN_W, GDN_W, ATT_W = 0, 3, 6, 10
AHEAD = ("ahead", "taken")
W_SEMS = ("w0", "w1", "w2", "w3")


def norm_stage(nc, T, l, first):
    names = ("x_in", "small_in", "const_in", "squared", "summed", "scaled", "rooted", "chain_v", "chain_a",
             "zeroed", "normed", "ab_done", "a_ready", "lam_ready", "exp_done", "sp_abs", "sp_exp", "sp_in",
             "sp_ln", "b_done", "al_done", "dc_in")
    with stage(nc, *names) as (block, s):
        @block.sync
        def _(sp):
            if first:
                sp.dma_start(T.h[:], T.d["xs"].rearrange("m p n -> p m n")).then_inc(s["x_in"], 16)
                sp.dma_start(T.pl[:], T.d["pl"][l]).then_inc(s["small_in"], 16)
                sp.dma_start(T.wab, T.d["w_ab"][l]).then_inc(s["small_in"], 16)
                sp.dma_start(T.general[:], T.d["gc"]).then_inc(s["const_in"], 16)
                sp.dma_start(T.dc, T.d["dc"]).then_inc(s["dc_in"], 16)
                sp.wait_ge(s["dc_in"], 16)

        @block.scalar
        def _(act):
            if first:
                act.wait_ge(s["x_in"], 16)
            for k in range(KD):
                nc.scalar.activation(T.sq[:, k, :], T.h[:, k, :], ACT.Square).then_inc(s["squared"], 1)
            act.wait_ge(s["summed"], 1)
            nc.scalar.activation(T.rs, halves(T, 0), ACT.Ln, bias=T.eps, scale=1.0 / D).then_inc(s["scaled"], 1)
            act.wait_ge(s["scaled"], 1)
            nc.scalar.activation(T.rs, T.rs, ACT.Exp, scale=-0.5).then_inc(s["rooted"], 1)
            if first:
                act.wait_ge(s["lam_ready"], 1)
                nc.scalar.activation(T.lam[:, 0:2], T.lam[:, 0:2], ACT.Exp).then_inc(s["exp_done"], 1)
                nc.scalar.activation(T.nea, T.pl[:, L_AL:L_AL + H], ACT.Exp).then_inc(s["al_done"], 1)
                act.wait_ge(s["a_ready"], 1)
                nc.scalar.activation(T.ga2, T.ga, ACT.Abs).then_inc(s["chain_a"], 1)
                act.wait_ge(s["chain_a"], 1)
                nc.scalar.activation(T.ga2, T.ga2, ACT.Exp, scale=-1.0).then_inc(s["sp_exp"], 1)
                act.wait_ge(s["sp_in"], 1)
                nc.scalar.activation(T.ga2, T.ga2, ACT.Ln).then_inc(s["sp_ln"], 1)
                act.wait_ge(s["ab_done"], 1)
                nc.scalar.activation(T.beta, bank(T, 2, TILES * 2 * H).rearrange("p (t c) -> p t c", c=2 * H)[:, :, H:],
                                     ACT.Sigmoid).then_inc(s["b_done"], 1)
                act.wait_ge(s["b_done"], 1)

        @block.tensor
        def _(pe):
            if first:
                pe.wait_ge(s["const_in"], 16)
            pe.wait_ge(s["squared"], KD)
            wide_product(nc, T, 0, lambda k: T.ones, lambda k: T.sq[:, k, :], KD).then_inc(s["summed"], 1)
            if first:
                pe.wait_ge(s["small_in"], 32)
                pe.wait_ge(s["zeroed"], 1)
                pe.wait_ge(s["normed"], KD)
                for t in range(TILES):
                    for k in range(KD):
                        last = nc.tensor.matmul(T.ps[:, 2 * BANK + t * 2 * H:2 * BANK + (t + 1) * 2 * H],
                                                tile(T.xn[:, k, :], t), T.wab[:, k, :],
                                                start=(k == 0), stop=(k == KD - 1))
                last.then_inc(s["ab_done"], 1)

        @block.vector
        def _(dve):
            link = chained(dve, s["chain_v"])
            if first:
                nc.vector.memset(T.xn[:, :, N:NP_], 0.0).then_inc(s["zeroed"], 1)
                link(nc.vector.memset(T.pr[:], 0.0))
            dve.wait_ge(s["rooted"], 1)
            g0 = L_NM if first else L_NF
            if first:
                dve.wait_ge(s["small_in"], 32)
            for k in range(KD):
                nc.vector.scalar_tensor_tensor(out=two(T.xn[:, k, :]), in0=two(T.h[:, k, :]),
                                               scalar=T.pl[:, g0 + k:g0 + k + 1], in1=T.rs,
                                               op0=ALU.mult, op1=ALU.mult).then_inc(s["normed"], 1)
            if first:
                lp = T.pl[:, L_LAM:L_LAM + 4 * DK].rearrange("p (a b d) -> p a b d", a=2, b=2)
                link(nc.vector.tensor_tensor(T.lprod, lp[:, :, 0, :], lp[:, :, 1, :], ALU.mult))
                nc.vector.tensor_reduce(T.lam[:, 0:2], T.lprod, AX_X, ALU.add).then_inc(s["lam_ready"], 1)
                dve.wait_ge(s["exp_done"], 1)
                link(nc.vector.tensor_tensor(T.lam[:, 2:3], T.lam[:, 1:2], T.lam[:, 0:1], ALU.subtract))
                link(nc.vector.tensor_tensor(T.lam[:, 2:3], T.lam[:, 2:3], T.pl[:, L_LI:L_LI + 1], ALU.subtract))
                link(nc.vector.scalar_tensor_tensor(out=T.lam[:, 3:4], in0=T.general[:, C_SELB:C_SELB + 1],
                                                    scalar=T.lam[:, 2:3], in1=T.general[:, C_SELA:C_SELA + 1],
                                                    op0=ALU.mult, op1=ALU.add))
                dve.wait_ge(s["ab_done"], 1)
                ab = bank(T, 2, TILES * 2 * H).rearrange("p (t c) -> p t c", c=2 * H)
                nc.vector.tensor_tensor(T.ga, ab[:, :, 0:H],
                                        T.pl[:, L_DT:L_DT + H].unsqueeze(1).to_broadcast([P, TILES, H]),
                                        ALU.add).then_inc(s["a_ready"], 1)
                dve.wait_ge(s["sp_exp"], 1)
                nc.vector.tensor_scalar(T.ga2, T.ga2, 1.0, None, ALU.add).then_inc(s["sp_in"], 1)
                dve.wait_ge(s["sp_ln"], 1)
                link(nc.vector.scalar_tensor_tensor(out=T.ga, in0=T.ga, scalar=0.0, in1=T.ga2,
                                                    op0=ALU.max, op1=ALU.add))
                dve.wait_ge(s["al_done"], 1)
                link(nc.vector.scalar_tensor_tensor(out=T.logg, in0=T.ga, scalar=-1.0,
                                                    in1=T.nea.unsqueeze(1).to_broadcast([P, TILES, H]),
                                                    op0=ALU.mult, op1=ALU.mult))


def first_head_stage(nc, T, l):
    with stage(nc, *W_SEMS, *AHEAD, "hc_in", "values_in", "valued", "copied") as (block, s):
        s["w"] = [s["w0"], s["w1"], s["w2"], s["w3"]]

        @block.sync
        def _(sp):
            for c in range(3):
                load_tile(sp, T, s, l, 0, RET_W + c, c)
            load_tile(sp, T, s, l, 0, HGRN_W + 1, 3)
            sp.dma_start(T.hc[:], T.d["hc"][0]).then_inc(s["hc_in"], 16)
            sp.wait_ge(s["ahead"], 4)
            sp.dma_start(T.wtm, T.d["w_tm"][l, 0]).then_inc(s["values_in"], 16)
            load_tile(sp, T, s, l, 0, HGRN_W, 2, after=6)
            sp.wait_ge(s["hc_in"], 16)
            sp.wait_ge(s["w3"], 16)
            sp.wait_ge(s["w2"], 32)

        @block.tensor
        def _(pe):
            for u in range(6):
                pe_ahead(nc, pe, T, s, FIRST_SLOTS, u, u % 2, banks=2)
            pe.wait_ge(s["values_in"], 16)
            for t in range(TILES):
                pe_value_tile(nc, T, t, 2 + t).then_inc(s["valued"], 1)

        @block.scalar
        def _(act):
            for u in range(6):
                act_take(nc, act, T, s, u, u % 2, T.ret[u // 2], ACT.Silu if u >= 4 else ACT.Copy)
            for t in range(TILES):
                act.wait_ge(s["valued"], t + 1)
                nc.scalar.copy(T.vt[:, t, 0:2 * P], bank(T, 2 + t)[:, 0:2 * P]).then_inc(s["copied"], 1)


def pe_state_products(nc, pe, T, s, values):
    pe.wait_ge(s["keys_ready"], 1)
    for t in range(4):
        last = nc.tensor.matmul(T.ps[:, t * P:(t + 1) * P], T.kt[:, t, :], values(t), start=True, stop=True)
    last.then_inc(s["u_prompt"], 1)
    pe_sample_state(nc, pe, T, s)


def pe_sample_state(nc, pe, T, s):
    pe.wait_ge(s["vx_ready"], 1)
    for a in range(2):
        last = nc.tensor.matmul(bank(T, 2 + a), T.kt[0:NS, 4, :],
                                T.vx[0:NS, 4 * a:4 * a + 4, :], start=True, stop=True)
    last.then_inc(s["u_sample"], 1)


def pe_outputs(nc, pe, T, s, values, q_prompt, q_sample):
    for t in range(4):
        o = T.ps[:, 4 * BANK + t * P:4 * BANK + (t + 1) * P]
        nc.tensor.matmul(o, values(t), tile(T.sc, t), start=True, stop=(t == 0))
        if t:
            nc.tensor.matmul(o, T.st[:, t, :], tile(q_prompt, t), start=False, stop=True)
    nc.tensor.matmul(bank(T, 5, P), values(4), tile(T.sc, 4), start=True, stop=False)
    for b in range(DEC_B):
        last = nc.tensor.matmul(bank(T, 5)[:, b * DEC_T:(b + 1) * DEC_T], T.s_in[:, b, :],
                                q_sample[:, SEQ + b * DEC_T:SEQ + (b + 1) * DEC_T],
                                start=False, stop=(b == DEC_B - 1))
    last.then_inc(s["o_ready"], 1)


def dve_spread_values(nc, T, s, values):
    nc.vector.tensor_tensor(T.vx[0:NS], values.unsqueeze(1).to_broadcast([NS, DEC_B, P]),
                            T.general[0:NS, C_BS:C_BS + DEC_B].unsqueeze(2).to_broadcast([NS, DEC_B, P]),
                            ALU.mult).then_inc(s["vx_ready"], 1)


def dve_prompt_states(nc, dve, T, s, link, decay):
    dve.wait_ge(s["u_prompt"], 1)
    link(nc.vector.tensor_copy(T.st[:, 1, :], T.ps[:, 0:P]))
    for t in range(1, 4):
        op = nc.vector.scalar_tensor_tensor(out=T.st[:, t + 1, :], in0=T.st[:, t, :], scalar=decay[:, t:t + 1],
                                            in1=T.ps[:, t * P:(t + 1) * P], op0=ALU.mult, op1=ALU.add)
        if t < 3:
            link(op)
    op.then_inc(s["st_ready"], 1)


def dve_sample_states(nc, dve, T, s, link, decay):
    dve.wait_ge(s["s_loaded"], 16)
    link(nc.vector.tensor_tensor(T.s_new[:], T.s_in[:], decay.unsqueeze(2).to_broadcast([P, DEC_B, P]), ALU.mult))
    dve.wait_ge(s["u_sample"], 1)
    nc.vector.tensor_tensor(T.s_new[:], T.s_new[:],
                            T.ps[:, 2 * BANK:4 * BANK].rearrange("p (s v) -> p s v", s=DEC_B),
                            ALU.add).then_inc(s["s_ready"], 1)


def sp_states(sp, T, s, l, h, prompt, sample):
    sp.wait_ge(s["st_ready"], 1)
    sp.dma_start(prompt[l, h], T.st[:, 4, :]).then_inc(s["states_out"], 16)
    sp.wait_ge(s["s_ready"], 1)
    sp.dma_start(sample[l, :, h].rearrange("s k v -> k s v"), T.s_new[:]).then_inc(s["states_out"], 16)
    sp.wait_ge(s["states_out"], 32)


def act_square(nc, act, T, s):
    act.wait_ge(s["o_ready"], 1)
    nc.scalar.activation(T.wk[:, 1, 0:N], bank(T, 4, N), ACT.Square).then_inc(s["o_squared"], 1)


def act_root(nc, act, T, s):
    act.wait_ge(s["o_summed"], 1)
    nc.scalar.activation(T.rs, halves(T, 6), ACT.Ln, bias=T.eps, scale=1.0 / P).then_inc(s["o_mean"], 1)
    act.wait_ge(s["o_mean"], 1)
    nc.scalar.activation(T.rs, T.rs, ACT.Exp, scale=-0.5).then_inc(s["o_root"], 1)


def pe_finish(nc, pe, T, s):
    pe.wait_ge(s["o_squared"], 1)
    wide_product(nc, T, 6, lambda k: T.ones, lambda k: T.wk[:, 1, :], 1).then_inc(s["o_summed"], 1)


def dve_finish(nc, dve, T, s, link, gain, slot, gate):
    dve.wait_ge(s["o_root"], 1)
    out = T.br[:, slot, :].rearrange("p a n -> p (a n)")
    link(nc.vector.scalar_tensor_tensor(out=two(out), in0=two(bank(T, 4, N)), scalar=gain, in1=T.rs,
                                        op0=ALU.mult, op1=ALU.mult))
    if gate is not None:
        link(nc.vector.tensor_tensor(out, out, gate[:, 0:N], ALU.mult))


FINISH = ("o_ready", "o_squared", "o_summed", "o_mean", "o_root", "chain_v")
STATES = ("keys_ready", "u_prompt", "u_sample", "vx_ready", "st_ready", "s_ready", "s_loaded", "states_out")


def load_sample_state(sp, T, s, l, h, state):
    sp.dma_start(T.s_in[:], state[l, :, h].rearrange("s k v -> k s v")).then_inc(s["s_loaded"], 16)


def retention_stage(nc, T, l, h, slot):
    q, k, g = T.ret
    hq, hf, hg, hneg = T.hgrn
    qd = T.wk[:, 2, :]
    with stage(nc, *W_SEMS, *AHEAD, "small_in", "scored", "turned", "sc_ready", *FINISH, *STATES) as (block, s):
        s["w"] = [s["w0"], s["w1"], s["w2"], s["w3"]]

        @block.sync
        def _(sp):
            load_tile(sp, T, s, l, h, HGRN_W + 2, 0)
            sp.dma_start(T.ph[:], T.d["ph"][l, h]).then_inc(s["small_in"], 16)
            load_tile(sp, T, s, l, h, GDN_W, 1)
            load_sample_state(sp, T, s, l, h, T.d["state_ret"])
            sp_states(sp, T, s, l, h, T.d["ret_prompt"], T.d["ret_sample"])
            sp.wait_ge(s["w1"], 16)

        @block.tensor
        def _(pe):
            for t in range(TILES):
                last = nc.tensor.matmul(tile(bank(T, 4, NP_), t), tile(k, t), tile(q, t), start=True, stop=True)
            last.then_inc(s["scored"], 1)
            for t in range(TILES):
                last = nc.tensor.transpose(tile(bank(T, 6, NP_), t), tile(k, t), T.ident)
            last.then_inc(s["turned"], 1)
            pe_ahead(nc, pe, T, s, HGRN_SLOTS, 0, 1)
            pe_state_products(nc, pe, T, s, lambda t: T.vt[:, t, 0:P])
            pe_ahead(nc, pe, T, s, HGRN_SLOTS, 1, 1)
            pe.wait_ge(s["sc_ready"], 1)
            pe.wait_ge(s["st_ready"], 1)
            pe.wait_ge(s["s_loaded"], 16)
            pe_outputs(nc, pe, T, s, lambda t: T.vt[:, t, 0:P], qd, qd)
            pe_ahead(nc, pe, T, s, HGRN_SLOTS, 2, 1)
            pe_finish(nc, pe, T, s)
            for u in range(3, 6):
                pe_ahead(nc, pe, T, s, HGRN_SLOTS, u, 1 - u % 2, banks=2)

        @block.scalar
        def _(act):
            def take(u):
                b = 1 if u < 3 else 1 - u % 2
                if u < 2:
                    act_take(nc, act, T, s, u, b, hq, scale=K_SCALE)
                elif u < 4:
                    act_take(nc, act, T, s, u, b, hf, ACT.Sigmoid, dst_minus=hneg)
                else:
                    act_take(nc, act, T, s, u, b, hg, ACT.Silu)

            take(0)
            take(1)
            act_square(nc, act, T, s)
            take(2)
            act_root(nc, act, T, s)
            for u in range(3, 6):
                take(u)

        @block.vector
        def _(dve):
            link = chained(dve, s["chain_v"])
            dve_spread_values(nc, T, s, T.vt[0:NS, 4, 0:P])
            dve.wait_ge(s["turned"], 1)
            nc.vector.tensor_tensor(T.kt[:], bank(T, 6, NP_).rearrange("p (t k) -> p t k", t=TILES),
                                    T.hc[:, H_KD:H_KD + TILES].unsqueeze(2).to_broadcast([P, TILES, P]),
                                    ALU.mult).then_inc(s["keys_ready"], 1)
            link(nc.vector.tensor_tensor(qd, q, T.hc[:, H_QD:H_QD + NP_], ALU.mult))
            nc.vector.tensor_tensor(T.sc, bank(T, 4, NP_), T.hc[:, H_RM:H_RM + NP_], ALU.mult).then_inc(s["sc_ready"], 1)
            dve_prompt_states(nc, dve, T, s, link, T.hc[:, H_GT:H_GT + TILES])
            dve_sample_states(nc, dve, T, s, link, T.hc[:, H_G8:H_G8 + DEC_B])
            dve.wait_ge(s["small_in"], 16)
            dve_finish(nc, dve, T, s, link, T.ph[:, Q_RN:Q_RN + 1], slot, g)


def history(ap):
    return ap[:, SEQ + 3:SEQ + 3 + DEC_B * (DEC_T + 3)].rearrange("p (s t) -> p s t", s=DEC_B)


def act_take_gdn(nc, act, T, s, u, b):
    c, a = divmod(u, 2)
    if c == 3:
        act_take(nc, act, T, s, u, b, T.gdn_gate, ACT.Silu)
        return
    xp = T.conv[c]
    act.wait_ge(s["ahead"], u + 1)
    if a == 0:
        nc.scalar.copy(xp[:, 3:3 + HALF], bank(T, b)[:, 0:HALF]).then_inc(s["taken"], 1)
    else:
        nc.scalar.copy(xp[:, 3 + HALF:3 + SEQ], bank(T, b)[:, 0:SEQ - HALF])
        nc.scalar.copy(history(xp)[:, :, 3:3 + DEC_T],
                       bank(T, b)[:, SEQ - HALF:HALF].rearrange("p (s t) -> p s t", s=DEC_B)).then_inc(s["taken"], 1)


def hgrn_stage(nc, T, l, h, slot):
    q, f, g, sneg = T.hgrn
    qf = [T.wk[:, 2 + r, :] for r in range(LEVELS + 1)]
    ke = [T.wk[:, 10 + r, :] for r in range(LEVELS + 1)]
    fd = T.wk[:, 1, :]
    masked = T.masked
    vt = lambda t: T.vt[:, t, P:2 * P]
    with stage(nc, *W_SEMS, *AHEAD, "lb_in", "lb_exp", "level_v", "level_a", "scored", "masked_",
               "summed_", "turned", "sc_ready", *FINISH, *STATES) as (block, s):
        s["w"] = [s["w0"], s["w1"], s["w2"], s["w3"]]

        def blocks(ap, r):
            return ap.rearrange("p (n two b) -> p n two b", two=2, b=1 << r)

        @block.sync
        def _(sp):
            load_tile(sp, T, s, l, h, GDN_W + 1, 0)
            load_tile(sp, T, s, l, h, GDN_W + 2, 2)
            load_tile(sp, T, s, l, h, GDN_W + 3, 3)
            load_sample_state(sp, T, s, l, h, T.d["state_hgrn"])
            load_tile(sp, T, s, l, h, ATT_W, 1, after=2)
            sp_states(sp, T, s, l, h, T.d["hgrn_prompt"], T.d["hgrn_sample"])
            sp.wait_ge(s["w1"], 16)

        @block.tensor
        def _(pe):
            for u in range(4):
                pe_ahead(nc, pe, T, s, GDN_SLOTS, u, 4 + u % 2, banks=2)
            pe.wait_ge(s["level_v"], LEVELS + 1)
            pe.wait_ge(s["level_a"], LEVELS)
            for t in range(TILES):
                n = 1 + (LEVELS if t < 4 else 3)
                b = 2 * (t % 2)
                if t >= 2:
                    pe.wait_ge(s["masked_"], t - 1)
                for i in range(n):
                    lhs, rhs = (ke[0], q) if i == 0 else (ke[i - 1], qf[i - 1])
                    last = nc.tensor.matmul(T.ps[:, b * BANK + i * P:b * BANK + (i + 1) * P],
                                            tile(lhs, t), tile(rhs, t), start=True, stop=True)
                last.then_inc(s["scored"], 1)
            for t in range(TILES):
                last = nc.tensor.transpose(tile(bank(T, 6, NP_), t), tile(ke[LEVELS if t < 4 else 3], t), T.ident)
            last.then_inc(s["turned"], 1)
            pe_ahead(nc, pe, T, s, GDN_SLOTS, 4, 4, banks=2)
            pe.wait_ge(s["masked_"], TILES)
            pe_state_products(nc, pe, T, s, vt)
            pe_ahead(nc, pe, T, s, GDN_SLOTS, 5, 1)
            pe.wait_ge(s["sc_ready"], TILES)
            pe.wait_ge(s["st_ready"], 1)
            pe.wait_ge(s["s_loaded"], 16)
            pe_outputs(nc, pe, T, s, vt, qf[LEVELS], qf[3])
            pe_ahead(nc, pe, T, s, GDN_SLOTS, 6, 0, banks=2)
            pe_finish(nc, pe, T, s)
            pe_ahead(nc, pe, T, s, GDN_SLOTS, 7, 1, banks=2)

        @block.scalar
        def _(act):
            act.wait_ge(s["lb_in"], 1)
            nc.scalar.activation(T.lb[:, 0:2], T.lb[:, 0:2], ACT.Exp).then_inc(s["lb_exp"], 1)
            take = lambda u: act_take_gdn(nc, act, T, s, u, 4 + u % 2 if u < 5 else u % 2)
            for r in range(LEVELS):
                act.wait_ge(s["level_v"], r + 1)
                if r:
                    act.wait_ge(s["level_a"], r)
                nc.scalar.copy(blocks(qf[r + 1], r)[:, :, 0, :], blocks(qf[r], r)[:, :, 0, :])
                nc.scalar.copy(blocks(ke[r + 1], r)[:, :, 1, :], blocks(ke[r], r)[:, :, 1, :]).then_inc(s["level_a"], 1)
                if r in (1, 3):
                    take(r // 2)
            for u in range(2, 6):
                take(u)
            act_square(nc, act, T, s)
            take(6)
            act_root(nc, act, T, s)
            take(7)

        @block.vector
        def _(dve):
            link = chained(dve, s["chain_v"])
            dve_spread_values(nc, T, s, T.vt[0:NS, 4, P:2 * P])
            lg, lb = T.ph[:, Q_LB:Q_LB + 2], T.lb
            link(nc.vector.tensor_reduce(lb[:, 2:3], lg, AX_X, ALU.max))
            nc.vector.tensor_scalar(lb[:, 0:2], lg, lb[:, 2:3], None, ALU.subtract).then_inc(s["lb_in"], 1)
            dve.wait_ge(s["lb_exp"], 1)
            link(nc.vector.tensor_reduce(lb[:, 2:3], lb[:, 0:2], AX_X, ALU.add))
            link(nc.vector.reciprocal(lb[:, 2:3], lb[:, 2:3]))
            link(nc.vector.tensor_scalar(lb[:, 0:2], lb[:, 0:2], lb[:, 2:3], None, ALU.mult))
            link(nc.vector.tensor_tensor(lb[:, 1:2], lb[:, 0:1], lb[:, 1:2], ALU.add))
            link(nc.vector.tensor_tensor(lb[:, 1:2], lb[:, 1:2], lb[:, 0:1], ALU.subtract))
            link(nc.vector.tensor_tensor(lb[:, 1:2], lb[:, 1:2], T.pl[:, L_LB:L_LB + 1], ALU.mult))
            link(nc.vector.tensor_scalar(lb[:, 3:4], lb[:, 1:2], -1.0, 1.0, ALU.mult, ALU.add))
            link(nc.vector.tensor_scalar(fd, f, lb[:, 3:4], lb[:, 1:2], ALU.mult, ALU.add))
            link(nc.vector.tensor_scalar(ke[0], sneg, lb[:, 3:4], None, ALU.mult))
            nc.vector.tensor_tensor(qf[0], q, fd, ALU.mult).then_inc(s["level_v"], 1)
            tot = fd
            at = 0
            for r in range(LEVELS):
                nb = NP_ >> (r + 1)
                pair = tot.rearrange("p (n two) -> p n two", two=2)
                if r:
                    dve.wait_ge(s["level_a"], r)
                else:
                    dve.wait_ge(s["level_v"], 1)
                wide = lambda c: pair[:, :, c].unsqueeze(2).to_broadcast([P, nb, 1 << r])
                nxt = T.tot[:, at:at + nb]
                link(nc.vector.tensor_tensor(nxt, pair[:, :, 0], pair[:, :, 1], ALU.mult))
                link(nc.vector.tensor_tensor(blocks(qf[r + 1], r)[:, :, 1, :], blocks(qf[r], r)[:, :, 1, :],
                                             wide(0), ALU.mult))
                link(nc.vector.tensor_tensor(blocks(ke[r + 1], r)[:, :, 0, :], blocks(ke[r], r)[:, :, 0, :],
                                             wide(1), ALU.mult))
                dve.sem_inc(s["level_v"], 1)
                tot = nxt
                if r == 2:
                    tot8 = T.tot[:, at + SEQ // 8:at + SEQ // 8 + DEC_B]
                at += nb
            for t in range(TILES):
                n = 1 + (LEVELS if t < 4 else 3)
                b = 2 * (t % 2)
                dve.wait_ge(s["scored"], t + 1)
                nc.vector.tensor_tensor(masked[:, 0:n * P], T.ps[:, b * BANK:b * BANK + n * P],
                                        T.general[:, C_MSK:C_MSK + n * P], ALU.mult).then_inc(s["masked_"], 1)
                dve.wait_ge(s["masked_"], t + 1)
                link(nc.vector.tensor_reduce(tile(T.sc, t), masked[:, 0:n * P].rearrange("p (m i) -> p i m", m=n),
                                             AX_X, ALU.add))
                dve.sem_inc(s["sc_ready"], 1)
            dve.wait_ge(s["turned"], 1)
            nc.vector.tensor_copy(T.kt[:], bank(T, 6, NP_).rearrange("p (t k) -> p t k", t=TILES)
                                  ).then_inc(s["keys_ready"], 1)
            dve_prompt_states(nc, dve, T, s, link, tot)
            dve_sample_states(nc, dve, T, s, link, tot8)
            dve_finish(nc, dve, T, s, link, T.ph[:, Q_HN:Q_HN + 1], slot, g)


def gdn_stage(nc, T, l, h, slot, more):
    q, k, v = T.gdn
    g = T.gdn_gate
    w = lambda i: T.wk[:, i, :]
    xp = T.conv
    sq = [w(5), w(6)]
    lgb, btb = w(7), w(8)
    dec, ec, bmat = w(9), w(10), w(11)
    boff, rr, rt, wz = w(12), w(13), w(14), w(15)
    qe, bv, delta, xr, kss = w(16), w(2), w(3), w(4), w(5)
    mask = lambda i: T.general[:, C_MSK + i * P:C_MSK + (i + 1) * P]
    tiled = lambda ap, n=TILES: ap[:, 0:n * P].rearrange("p (t i) -> p t i", t=n)
    col, ecol, tcol, kcol, becol = (T.cols[:, i * TILES:(i + 1) * TILES] for i in range(5))
    d8 = T.cols[:, 5 * TILES:5 * TILES + DEC_B]
    names = ("hist_in", "conv_done", "silu_done", "sq_done", "ss_done", "ss_ln",
             "ss_root", "qk_ready", "lgb_ready", "cum_done", "col_done", "dec_in", "dec_exp", "exp_done", "scored",
             "betab_done", "b_ready", "turned", "vt_ready", "r1_ready", "rt_turned", "rt_ready", "boff_ready",
             "w_done", "w_out", "z_done", "level_done", "kt_turned", "ks_done", "x_ready", "delta_done",
             "delta_ready", "u_done", "st_step", "kss_done", "kss_copied", "kss_turned", "sc_ready", "conv_out",
             "small_done", "cols_done", "ec_done", "values_in")
    with stage(nc, *W_SEMS, *AHEAD, *names, *FINISH, *STATES) as (block, s):
        s["w"] = [s["w0"], s["w1"], s["w2"], s["w3"]]

        hist = lambda c: history(xp[c])

        @block.sync
        def _(sp):
            for c in range(3):
                sp.dma_start(hist(c)[:, :, 0:3], T.d["conv_in"][l, h, c]).then_inc(s["hist_in"], 16)
            load_tile(sp, T, s, l, h, ATT_W + 1, 0)
            load_tile(sp, T, s, l, h, ATT_W + 2, 2)
            if more:
                load_tile(sp, T, s, l, h + 1, RET_W, 3)
            load_sample_state(sp, T, s, l, h, T.d["state_gdn"])
            sp.wait_ge(s["hist_in"], 48)
            for c in range(3):
                sp.dma_start(T.d["conv_prompt"][l, h, c], xp[c][:, SEQ:SEQ + 3]).then_inc(s["conv_out"], 16)
                sp.dma_start(T.d["conv_sample"][l, h, c], hist(c)[:, :, DEC_T:DEC_T + 3]).then_inc(s["conv_out"], 16)
            if more:
                sp.wait_ge(s["ahead"], 4)
                sp.dma_start(T.wtm, T.d["w_tm"][l, h + 1]).then_inc(s["values_in"], 16)
                load_tile(sp, T, s, l, h + 1, RET_W + 1, 2, after=6)
                load_tile(sp, T, s, l, h + 1, RET_W + 2, 3, after=8)
                sp.wait_ge(s["values_in"], 16)
            sp.wait_ge(s["conv_out"], 96)
            sp_states(sp, T, s, l, h, T.d["gdn_prompt"], T.d["gdn_sample"])

        @block.tensor
        def _(pe):
            ahead = lambda u, b, banks=1: pe_ahead(nc, pe, T, s, ATT_SLOTS, u, b, banks)
            ahead(0, 7)
            ahead(1, 3, banks=2)
            pe.wait_ge(s["lgb_ready"], 1)
            ut = lambda t: T.general[:, C_UT + t * P:C_UT + (t + 1) * P]
            for t in range(TILES):
                last = nc.tensor.matmul(tile(bank(T, 4, NP_), t), tile(lgb, t), ut(t), start=True, stop=True)
            last.then_inc(s["cum_done"], 1)
            one = lambda c: bank(T, 6)[:, c:c + 1]
            for t in range(TILES):
                nc.tensor.matmul(one(t), ut(t), T.lgh[:, t, :], start=True, stop=True)
                total = T.ones if t < 4 else T.general[:, C_BLK:C_BLK + P]
                nc.tensor.matmul(one(TILES + t), total, T.lgh[:, t, :], start=True, stop=True)
            nc.tensor.matmul(bank(T, 6)[:, 2 * TILES:2 * TILES + DEC_B], tile(lgb, 4), T.general[:, C_BS:C_BS + DEC_B],
                             start=True, stop=True).then_inc(s["col_done"], 1)
            ahead(2, 7, banks=2)
            ahead(3, 7)
            for c in range(2):
                pe.wait_ge(s["sq_done"], c + 1)
                wide_product(nc, T, 2 * c, lambda kk: T.ones, lambda kk: sq[c], 1).then_inc(s["ss_done"], 1)

            def attention_values(tiles, b):
                for t in tiles:
                    for kk in range(KD):
                        last = nc.tensor.matmul(bank(T, b)[:, t % 4 * P:(t % 4 + 1) * P], tile(T.xn[:, kk, :], t),
                                                T.wr[:, 2, kk, :], start=(kk == 0), stop=(kk == KD - 1))
                last.then_inc(s["ahead"], 1)

            pe.wait_ge(s["w"][2], 16)
            pe.wait_ge(s["taken"], 4)
            attention_values(range(4), 7)
            pe.wait_ge(s["qk_ready"], 2)
            for i, rhs in enumerate((k, q)):
                for t in range(TILES):
                    last = nc.tensor.matmul(tile(bank(T, 2 * i, NP_), t), tile(k, t), tile(rhs, t), start=True, stop=True)
                last.then_inc(s["scored"], 1)
            pe.wait_ge(s["exp_done"], 1)
            for t in range(TILES):
                last = nc.tensor.matmul(tile(bank(T, 4, NP_), t), tile(btb, t), T.ident, start=True, stop=True)
            last.then_inc(s["betab_done"], 1)
            pe.wait_ge(s["cols_done"], 1)
            pe.wait_ge(s["taken"], 5)
            for t in range(TILES):
                last = nc.tensor.transpose(tile(bank(T, 6, NP_), t), tile(v, t), T.ident)
            last.then_inc(s["turned"], 1)
            pe.wait_ge(s["r1_ready"], 1)
            for t in range(TILES):
                last = nc.tensor.transpose(tile(bank(T, 4, NP_), t), tile(rr, t), T.ident)
            last.then_inc(s["rt_turned"], 1)
            for r in range(1, LEVELS):
                n = TILES if r < 3 else 4
                pe.wait_ge(s["boff_ready"], r)
                pe.wait_ge(s["rt_ready"], r)
                for t in range(n):
                    last = nc.tensor.matmul(tile(bank(T, 0, NP_), t), tile(boff, t), tile(rt, t), start=True, stop=True)
                last.then_inc(s["w_done"], 1)
                pe.wait_ge(s["w_out"], r)
                for t in range(n):
                    nc.tensor.matmul(tile(bank(T, 2, NP_), t), tile(wz, t), tile(rr, t), start=True, stop=True)
                for t in range(n):
                    last = nc.tensor.matmul(tile(bank(T, 4, NP_), t), tile(rr, t), tile(wz, t), start=True, stop=True)
                last.then_inc(s["z_done"], 1)
                if r == 1:
                    pe.wait_ge(s["vt_ready"], 1)
                    attention_values((4,), 7)
                elif more and r < 5:
                    ahead(4 + r, 7)
            pe.wait_ge(s["taken"], 9 if more else 6)
            for t in range(TILES):
                last = nc.tensor.transpose(tile(bank(T, 6, NP_), t), tile(k, t), T.ident)
            last.then_inc(s["kt_turned"], 1)
            pe.wait_ge(s["s_loaded"], 16)
            pe.wait_ge(s["level_done"], 1)
            for b in range(DEC_B):
                last = nc.tensor.matmul(bank(T, 4)[:, b * DEC_T:(b + 1) * DEC_T], T.s_in[:, b, :],
                                        k[:, SEQ + b * DEC_T:SEQ + (b + 1) * DEC_T], start=True, stop=True)
            last.then_inc(s["kss_done"], 1)
            pe.wait_ge(s["kss_copied"], 1)
            nc.tensor.transpose(bank(T, 5, P), kss[:, 0:P], T.ident).then_inc(s["kss_turned"], 1)
            pe.wait_ge(s["keys_ready"], 1)
            for t in range(4):
                if t:
                    pe.wait_ge(s["st_step"], t)
                    nc.tensor.matmul(bank(T, 0, P), tile(k, t), T.st[:, t, :], start=True, stop=True).then_inc(s["ks_done"], 1)
                pe.wait_ge(s["x_ready"], t + 1)
                nc.tensor.matmul(bank(T, 1, P), tile(rr, t), tile(xr, t), start=True, stop=True).then_inc(s["delta_done"], 1)
                pe.wait_ge(s["delta_ready"], t + 1)
                nc.tensor.matmul(bank(T, 6, P), T.kt[:, t, :], tile(delta, t), start=True, stop=True).then_inc(s["u_done"], 1)
                if more and t == 1:
                    ahead(9, 7)
            pe.wait_ge(s["x_ready"], 5)
            nc.tensor.matmul(bank(T, 1, P), tile(rr, 4), tile(xr, 4), start=True, stop=True).then_inc(s["delta_done"], 1)
            pe_sample_state(nc, pe, T, s)
            pe.wait_ge(s["sc_ready"], 1)
            pe.wait_ge(s["st_ready"], 1)
            pe_outputs(nc, pe, T, s, lambda t: tile(delta, t), qe, qe)
            if more:
                ahead(10, 0)
            pe_finish(nc, pe, T, s)
            if more:
                ahead(11, 1, banks=2)

        @block.scalar
        def _(act):
            def take(u):
                if u < 4:
                    act_take(nc, act, T, s, u, 3 if u == 1 else 7, T.att[u // 2])
                else:
                    act_take(nc, act, T, s, u, 7 if u < 10 else u - 10, T.ret[u // 2 - 3],
                             ACT.Silu if u >= 10 else ACT.Copy)

            take(0)
            take(1)
            for c, dst in enumerate((q, k, v)):
                act.wait_ge(s["conv_done"], c + 1)
                nc.scalar.activation(dst[:, 0:N], dst[:, 0:N], ACT.Silu).then_inc(s["silu_done"], 1)
                if c < 2:
                    take(c + 2)
            act.wait_ge(s["silu_done"], 3)
            for c, src in enumerate((q, k)):
                nc.scalar.activation(sq[c][:, 0:N], src[:, 0:N], ACT.Square).then_inc(s["sq_done"], 1)
            for c in range(2):
                act.wait_ge(s["ss_done"], c + 1)
                nc.scalar.activation(two(sq[c]), halves(T, 2 * c), ACT.Ln, bias=T.eps).then_inc(s["ss_ln"], 1)
            for c in range(2):
                act.wait_ge(s["ss_ln"], c + 1)
                nc.scalar.activation(sq[c][:, 0:N], sq[c][:, 0:N], ACT.Exp, scale=-0.5).then_inc(s["ss_root"], 1)
            act.wait_ge(s["ahead"], 5)
            nc.scalar.copy(T.vt[:, 0:4, 2 * P:3 * P], bank(T, 7).rearrange("p (t v) -> p t v", t=4)
                           ).then_inc(s["taken"], 1)
            act.wait_ge(s["cum_done"], 1)
            nc.scalar.activation(ec, bank(T, 4, NP_), ACT.Exp).then_inc(s["ec_done"], 1)
            act.wait_ge(s["dec_in"], 1)
            nc.scalar.activation(dec, dec, ACT.Exp).then_inc(s["dec_exp"], 1)
            act.wait_ge(s["small_done"], 1)
            nc.scalar.activation(ecol, col, ACT.Exp)
            nc.scalar.activation(kcol, kcol, ACT.Exp)
            nc.scalar.activation(tcol, tcol, ACT.Exp)
            nc.scalar.activation(d8, d8, ACT.Exp).then_inc(s["exp_done"], 1)
            act.wait_ge(s["rt_turned"], 1)
            nc.scalar.copy(rt, bank(T, 4, NP_)).then_inc(s["rt_ready"], 1)
            for r in range(1, LEVELS):
                n = TILES if r < 3 else 4
                act.wait_ge(s["w_done"], r)
                nc.scalar.copy(wz[:, 0:n * P], bank(T, 0, n * P)).then_inc(s["w_out"], 1)
                if r == 1:
                    act.wait_ge(s["ahead"], 6)
                    nc.scalar.copy(T.vt[:, 4, 2 * P:3 * P], bank(T, 7, P)).then_inc(s["taken"], 1)
                elif more and r < 5:
                    if r == 2:
                        act.wait_ge(s["conv_out"], 96)
                    take(4 + r)
            act.wait_ge(s["kss_done"], 1)
            nc.scalar.copy(kss[:, 0:NS], bank(T, 4)[:, 0:NS]).then_inc(s["kss_copied"], 1)
            for t in range(TILES):
                act.wait_ge(s["delta_done"], t + 1)
                nc.scalar.copy(tile(delta, t), bank(T, 1, P)).then_inc(s["delta_ready"], 1)
                if more and t == 1:
                    take(9)
            act_square(nc, act, T, s)
            if more:
                take(10)
            act_root(nc, act, T, s)
            if more:
                take(11)

        @block.vector
        def _(dve):
            link = chained(dve, s["chain_v"])
            wide = lambda ap: ap.unsqueeze(2).to_broadcast([P, TILES, P])
            link(nc.vector.tensor_copy(T.lgh, T.logg[:, :, bass.ds(h, 1)]))
            link(nc.vector.tensor_copy(T.bth, T.beta[:, :, bass.ds(h, 1)]))
            nc.vector.tensor_copy(tiled(btb), wide(T.bth[:, :, 0]))
            nc.vector.tensor_copy(tiled(lgb), wide(T.lgh[:, :, 0])).then_inc(s["lgb_ready"], 1)
            for c in range(3):
                link(nc.vector.memset(xp[c][:, 0:3], 0.0))
            dve.wait_ge(s["hist_in"], 48)
            for c, dst in enumerate((q, k, v)):
                tap = lambda j: T.ph[:, Q_CONV + 4 * c + j:Q_CONV + 4 * c + j + 1]
                ds = dst[:, SEQ:N].rearrange("p (s t) -> p s t", s=DEC_B)
                nc.vector.tensor_scalar(dst[:, 0:SEQ], xp[c][:, 0:SEQ], tap(0), None, ALU.mult)
                link(nc.vector.tensor_scalar(ds, hist(c)[:, :, 0:DEC_T], tap(0), None, ALU.mult))
                for j in range(1, 4):
                    nc.vector.scalar_tensor_tensor(out=dst[:, 0:SEQ], in0=xp[c][:, j:j + SEQ], scalar=tap(j),
                                                   in1=dst[:, 0:SEQ], op0=ALU.mult, op1=ALU.add)
                    link(nc.vector.scalar_tensor_tensor(out=ds, in0=hist(c)[:, :, j:j + DEC_T], scalar=tap(j),
                                                        in1=ds, op0=ALU.mult, op1=ALU.add))
                dve.sem_inc(s["conv_done"], 1)
            for c, dst in enumerate((q, k)):
                dve.wait_ge(s["ss_root"], c + 1)
                nc.vector.scalar_tensor_tensor(out=dst[:, 0:N], in0=dst[:, 0:N], scalar=K_SCALE if c == 0 else 1.0,
                                               in1=sq[c][:, 0:N], op0=ALU.mult, op1=ALU.mult).then_inc(s["qk_ready"], 1)
            dve.wait_ge(s["cum_done"], 1)
            dve.wait_ge(s["col_done"], 1)
            link(nc.vector.tensor_copy(col, bank(T, 6)[:, 0:TILES]))
            link(nc.vector.tensor_copy(tcol, bank(T, 6)[:, TILES:2 * TILES]))
            link(nc.vector.tensor_copy(d8, bank(T, 6)[:, 2 * TILES:2 * TILES + DEC_B]))
            dve.sem_inc(s["cols_done"], 1)
            link(nc.vector.tensor_tensor(kcol, tcol, col, ALU.subtract))
            dve.sem_inc(s["small_done"], 1)
            dve.wait_ge(s["ec_done"], 1)
            for t in range(TILES):
                last = nc.vector.tensor_scalar(tile(dec, t), tile(bank(T, 4, NP_), t), col[:, t:t + 1], 0.0,
                                               ALU.subtract, ALU.min)
            last.then_inc(s["dec_in"], 1)
            dve.wait_ge(s["dec_exp"], 1)
            link(nc.vector.tensor_tensor(dec, dec, T.general[:, C_UT:C_UT + NP_], ALU.mult))
            dve.wait_ge(s["exp_done"], 1)
            dve.wait_ge(s["betab_done"], 1)
            dve.wait_ge(s["scored"], 1)
            link(nc.vector.tensor_tensor(bmat, bank(T, 0, NP_), dec, ALU.mult))
            link(nc.vector.tensor_tensor(bmat, bmat, bank(T, 4, NP_), ALU.mult))
            dve.wait_ge(s["scored"], 2)
            link(nc.vector.tensor_tensor(T.sc, bank(T, 2, NP_), dec, ALU.mult))
            dve.sem_inc(s["sc_ready"], 1)
            spread = lambda i, n=TILES: mask(i).unsqueeze(1).to_broadcast([P, n, P])
            link(nc.vector.tensor_tensor(tiled(rr), tiled(bmat), spread(1), ALU.mult))
            link(nc.vector.scalar_tensor_tensor(out=tiled(rr), in0=tiled(rr), scalar=-1.0, in1=spread(0),
                                                op0=ALU.mult, op1=ALU.add))
            dve.sem_inc(s["r1_ready"], 1)
            dve.wait_ge(s["turned"], 1)
            nc.vector.tensor_tensor(tiled(bv), bank(T, 6, NP_).rearrange("p (t i) -> p t i", t=TILES),
                                    wide(T.bth[:, :, 0]), ALU.mult).then_inc(s["vt_ready"], 1)
            link(nc.vector.tensor_tensor(qe, q, ec, ALU.mult))
            link(nc.vector.scalar_tensor_tensor(out=becol, in0=ecol, scalar=-1.0, in1=T.bth[:, :, 0],
                                                op0=ALU.mult, op1=ALU.mult))
            link(nc.vector.memset(kss, 0.0))
            for r in range(1, LEVELS):
                n = TILES if r < 3 else 4
                nc.vector.tensor_tensor(tiled(boff, n), tiled(bmat, n), spread(1 + r, n), ALU.mult
                                        ).then_inc(s["boff_ready"], 1)
                dve.wait_ge(s["z_done"], r)
                link(nc.vector.tensor_tensor(rr[:, 0:n * P], rr[:, 0:n * P], bank(T, 2, n * P), ALU.subtract))
                link(nc.vector.tensor_tensor(rt[:, 0:n * P], rt[:, 0:n * P], bank(T, 4, n * P), ALU.subtract))
                dve.sem_inc(s["rt_ready"], 1)
                if r == LEVELS - 1:
                    dve.sem_inc(s["level_done"], 1)
            dve.wait_ge(s["kt_turned"], 1)
            nc.vector.tensor_tensor(T.kt[:], bank(T, 6, NP_).rearrange("p (t i) -> p t i", t=TILES), wide(kcol),
                                    ALU.mult).then_inc(s["keys_ready"], 1)
            dve.wait_ge(s["keys_ready"], 1)
            for t in range(4):
                if t == 0:
                    nc.vector.tensor_copy(tile(xr, 0), tile(bv, 0)).then_inc(s["x_ready"], 1)
                else:
                    dve.wait_ge(s["ks_done"], t)
                    nc.vector.scalar_tensor_tensor(out=tile(xr, t), in0=bank(T, 0, P), scalar=becol[:, t:t + 1],
                                                   in1=tile(bv, t), op0=ALU.mult, op1=ALU.add).then_inc(s["x_ready"], 1)
                dve.wait_ge(s["u_done"], t + 1)
                if t == 0:
                    nc.vector.tensor_copy(T.st[:, 1, :], bank(T, 6, P)).then_inc(s["st_step"], 1)
                else:
                    nc.vector.scalar_tensor_tensor(out=T.st[:, t + 1, :], in0=T.st[:, t, :], scalar=tcol[:, t:t + 1],
                                                   in1=bank(T, 6, P), op0=ALU.mult, op1=ALU.add).then_inc(s["st_step"], 1)
                dve.wait_ge(s["st_step"], t + 1)
            dve.sem_inc(s["st_ready"], 1)
            dve.wait_ge(s["kss_turned"], 1)
            nc.vector.scalar_tensor_tensor(out=tile(xr, 4), in0=bank(T, 5, P), scalar=becol[:, 4:5],
                                           in1=tile(bv, 4), op0=ALU.mult, op1=ALU.add).then_inc(s["x_ready"], 1)
            dve.wait_ge(s["delta_ready"], 5)
            dve_spread_values(nc, T, s, delta[0:NS, 4 * P:5 * P])
            dve_sample_states(nc, dve, T, s, link, d8)
            dve_finish(nc, dve, T, s, link, T.ph[:, Q_GN:Q_GN + 1], slot, g)



def attention_stage(nc, T, l, h, slot, more):
    q, k = T.att
    w = lambda i: T.wk[:, i, :]
    sq = [w(2), w(3)]
    score = [w(2), w(3)]
    prob = [w(4), w(5)]
    diag = [w(6)[:, 0:P], w(6)[:, P:2 * P]]
    at = w(7)
    qm = T.wk[:, 8:10, :].rearrange("p a b -> p (a b)")[:, 0:(DEC_B + 1) * P]
    kc = T.wk[:, 10:14, :].rearrange("p a b -> p (a b)")[:, 0:DEC_B * PAST]
    vc = T.wk[:, 14:18, :].rearrange("p a b -> p (a b)")[:, 0:DEC_B * PAST]
    mx, sm = T.cols[:, 0:2], T.cols[:, 2:4]
    vt = lambda t: T.vt[:, t, 2 * P:3 * P]
    dc = T.dc
    names = ("w2", "w3", "hc_in", "valued", "copied", "v_out", "pt_in", "kv_in", "sq_done", "ss_done", "ss_ln", "ss_root", "qk_ready",
             "k_out", "scored", "biased", "exp_in", "exped", "diag_ready", "turned", "at_ready", "o_tile",
             "qm_ready", "s_scored", "s_turned", "s_at")
    rounds = [(t, c) for t in range(4) for c in range(2)]
    with stage(nc, *names, *FINISH) as (block, s):
        s["w"] = [None, None, s["w2"], s["w3"]]

        @block.sync
        def _(sp):
            sp.dma_start(T.pt[0:1, :], T.d["page_table"]).then_inc(s["pt_in"], 16)
            if more:
                load_tile(sp, T, s, l, h + 1, HGRN_W, 2)
                load_tile(sp, T, s, l, h + 1, HGRN_W + 1, 3)
                sp.dma_start(T.hc[:], T.d["hc"][h + 1]).then_inc(s["hc_in"], 16)
            sp.dma_start(T.d["v_prompt"][l, h].rearrange("(t p) d -> p t d", p=P),
                         T.vt[:, 0:4, 2 * P:3 * P]).then_inc(s["v_out"], 16)
            sp.dma_start(T.d["v_sample"][l, h], T.vt[0:NS, 4, 2 * P:3 * P]).then_inc(s["v_out"], 16)
            sp.wait_ge(s["pt_in"], 16)
            with sp.Fori(0, DEC_B * PAGES) as i:
                page = sp.value_load(T.pt[0:1, bass.ds(i, 1)], min_val=0, max_val=N_PHYS - 1)
                sp.dma_start(kc[:, bass.ds(i * PAGE, PAGE)], T.d["cache_k"][l, page, h]).then_inc(s["kv_in"], 16)
                sp.dma_start(vc[:, bass.ds(i * PAGE, PAGE)], T.d["cache_v"][l, page, h]).then_inc(s["kv_in"], 16)
            sp.wait_ge(s["qk_ready"], 2)
            sp.dma_start(T.d["k_out"][l, h], k[:, 0:N]).then_inc(s["k_out"], 16)
            sp.wait_ge(s["k_out"], 16)
            sp.wait_ge(s["v_out"], 32)
            if more:
                sp.wait_ge(s["w2"], 16)
                sp.wait_ge(s["w3"], 16)
                sp.wait_ge(s["hc_in"], 16)

        @block.tensor
        def _(pe):
            def value_tile(t):
                if t:
                    pe.wait_ge(s["copied"], t)
                pe_value_tile(nc, T, t, 3).then_inc(s["valued"], 1)

            if more:
                value_tile(0)
            for c in range(2):
                pe.wait_ge(s["sq_done"], c + 1)
                wide_product(nc, T, 4 + 2 * c, lambda kk: T.general[:, C_COMP:C_COMP + P], lambda kk: sq[c],
                             1).then_inc(s["ss_done"], 1)
            if more:
                value_tile(1)
            pe.wait_ge(s["qk_ready"], 2)

            def scores(t, c):
                if t:
                    pe.wait_ge(s["biased"], 2 * (t - 1) + c + 1)
                rows = slice(c * DK, (c + 1) * DK)
                nc.tensor.matmul(bank(T, c)[:, 0:(t + 1) * P], tile(q, t)[rows], k[rows, 0:(t + 1) * P],
                                 start=True, stop=True).then_inc(s["scored"], 1)

            scores(0, 0)
            scores(0, 1)
            for t in range(4):
                pe.wait_ge(s["diag_ready"], 2 * (t + 1))
                for i in range(t + 1):
                    for c in range(2):
                        last = nc.tensor.matmul(tile(bank(T, 2), i), tile(prob[c], i), diag[c],
                                                start=(c == 0), stop=(c == 1))
                last.then_inc(s["turned"], 1)
                if t < 3:
                    scores(t + 1, 0)
                    scores(t + 1, 1)
                    if more and t < 2:
                        value_tile(t + 2)
                pe.wait_ge(s["at_ready"], t + 1)
                for i in range(t + 1):
                    last = nc.tensor.matmul(tile(bank(T, 4), t), vt(i), tile(at, i), start=(i == 0), stop=(i == t))
                last.then_inc(s["o_tile"], 1)
            pe.wait_ge(s["qm_ready"], 1)
            pe.wait_ge(s["kv_in"], 32 * DEC_B * PAGES)
            new = bank(T, 0)[:, PAST:PAST + NS]
            pe.wait_ge(s["biased"], 8)
            nc.tensor.matmul(new, qm[:, DEC_B * P:(DEC_B + 1) * P], k[:, SEQ:N], start=True, stop=True)
            for b in range(DEC_B):
                last = nc.tensor.matmul(bank(T, 0)[:, 0:PAST], tile(qm, b), kc[:, b * PAST:(b + 1) * PAST],
                                        start=(b == 0), stop=(b == DEC_B - 1))
            last.then_inc(s["s_scored"], 1)
            if more:
                value_tile(4)
            pe.wait_ge(s["diag_ready"], 9)
            for i in range(PAGES):
                nc.tensor.matmul(bank(T, 2)[:, i * NS:(i + 1) * NS], tile(prob[0], i), diag[0][:, 0:NS],
                                 start=True, stop=True)
            nc.tensor.matmul(bank(T, 2)[0:NS, PAGES * NS:(PAGES + 1) * NS], prob[0][:, PAST:PAST + NS],
                             diag[0][:, 0:NS], start=True, stop=True).then_inc(s["s_turned"], 1)
            pe.wait_ge(s["s_at"], 2)
            o = bank(T, 5)
            nc.tensor.matmul(o[:, 0:NS], T.vt[0:NS, 4, 2 * P:3 * P], at[0:NS, PAGES * NS:(PAGES + 1) * NS],
                             start=True, stop=False)
            for b in range(DEC_B):
                for i in range(PAGES):
                    last = nc.tensor.matmul(o[:, b * DEC_T:(b + 1) * DEC_T], tile(vc, b * PAGES + i),
                                            at[:, i * NS + b * DEC_T:i * NS + (b + 1) * DEC_T], start=False,
                                            stop=(b == DEC_B - 1 and i == PAGES - 1))
            last.then_inc(s["o_ready"], 1)
            pe_finish(nc, pe, T, s)

        @block.scalar
        def _(act):
            def copy_values(t):
                act.wait_ge(s["valued"], t + 1)
                nc.scalar.copy(T.vt[:, t, 0:2 * P], bank(T, 3)[:, 0:2 * P]).then_inc(s["copied"], 1)

            for c, src in enumerate((q, k)):
                nc.scalar.activation(sq[c][:, 0:N], src[:, 0:N], ACT.Square).then_inc(s["sq_done"], 1)
            if more:
                copy_values(0)
            for c in range(2):
                act.wait_ge(s["ss_done"], c + 1)
                nc.scalar.activation(two(sq[c]), halves(T, 4 + 2 * c), ACT.Ln, bias=T.eps, scale=1.0 / DK
                                     ).then_inc(s["ss_ln"], 1)
            for c in range(2):
                act.wait_ge(s["ss_ln"], c + 1)
                nc.scalar.activation(sq[c][:, 0:N], sq[c][:, 0:N], ACT.Exp, scale=-0.5).then_inc(s["ss_root"], 1)
            if more:
                copy_values(1)
            for i, (t, c) in enumerate(rounds):
                act.wait_ge(s["exp_in"], i + 1)
                if t:
                    act.wait_ge(s["turned"], t)
                nc.scalar.activation(prob[c][:, 0:(t + 1) * P], score[c][:, 0:(t + 1) * P], ACT.Exp,
                                     bias=mx[:, c:c + 1], scale=S_SCALE, accum_out=sm[:, c:c + 1]).then_inc(s["exped"], 1)
                if c == 1:
                    act.wait_ge(s["turned"], t + 1)
                    if t:
                        act.wait_ge(s["o_tile"], t)
                    nc.scalar.copy(at[:, 0:(t + 1) * P], bank(T, 2)[:, 0:(t + 1) * P]).then_inc(s["at_ready"], 1)
                    if more and t < 2:
                        copy_values(t + 2)
            act.wait_ge(s["exp_in"], 9)
            nc.scalar.activation(prob[0][:, 0:PAST + NS], score[0][:, 0:PAST + NS], ACT.Exp, bias=mx[:, 0:1],
                                 scale=S_SCALE, accum_out=sm[:, 0:1]).then_inc(s["exped"], 1)
            if more:
                copy_values(4)
            act.wait_ge(s["s_turned"], 1)
            act.wait_ge(s["o_tile"], 4)
            nc.scalar.copy(at[:, 0:PAGES * NS], bank(T, 2)[:, 0:PAGES * NS]).then_inc(s["s_at"], 1)
            nc.scalar.copy(at[0:NS, PAGES * NS:(PAGES + 1) * NS],
                           bank(T, 2)[0:NS, PAGES * NS:(PAGES + 1) * NS]).then_inc(s["s_at"], 1)
            act_square(nc, act, T, s)
            act_root(nc, act, T, s)

        @block.vector
        def _(dve):
            link = chained(dve, s["chain_v"])
            for c, dst in enumerate((q, k)):
                dve.wait_ge(s["ss_root"], c + 1)
                nc.vector.scalar_tensor_tensor(out=dst[:, 0:N], in0=dst[:, 0:N],
                                               scalar=T.ph[:, Q_QN + c:Q_QN + c + 1], in1=sq[c][:, 0:N],
                                               op0=ALU.mult, op1=ALU.mult).then_inc(s["qk_ready"], 1)
            dve.wait_ge(s["qk_ready"], 2)
            slope = T.ph[:, Q_SL:Q_SL + 1]

            def softmax_input(i, c, dist, src, n):
                if i >= 2:
                    dve.wait_ge(s["exped"], min(i, 8) - 1 if i < 8 else 8)
                nc.vector.scalar_tensor_tensor(out=score[c][:, 0:n], in0=dist, scalar=slope, in1=src,
                                               op0=ALU.mult, op1=ALU.add).then_inc(s["biased"], 1)
                dve.wait_ge(s["biased"], i + 1)
                link(nc.vector.tensor_reduce(mx[:, c:c + 1], score[c][:, 0:n], AX_X, ALU.max))
                nc.vector.tensor_scalar(mx[:, c:c + 1], mx[:, c:c + 1], -S_SCALE, None, ALU.mult).then_inc(s["exp_in"], 1)

            for t in range(4):
                n = (t + 1) * P
                for c in range(2):
                    i = 2 * t + c
                    dve.wait_ge(s["scored"], i + 1)
                    softmax_input(i, c, dc[:, C_DP + SEQ - n:C_DP + SEQ], bank(T, c)[:, 0:n], n)
                for c in range(2):
                    i = 2 * t + c
                    dve.wait_ge(s["exped"], i + 1)
                    if t:
                        dve.wait_ge(s["turned"], t)
                    link(nc.vector.reciprocal(sm[:, c:c + 1], sm[:, c:c + 1]))
                    if c:
                        link(nc.vector.tensor_scalar(sm[:, 1:2], sm[:, 1:2], T.lam[:, 2:3], None, ALU.mult))
                    nc.vector.tensor_scalar(diag[c], T.ident, sm[:, c:c + 1], None, ALU.mult
                                            ).then_inc(s["diag_ready"], 1)
            nc.vector.tensor_tensor(qm.rearrange("p (a t) -> p a t", t=NS),
                                    q[:, SEQ:N].unsqueeze(1).to_broadcast([P, 2 * (DEC_B + 1), NS]),
                                    dc[:, C_QM:C_QM + (DEC_B + 1) * P].rearrange("p (a t) -> p a t", t=NS),
                                    ALU.mult).then_inc(s["qm_ready"], 1)
            dve.wait_ge(s["s_scored"], 1)
            softmax_input(8, 0, dc[:, C_DS:C_DS + PAST + NS], bank(T, 0)[:, 0:PAST + NS], PAST + NS)
            dve.wait_ge(s["exped"], 9)
            dve.wait_ge(s["turned"], 4)
            link(nc.vector.reciprocal(sm[:, 0:1], sm[:, 0:1]))
            link(nc.vector.tensor_scalar(sm[:, 0:1], sm[:, 0:1], T.lam[:, 3:4], None, ALU.mult))
            nc.vector.tensor_scalar(diag[0][:, 0:NS], dc[:, C_STK:C_STK + NS], sm[:, 0:1], None, ALU.mult
                                    ).then_inc(s["diag_ready"], 1)
            link(nc.vector.tensor_tensor(T.cols[:, 4:5], T.ph[:, Q_DN:Q_DN + 1], T.pl[:, L_OL:L_OL + 1], ALU.mult))
            dve_finish(nc, dve, T, s, link, T.cols[:, 4:5], slot, None)


def head(nc, T, l, h, more):
    retention_stage(nc, T, l, h, br_slot(0, h))
    hgrn_stage(nc, T, l, h, br_slot(1, h))
    gdn_stage(nc, T, l, h, br_slot(2, h), more)
    attention_stage(nc, T, l, h, br_slot(3, h), more)


def merge_stage(nc, T, l):
    with stage(nc, "w_even", "w_odd", "w_free", "gated", "sig_done", "added", "chain_v") as (block, s):
        w_in = (s["w_even"], s["w_odd"])

        @block.sync
        def _(sp):
            with sp.Fori(0, KD) as m:
                for b in range(4):
                    sp.wait_ge(s["w_free"], 4 * m + b + 1)
                    sp.dma_start(T.wm[:, b % 2], T.d["w_merge"][l, m, b]).then_inc(w_in[b % 2], 16)

        @block.tensor
        def _(pe):
            pe.sem_inc(s["w_free"], 2)
            with pe.Fori(0, KD) as m:
                for b in range(4):
                    i = b % 2
                    pe.wait_ge(w_in[i], 32 * m + 16 * (b // 2) + 16)
                    pe.wait_ge(s["added"], 4 * m + b + 1)
                    wide_product(nc, T, 4 * i, lambda k: T.wm[:, i, k, :], lambda k: T.xn[:, k, :], KD
                                 ).then_inc(s["gated"], 1)
                    wide_product(nc, T, 4 * i + 2, lambda k: T.wm[:, i, KD + k, :],
                                 lambda k: T.br[:, 4 * b + k, :], 4).then_inc(s["w_free"], 1)

        @block.scalar
        def _(act):
            with act.Fori(0, KD) as m:
                for b in range(4):
                    i = b % 2
                    act.wait_ge(s["gated"], 4 * m + b + 1)
                    act.wait_ge(s["added"], 4 * m + b + 1)
                    nc.scalar.activation(T.sg[i], halves(T, 4 * i), ACT.Sigmoid).then_inc(s["sig_done"], 1)

        @block.vector
        def _(dve):
            dve.sem_inc(s["added"], 2)
            with dve.Fori(0, KD) as m:
                for b in range(4):
                    i = b % 2
                    dve.wait_ge(s["sig_done"], 4 * m + b + 1)
                    dve.wait_ge(s["w_free"], 4 * m + b + 3)
                    if b == 0:
                        dve.wait_ge(s["added"], 4 * m + 2)
                        nc.vector.tensor_tensor(T.ma, T.sg[i], halves(T, 4 * i + 2), ALU.mult).then_inc(s["added"], 1)
                    else:
                        nc.vector.tensor_tensor(T.sg[i], T.sg[i], halves(T, 4 * i + 2), ALU.mult
                                                ).then_inc(s["chain_v"], 1)
                        dve.wait_ge(s["chain_v"], 3 * m + b)
                        dve.wait_ge(s["added"], 4 * m + b + 2)
                        out = T.ma if b < 3 else two(T.mt[:, bass.ds(m, 1), :].rearrange("p a n -> p (a n)"))
                        nc.vector.tensor_tensor(out, T.ma, T.sg[i], ALU.add).then_inc(s["added"], 1)


def out_stage(nc, T, l):
    with stage(nc, "w_even", "w_odd", "x_in", "produced", "added", "x_out") as (block, s):
        w_in = (s["w_even"], s["w_odd"])

        @block.sync
        def _(sp):
            sp.dma_start(T.h[:], T.d["xs"].rearrange("m p n -> p m n")).then_inc(s["x_in"], 16)
            with sp.Fori(0, KD // 2) as g:
                for i in range(2):
                    sp.wait_ge(s["produced"], 2 * g + i + 1)
                    sp.dma_start(T.wm[:, i, 0:KD, :], T.d["w_out"][l, 2 * g + i]).then_inc(w_in[i], 16)
            sp.wait_ge(s["added"], KD + 2)
            sp.dma_start(T.d["xs"].rearrange("m p n -> p m n"), T.h[:]).then_inc(s["x_out"], 16)
            sp.wait_ge(s["x_out"], 16)

        @block.tensor
        def _(pe):
            pe.sem_inc(s["produced"], 2)
            with pe.Fori(0, KD // 2) as g:
                for i in range(2):
                    pe.wait_ge(w_in[i], 16 * g + 16)
                    pe.wait_ge(s["added"], 2 * g + i + 1)
                    wide_product(nc, T, 2 * i, lambda k: T.wm[:, i, k, :], lambda k: T.mt[:, k, :], KD
                                 ).then_inc(s["produced"], 1)

        @block.vector
        def _(dve):
            dve.sem_inc(s["added"], 2)
            dve.wait_ge(s["x_in"], 16)
            with dve.Fori(0, KD // 2) as g:
                for i in range(2):
                    dve.wait_ge(s["produced"], 2 * g + i + 3)
                    row = two(T.h[:, bass.ds(2 * g + i, 1), :].rearrange("p a n -> p (a n)"))
                    nc.vector.tensor_tensor(row, row, halves(T, 2 * i), ALU.add).then_inc(s["added"], 1)


def key_scores_stage(nc, T, l):
    with stage(nc, "w_even", "w_odd", "keys_in", "w_free", "q_done", "q_out", "scored", "kept",
               "zeroed", "counted", "cast") as (block, s):
        w_in = (s["w_even"], s["w_odd"])

        @block.gpsimd
        def _(pool):
            nc.gpsimd.iota(T.iota[:], pattern=[[1, P]], base=0, channel_multiplier=0,
                           allow_small_or_imprecise_dtypes=True).then_inc(s["counted"], 1)

        @block.sync
        def _(sp):
            sp.dma_start(T.keys, T.d["keys"][l]).then_inc(s["keys_in"], 16)
            with sp.Fori(0, PH_HEADS) as g:
                for i in range(2):
                    sp.wait_ge(s["q_done"], 2 * g + i + 1)
                    sp.dma_start(T.wm2[:, i], T.d["w_query"][l, 2 * g + i]).then_inc(w_in[i], 16)

        @block.tensor
        def _(pe):
            pe.sem_inc(s["q_done"], 2)
            pe.wait_ge(s["keys_in"], 16)

            def queries(j, i):
                pe.wait_ge(w_in[i], 8 * (j - i) + 16)
                pe.wait_ge(s["q_out"], j + 1)
                wide_product(nc, T, 2 * i, lambda k: T.wm2[:, i, k, :], lambda k: T.xn[:, k, :], KD
                             ).then_inc(s["q_done"], 1)

            def scores(j, i):
                pe.wait_ge(s["q_out"], j + 3)
                pe.wait_ge(s["kept"], j + 1)
                for t in range(TILES):
                    last = nc.tensor.matmul(tile(bank(T, 4 + 2 * i, NP_), t), tile(T.qt[i], t),
                                            T.keys[:, bass.ds(j, 1), :].rearrange("p a n -> p (a n)"),
                                            start=True, stop=True)
                last.then_inc(s["scored"], 1)

            queries(0, 0)
            with pe.Fori(0, PH_HEADS - 1) as g:
                for i in range(2):
                    queries(2 * g + i + 1, 1 - i)
                    scores(2 * g + i, i)
            queries(2 * PH_HEADS - 1, 1)
            scores(2 * PH_HEADS - 2, 0)
            scores(2 * PH_HEADS - 1, 1)

        @block.scalar
        def _(act):
            act.wait_ge(s["zeroed"], 1)
            act.sem_inc(s["q_out"], 2)
            with act.Fori(0, PH_HEADS) as g:
                for i in range(2):
                    act.wait_ge(s["q_done"], 2 * g + i + 3)
                    act.wait_ge(s["kept"], 2 * g + i + 1)
                    nc.scalar.copy(two(T.qt[i]), halves(T, 2 * i)).then_inc(s["q_out"], 1)

        @block.vector
        def _(dve):
            for i in range(2):
                last = nc.vector.memset(T.qt[i], 0.0)
            last.then_inc(s["zeroed"], 1)
            dve.sem_inc(s["kept"], 2)
            nc.vector.memset(T.zero, 0.0).then_inc(s["cast"], 1)
            dve.wait_ge(s["counted"], 1)
            nc.vector.tensor_copy(T.iota_b, T.iota[:]).then_inc(s["cast"], 1)
            dve.wait_ge(s["cast"], 2)
            with dve.Fori(0, PH_HEADS) as g:
                for i in range(2):
                    dve.wait_ge(s["scored"], 2 * g + i + 1)
                    nc.vector.tensor_copy(T.scr[:, :, bass.ds(2 * g + i, 1), :],
                                          bank(T, 4 + 2 * i, NP_).rearrange("p (t a k) -> p t a k", t=TILES, a=1)
                                          ).then_inc(s["kept"], 1)


def retrieval_stage(nc, T, l):
    LOW = -3.0e38
    STEPS = 20
    with stage(nc, "u_even", "u_odd", "dotted", "activated", "chain_v", "exp_in", "exped", "found", "turned",
               "tail") as (block, s):
        @block.sync
        def _(sp):
            sp_expert_weights(sp, T, s, T.d["u"], l, 0)

        @block.scalar
        def _(act):
            act_gelu(nc, act, T, s, 0)
            act.wait_ge(s["exp_in"], 1)
            nc.scalar.activation(T.t2[:], T.t2[:], ACT.Exp).then_inc(s["exped"], 1)

        @block.tensor
        def _(pe):
            pe.sem_inc(s["dotted"], 2)
            with pe.Fori(0, PART // 2) as j:
                for i in range(2):
                    pe_expert_dots(nc, pe, T, s, j, i)
            pe.wait_ge(s["found"], 1)
            for z in range(3):
                pe.wait_ge(s["turned"], z)
                if z:
                    pe.wait_ge(s["tail"], z)
                for t in range(TILES):
                    last = nc.tensor.transpose(tile(bank(T, 4, NP_), t), T.found[:, z, t, :], T.ident)
                last.then_inc(s["turned"], 1)

        @block.vector
        def _(dve):
            count = [0]

            def link(instruction, t):
                count[0] += 1
                instruction.then_inc(s["chain_v"], 1)
                dve.wait_ge(s["chain_v"], STEPS * t + count[0])

            def best(t, values, idx, scores):
                rows = range(scores.shape[1])
                v = nc.vector
                for r in range(2):
                    part = slice(8 * r, 8 * r + 8)
                    v.memset(T.spare, 0.0)
                    for j in rows:
                        last = v.max(values[:, j, part], scores[:, j, :])
                    link(last, t)
                    v.memset(T.spare, 0.0)
                    for j in rows:
                        last = v.max_index(idx[:, j, part], values[:, j, part], scores[:, j, :])
                    link(last, t)
                    if r == 0:
                        v.memset(T.spare, 0.0)
                        for j in rows:
                            last = v.match_replace(scores[:, j, :], values[:, j, part], scores[:, j, :], LOW)
                        link(last, t)

            with dve.Fori(0, TILES) as t:
                count[0] = 0
                link(nc.vector.tensor_copy(T.x1, T.scr[:, bass.ds(t, 1)].rearrange("p a h k -> p (a h) k")), t)
                best(t, T.t1, T.i1u, T.x1)
                nc.vector.tensor_copy(T.i1f, T.i1u)
                side = T.t1.rearrange("p (h z) a -> p h z a", z=2)
                link(nc.vector.tensor_tensor(
                    T.cand.rearrange("p h (a b) -> p h a b", a=TOPK),
                    side[:, :, 0, :].unsqueeze(3).to_broadcast([P, PH_HEADS, TOPK, TOPK]),
                    side[:, :, 1, :].unsqueeze(2).to_broadcast([P, PH_HEADS, TOPK, TOPK]), ALU.add), t)
                best(t, T.tv, T.posu, T.cand)
                nc.vector.tensor_copy(T.t2[:, bass.ds(t, 1)].rearrange("p a h k -> p (a h) k"), T.tv)
                nc.vector.tensor_scalar(T.pau, T.posu, 4, None, ALU.logical_shift_right)
                link(nc.vector.tensor_scalar(T.pbu, T.posu, 15, None, ALU.bitwise_and), t)
                nc.vector.tensor_copy(T.paf, T.pau)
                link(nc.vector.tensor_copy(T.pbf, T.pbu), t)
                sidei = T.i1f.rearrange("p (h z) a -> p h z a", z=2)
                iota = T.iota[:, 0:TOPK].unsqueeze(1).to_broadcast([P, P, TOPK])
                for z, place in enumerate((T.paf, T.pbf)):
                    eq = T.x1.rearrange("p h k -> p (h k)").rearrange("p (c a) -> p c a", a=TOPK)
                    link(nc.vector.tensor_tensor(eq, place.rearrange("p h k -> p (h k)").unsqueeze(2).to_broadcast(
                        [P, P, TOPK]), iota, ALU.is_equal), t)
                    eq4 = eq.rearrange("p (h k) a -> p h k a", h=PH_HEADS)
                    link(nc.vector.tensor_tensor(eq4, eq4, sidei[:, :, z, :].unsqueeze(2).to_broadcast(
                        [P, PH_HEADS, TOPK, TOPK]), ALU.mult), t)
                    out = T.found[:, z, bass.ds(t, 1), :].rearrange("p a c -> p (a c)")
                    if z == 0:
                        link(nc.vector.tensor_reduce(out, eq, AX_X, ALU.add), t)
                    else:
                        nc.vector.tensor_reduce(out, eq, AX_X, ALU.add).then_inc(s["chain_v"], 1)
                        dve.wait_ge(s["chain_v"], STEPS * t + STEPS)
                assert count[0] == STEPS - 1
            done = [STEPS * TILES]

            def then(instruction):
                done[0] += 1
                instruction.then_inc(s["chain_v"], 1)
                dve.wait_ge(s["chain_v"], done[0])

            t2 = T.t2.rearrange("p t h k -> p (t h) k")
            rows = [P, TILES * PH_HEADS, TOPK]
            then(nc.vector.tensor_copy(T.gs, t2[:, :, 0]))
            nc.vector.tensor_tensor(t2, t2, T.gs.unsqueeze(2).to_broadcast(rows), ALU.subtract
                                    ).then_inc(s["exp_in"], 1)
            dve.wait_ge(s["exped"], 1)
            then(nc.vector.tensor_reduce(T.gs, t2, AX_X, ALU.add))
            then(nc.vector.reciprocal(T.gs, T.gs))
            then(nc.vector.scalar_tensor_tensor(
                out=T.found[:, 2].rearrange("p t (h k) -> p (t h) k", k=TOPK), in0=t2, scalar=G_SCALE,
                in1=T.gs.unsqueeze(2).to_broadcast(rows), op0=ALU.mult, op1=ALU.mult))
            dve.sem_inc(s["found"], 1)
            for z in range(2):
                dve.wait_ge(s["turned"], z + 1)
                nc.vector.tensor_copy(T.idx[:, z, :], bank(T, 4, NP_)).then_inc(s["tail"], 1)
            dve.wait_ge(s["tail"], 2)
            dve.wait_ge(s["turned"], 3)
            then(nc.vector.tensor_copy(T.idx[:, 2, :], bank(T, 4, NP_)))
            then(nc.vector.tensor_tensor(T.idx[:, 3, :], bank(T, 4, NP_), T.idx[:, 2, :], ALU.subtract))


def sp_expert_weights(sp, T, s, table, l, part):
    with sp.Fori(0, PART // 2) as j:
        for i in range(2):
            sp.wait_ge(s["dotted"], 2 * j + i + 1)
            sp.dma_start(T.ur[:, i], table[l, part, 2 * j + i]).then_inc(s["u_odd" if i else "u_even"], 16)


def pe_expert_dots(nc, pe, T, s, j, i):
    pe.wait_ge(s["u_odd" if i else "u_even"], 16 * j + 16)
    pe.wait_ge(s["activated"], 2 * j + i + 1)
    wide_product(nc, T, 2 * i, lambda k: T.ur[:, i, k, :], lambda k: T.xn[:, k, :], KD).then_inc(s["dotted"], 1)


def act_gelu(nc, act, T, s, part):
    g = T.g[part % 2]
    act.sem_inc(s["activated"], 2)
    with act.Fori(0, PART // 2) as j:
        for i in range(2):
            act.wait_ge(s["dotted"], 2 * j + i + 3)
            nc.scalar.activation(two(g[:, bass.ds(2 * j + i, 1), :].rearrange("p a n -> p (a n)")),
                                 halves(T, 2 * i), ACT.Gelu).then_inc(s["activated"], 1)


def dve_iota(nc, dve, T, s, part):
    nc.vector.tensor_copy(T.iota_h, T.iota_b[:, part * PART:(part + 1) * PART]).then_inc(s["iota_ready"], 1)
    dve.wait_ge(s["iota_ready"], 1)


def dve_rows(nc, dve, T, s, step, i, gt):
    cols = bass.ds(step * gt, gt)
    one = lambda z: T.idx[:, z, cols]
    dve.wait_ge(s["summed"], step + 1)
    nc.vector.tensor_tensor(T.oh1[:, i], T.iota_b.unsqueeze(1).to_broadcast([P, gt, P]),
                            one(0).unsqueeze(2).to_broadcast([P, gt, P]), ALU.is_equal)
    nc.vector.tensor_tensor(T.eq2[:, i], T.iota_h.unsqueeze(1).to_broadcast([P, gt, PART]),
                            one(1).unsqueeze(2).to_broadcast([P, gt, PART]), ALU.is_equal).then_inc(s["eq_ready"], 1)
    dve.wait_ge(s["eq_ready"], step + 1)
    nc.vector.tensor_tensor(T.oh2[:, i], T.eq2[:, i].unsqueeze(2).to_broadcast([P, gt, 2, PART]),
                            T.idx[:, 2:4, cols].rearrange("p z n -> p n z").unsqueeze(3).to_broadcast(
                                [P, gt, 2, PART]), ALU.mult).then_inc(s["rows_ready"], 1)


def pe_sums(nc, pe, T, s, step, i, banks, gt):
    pe.wait_ge(s["rows_ready"], step + 1)
    pe.wait_ge(s["kept"], step + 1)
    n = gt // len(banks)
    for t in range(gt):
        out = bank(T, banks[t // n])[:, t % n * PART:][:, 0:PART]
        for z in range(2):
            last = nc.tensor.matmul(out, T.oh1[:, i, t, :], T.oh2[:, i, t, z, :], start=(z == 0), stop=(z == 1))
    last.then_inc(s["summed"], 1)


def dve_weigh(nc, dve, T, s, g, step, banks, gt):
    dve.wait_ge(s["summed"], step + 3)
    n = gt // len(banks)
    for a, b in enumerate(banks):
        dst = g[:, :, bass.ds(step * gt + a * n, n)]
        last = nc.vector.scalar_tensor_tensor(out=dst, in0=bank(T, b, n * PART).rearrange("p (n i) -> p i n", i=PART),
                                              scalar=1.0 / G_SCALE, in1=dst, op0=ALU.mult, op1=ALU.mult)
    last.then_inc(s["kept"], 1)


COEFFICIENTS = ("iota_ready", "rows_ready", "eq_ready", "summed", "kept")


def coefficient_stage(nc, T, l, part):
    g = T.g[part % 2]
    banks = ((4, 5), (6, 7))
    with stage(nc, "u_even", "u_odd", "dotted", "activated", *COEFFICIENTS) as (block, s):
        @block.sync
        def _(sp):
            sp_expert_weights(sp, T, s, T.d["u"], l, part + 1)

        @block.scalar
        def _(act):
            act_gelu(nc, act, T, s, part + 1)

        @block.tensor
        def _(pe):
            pe.sem_inc(s["dotted"], 2)
            pe.sem_inc(s["kept"], 2)
            with pe.Fori(0, PART // 2) as j:
                for i in range(2):
                    pe_expert_dots(nc, pe, T, s, j, i)
                    pe_sums(nc, pe, T, s, 2 * j + i, i, banks[i], GT)

        @block.vector
        def _(dve):
            dve_iota(nc, dve, T, s, part)
            dve.sem_inc(s["summed"], 2)
            with dve.Fori(0, PART // 2) as j:
                for i in range(2):
                    dve_rows(nc, dve, T, s, 2 * j + i, i, GT)
                for i in range(2):
                    dve_weigh(nc, dve, T, s, g, 2 * j + i, banks[i], GT)


WIDE = ((0, 4), (4, 4))
NARROW = ((0, 3), (3, 3), (6, 2))
GROUPS = (WIDE,) * (PARTS - 2) + (NARROW, WIDE)


def expert_out_stage(nc, T, l, part, groups, unroll, woven):
    g = T.g[part % 2]
    ahead = T.g[(part + 1) % 2]
    steps_at = {i: n for n, i in enumerate(i for i in range(unroll) if i % 4 != 3)} if woven else {}
    rounds = PART // unroll
    before = lambda n: sum(len(x) for x in GROUPS) * l + sum(len(x) for x in GROUPS[:part]) + n
    sums = [sum(mn for _, mn in groups[:n]) for n in range(len(groups) + 1)]
    step = lambda n, c, i: n * rounds * len(steps_at) + c * len(steps_at) + steps_at[i]
    with stage(nc, "v_even", "v_odd", "v_free", "v_high", "v_low", "used", "added", "g_low", "out_done",
               *COEFFICIENTS, shared=T.residual_sems) as (block, s):
        v_in = (s["v_even"], s["v_odd"])

        @block.gpsimd
        def _(pool):
            for n, (m0, mn) in enumerate(groups):
                rows = T.d["xs"][m0:m0 + mn].rearrange("m p n -> p m n")
                if woven:
                    with pool.Fori(0, rounds) as c:
                        for i in range(unroll):
                            row = g[:, bass.ds(unroll * c + i, 1), :].rearrange("p a n -> p (a n)")
                            pool.wait_ge(s["v_high"], n * PART + unroll * c + i + 1)
                            nc.gpsimd.tensor_tensor(T.gl[:, i % 2, :], row, T.gh[:, i % 2, :].bitcast(F32),
                                                    ALU.subtract).then_inc(s["g_low"], 1)
                if n:
                    pool.wait_ge(s["out_done"], n)
                pool.dma_start(T.ht[:, 0:mn, :], rows).then_inc(s["h_in"], 16)
                pool.wait_ge(s["added"], sums[n + 1])
                pool.dma_start(rows, T.ht[:, 0:mn, :]).then_inc(s["h_out"], 16)

        @block.sync
        def _(sp):
            for n, (m0, mn) in enumerate(groups):
                with sp.Fori(0, rounds) as c:
                    for i in range(unroll // 2):
                        sp.wait_ge(s["v_free"], n * PART + unroll * c + 2 * i + 2)
                        sp.dma_start(T.vr[:, i % 2, :, 0:mn * P],
                                     T.d["v"][l, part, (unroll // 2) * c + i, :, :, m0 * P:(m0 + mn) * P]
                                     ).then_inc(v_in[i % 2], 16)
                if n:
                    sp.wait_ge(s["h_out"], 16 * before(n))
                    sp.sem_inc(s["out_done"], 1)
            sp.wait_ge(s["h_out"], 16 * before(len(groups)))
            sp.sem_inc(s["out_done"], 1)

        @block.scalar
        def _(act):
            for n, (m0, mn) in enumerate(groups):
                with act.Fori(0, rounds) as c:
                    for i in range(unroll):
                        row = g[:, bass.ds(unroll * c + i, 1), :].rearrange("p a n -> p (a n)")
                        act.wait_ge(s["used"], n * PART + unroll * c + i + 1)
                        nc.scalar.copy(T.gh[:, i % 2, :], row)
                        if i % 2 == 0:
                            act.wait_ge(v_in[i // 2 % 2], 4 * PART * n + 4 * unroll * c + 16 * (i // 4) + 16)
                        nc.scalar.copy(T.vh[:, i % 2, 0:mn * P], T.vr[:, i // 2 % 2, i % 2, 0:mn * P]
                                       ).then_inc(s["v_high"], 1)

        @block.vector
        def _(dve):
            if woven:
                dve_iota(nc, dve, T, s, part + 1)
                dve.sem_inc(s["summed"], 2)
            for n, (m0, mn) in enumerate(groups):
                with dve.Fori(0, rounds) as c:
                    for i in range(unroll):
                        row = g[:, bass.ds(unroll * c + i, 1), :].rearrange("p a n -> p (a n)")
                        dve.wait_ge(s["v_high"], n * PART + unroll * c + i + 1)
                        if not woven:
                            nc.vector.tensor_tensor(T.gl[:, i % 2, :], row, T.gh[:, i % 2, :].bitcast(F32),
                                                    ALU.subtract)
                        nc.vector.tensor_tensor(T.vl[:, i % 2, 0:mn * P], T.vr[:, i // 2 % 2, i % 2, 0:mn * P],
                                                T.vh[:, i % 2, 0:mn * P].bitcast(F32), ALU.subtract
                                                ).then_inc(s["v_low"], 1)
                        dve.wait_ge(s["v_low"], n * PART + unroll * c + i + 1)
                        dve.sem_inc(s["v_free"], 1)
                        if i - 1 in steps_at:
                            dve_weigh(nc, dve, T, s, ahead, step(n, c, i - 1), (6 + steps_at[i - 1] % 2,), GT_W)
                        if i in steps_at:
                            dve_rows(nc, dve, T, s, step(n, c, i), steps_at[i] % 2, GT_W)
                dve.wait_ge(s["used"], (n + 1) * PART + 2)
                dve.wait_ge(s["h_in"], 16 * before(n + 1))
                for m in range(mn):
                    nc.vector.tensor_tensor(two(T.ht[:, m, :]), two(T.ht[:, m, :]), halves(T, 2 * m), ALU.add
                                            ).then_inc(s["added"], 1)

        @block.tensor
        def _(pe):
            pe.sem_inc(s["used"], 2)
            pe.sem_inc(s["v_free"], 4)
            if woven:
                pe.sem_inc(s["kept"], 2)
            for n, (m0, mn) in enumerate(groups):
                for m in range(mn):
                    if n:
                        pe.wait_ge(s["added"], sums[n - 1] + min(m + 1, groups[n - 1][1]))
                    for b in (2 * m, 2 * m + 1):
                        nc.tensor.matmul(bank(T, b)[:, 0:HALF], T.zero[:, 0:P], T.zero[:, 0:HALF], start=True,
                                         stop=False, skip_group_check=True)
                with pe.Fori(0, rounds) as c:
                    for i in range(unroll):
                        pe.wait_ge(s["v_low"], n * PART + unroll * c + i + 1)
                        if woven:
                            pe.wait_ge(s["g_low"], n * PART + unroll * c + i + 1)
                        for m in range(mn):
                            cols = slice(m * P, (m + 1) * P)
                            for vp, gp in ((T.vh, T.gh), (T.vh, T.gl), (T.vl, T.gh)):
                                for a in range(2):
                                    last = nc.tensor.matmul(bank(T, 2 * m + a)[:, 0:HALF], vp[:, i % 2, cols],
                                                            gp[:, i % 2, a * HALF:(a + 1) * HALF],
                                                            start=False, stop=False, skip_group_check=True)
                        last.then_inc(s["used"], 1)
                        if i in steps_at:
                            pe_sums(nc, pe, T, s, step(n, c, i), steps_at[i] % 2, (6 + steps_at[i] % 2,), GT_W)


def one_hot_rows(sb, ctx, T, n, gt):
    T.oh1 = sb(ctx, f"oh1_{n}", [P, 2, gt, P], F16)
    T.oh2 = sb(ctx, f"oh2_{n}", [P, 2, gt, 2, PART], F16)
    T.eq2 = sb(ctx, f"eq2_{n}", [P, 2, gt, PART], F16)


def program(nc, d):
    T = Memory()
    T.d = d
    with ExitStack() as keep:
        def sb(ctx, name, shape, dt=F32):
            return ctx.enter_context(nc.sbuf_tensor(name, shape, dt))

        T.ps = keep.enter_context(nc.psum_tensor("ps", [P, 8 * BANK], F32))
        T.xn = sb(keep, "xn", [P, KD, NP_])
        T.residual_sems = {n: keep.enter_context(nc.semaphore(n)) for n in ("h_in", "h_out")}
        core = sb(keep, "core", [P, 2, P])
        T.ident, T.ones = core[:, 0, :], core[:, 1, :]
        T.eps = sb(keep, "eps", [P, 1])[:]
        with stage(nc, "x_in", "filled") as (block, s):
            @block.vector
            def _(dve):
                nc.vector.memset(T.eps, EPS).then_inc(s["filled"], 1)
                dve.wait_ge(s["filled"], 1)

            @block.sync
            def _(sp):
                sp.dma_start(d["xs"], d["x"]).then_inc(s["x_in"], 16)
                sp.dma_start(T.ident, d["gc"][:, C_MSK:C_MSK + P]).then_inc(s["x_in"], 16)
                sp.dma_start(T.ones, d["gc"][:, C_ONES:C_ONES + P]).then_inc(s["x_in"], 16)
                sp.wait_ge(s["x_in"], 48)
        with nc.Fori(0, DEPTH) as l:
            with ExitStack() as ctx:
                T.general = sb(ctx, "gc", [P, GC_W])
                T.pl = sb(ctx, "pl", [P, PL_W])
                T.pr = sb(ctx, "pr", [P, 9, NP_])
                row = lambda i: T.pr[:, i, :]
                T.hgrn = [row(0), row(1), row(2), row(3)]
                T.gdn, T.gdn_gate = [row(0), row(1), row(2)], row(7)
                T.conv = T.ret = [row(4), row(5), row(6)]
                T.att = [row(8), row(3)]
                T.hc = sb(ctx, "hc", [P, HC_W])
                T.ph = sb(ctx, "ph", [P, PH_W])
                T.vt = sb(ctx, "vt", [P, TILES, 3 * P])
                T.br = sb(ctx, "br", [P, 16, N])
                T.st = sb(ctx, "st", [P, 5, P])
                T.s_in = sb(ctx, "s_in", [P, DEC_B, P])
                T.s_new = sb(ctx, "s_new", [P, DEC_B, P])
                T.kt = sb(ctx, "kt", [P, TILES, P])
                T.cols = sb(ctx, "cols", [P, 40])
                small = sb(ctx, "small", [P, 256])
                T.logg = small[:, 0:20].rearrange("p (t c) -> p t c", t=TILES)
                T.beta = small[:, 20:40].rearrange("p (t c) -> p t c", t=TILES)
                T.ga = small[:, 40:60].rearrange("p (t c) -> p t c", t=TILES)
                T.ga2 = small[:, 60:80].rearrange("p (t c) -> p t c", t=TILES)
                T.nea = small[:, 80:84]
                T.lam = small[:, 84:88]
                T.lb = small[:, 88:92]
                T.lgh = small[:, 96:101].unsqueeze(2)
                T.bth = small[:, 104:109].unsqueeze(2)
                T.lprod = small[:, 128:256].rearrange("p (a d) -> p a d", a=2)
                rs = sb(ctx, "rs", [P, N])
                T.rs = two(rs[:])
                T.tot = sb(ctx, "tot", [P, NP_])[:]
                T.pt = sb(ctx, "pt", [P, DEC_B * PAGES], I32)
                with ExitStack() as sub:
                    T.wr = sb(sub, "wr", [P, 4, KD, P])
                    T.wk = sb(sub, "wk", [P, 20, NP_])
                    flat = T.wk.rearrange("p a b -> p (a b)")
                    T.wtm = T.wr.rearrange("p a k c -> p (a k c)")[:, 0:KD * 2 * P].rearrange("p (k c) -> p k c", k=KD)
                    T.h = flat[:, 0:KD * N].rearrange("p (k n) -> p k n", k=KD)
                    T.sq = flat[:, KD * N:2 * KD * N].rearrange("p (k n) -> p k n", k=KD)
                    T.wab = flat[:, 2 * KD * N:2 * KD * N + 8 * KD].rearrange("p (k c) -> p k c", k=KD)
                    T.sc = T.wk[:, 0, :]
                    T.masked = flat[:, 18 * NP_:18 * NP_ + 8 * P]
                    T.vx = sb(sub, "vx", [P, DEC_B, P])
                    T.dc = sb(sub, "dc", [P, DC_W])[:]
                    norm_stage(nc, T, l, True)
                    first_head_stage(nc, T, l)
                    with nc.Fori(0, H - 1) as h:
                        head(nc, T, l, h, True)
                    head(nc, T, l, H - 1, False)
                with ExitStack() as sub:
                    T.wm = sb(sub, "wm", [P, 2, 12, P])
                    T.mt = sb(sub, "mt", [P, KD, N])
                    sg = sb(sub, "sg", [P, 3, N])
                    T.sg = [two(sg[:, i, :]) for i in range(2)]
                    T.ma = two(sg[:, 2, :])
                    merge_stage(nc, T, l)
                    T.h = sb(sub, "h2", [P, KD, N])
                    out_stage(nc, T, l)
                    T.sq = T.mt
                    norm_stage(nc, T, l, False)
            with ExitStack() as ctx:
                T.g = [sb(ctx, "g0", [P, PART, N])]
                T.idx = sb(ctx, "idx", [P, 4, NP_], F16)
                T.iota_b = sb(ctx, "iota_b", [P, P], F16)[:]
                T.iota_h = sb(ctx, "iota_h", [P, PART], F16)[:]
                T.zero = sb(ctx, "zero", [P, HALF], F16)[:]
                with ExitStack() as sub:
                    T.iota = sb(sub, "iota", [P, P])
                    T.scr = sb(sub, "scr", [P, TILES, 2 * PH_HEADS, NKEY])
                    with ExitStack() as early:
                        T.keys = sb(early, "keys", [P, 2 * PH_HEADS, P])[:]
                        T.wm2 = sb(early, "wm2", [P, 2, KD, P])
                        qt = sb(early, "qt", [P, 2, NP_])
                        T.qt = [qt[:, i, :] for i in range(2)]
                        key_scores_stage(nc, T, l)
                    T.x1 = sb(sub, "x1", [P, 2 * PH_HEADS, NKEY])[:]
                    T.t1 = sb(sub, "t1", [P, 2 * PH_HEADS, TOPK])[:]
                    T.i1u = sb(sub, "i1u", [P, 2 * PH_HEADS, TOPK], U32)[:]
                    T.i1f = sb(sub, "i1f", [P, 2 * PH_HEADS, TOPK])[:]
                    T.cand = sb(sub, "cand", [P, PH_HEADS, TOPK * TOPK])[:]
                    T.posu = sb(sub, "posu", [P, PH_HEADS, TOPK], U32)[:]
                    T.pau = sb(sub, "pau", [P, PH_HEADS, TOPK], U32)[:]
                    T.pbu = sb(sub, "pbu", [P, PH_HEADS, TOPK], U32)[:]
                    T.paf = sb(sub, "paf", [P, PH_HEADS, TOPK])[:]
                    T.pbf = sb(sub, "pbf", [P, PH_HEADS, TOPK])[:]
                    T.tv = sb(sub, "tv", [P, PH_HEADS, TOPK])[:]
                    T.t2 = sb(sub, "t2", [P, TILES, PH_HEADS, TOPK])
                    T.found = sb(sub, "found", [P, 3, TILES, P])
                    T.spare = sb(sub, "spare", [P, 1])[:]
                    T.gs = sb(sub, "gs", [P, TILES * PH_HEADS])[:]
                    T.ur = sb(sub, "ur0", [P, 2, KD, P])
                    retrieval_stage(nc, T, l)
                T.g.append(sb(ctx, "g1", [P, PART, N]))
                for part in range(PARTS):
                    if part < PARTS - 1:
                        with ExitStack() as sub:
                            T.ur = sb(sub, f"ur{part + 1}", [P, 2, KD, P])
                            one_hot_rows(sb, sub, T, part, GT)
                            coefficient_stage(nc, T, l, part)
                    woven = part == PARTS - 2
                    groups, unroll = GROUPS[part], 8 if woven else 4
                    with ExitStack() as sub:
                        width = groups[0][1]
                        T.vr = sb(sub, f"vr{part}", [P, 2, 2, width * P])
                        T.vh = sb(sub, f"vh{part}", [P, 2, width * P], F32R)
                        T.vl = sb(sub, f"vl{part}", [P, 2, width * P], F32R)
                        T.gh = sb(sub, f"gh{part}", [P, 2, N], F32R)
                        T.gl = sb(sub, f"gl{part}", [P, 2, N], F32R)
                        T.ht = sb(sub, f"ht{part}", [P, width, N])
                        if woven:
                            one_hot_rows(sb, sub, T, PARTS, GT_W)
                        expert_out_stage(nc, T, l, part, groups, unroll, woven)
        with stage(nc, "y_out") as (block, s):
            @block.sync
            def _(sp):
                sp.dma_start(d["y"], d["xs"]).then_inc(s["y_out"], 16)
                sp.wait_ge(s["y_out"], 16)


def br_slot(b, h):
    return bass.ds(4 * b + h, 1)


def constants():
    f = np.float32
    p = np.arange(P)
    key, qry = p[:, None], p[None, :]
    gc = np.zeros((P, GC_W), f)
    gc[:, C_MSK:C_MSK + P] = np.eye(P)
    for r in range(LEVELS):
        m = 1 << r
        pair = (key // (2 * m) == qry // (2 * m)) & (key // m % 2 == 0) & (qry // m % 2 == 1)
        gc[:, C_MSK + (1 + r) * P:C_MSK + (2 + r) * P] = pair
    gc[:, C_ONES:C_ONES + P] = 1
    causal = key <= qry
    same = key // DEC_T == qry // DEC_T
    for t in range(TILES):
        gc[:, C_UT + t * P:C_UT + (t + 1) * P] = causal if t < 4 else causal & same
    gc[:, C_BLK:C_BLK + P] = same
    gc[:, C_BS:C_BS + DEC_B] = key // DEC_T == np.arange(DEC_B)[None, :]
    gc[:, C_COMP:C_COMP + P] = key // DK == qry // DK
    gc[:, C_SELA] = p < DK
    gc[:, C_SELB] = p >= DK
    dc = np.zeros((P, DC_W), f)
    x = np.arange(SEQ)[None, :]
    dist = p[:, None] + (SEQ - P) - x
    dc[:, C_DP:C_DP + SEQ] = np.where(dist >= 0, dist, FAR)
    tok = p % NS
    pos = tok % DEC_T
    dc[:, C_DS:C_DS + PAST] = PAST + pos[:, None] - np.arange(PAST)[None, :]
    new = np.arange(NS)[None, :]
    gap = pos[:, None] - new % DEC_T
    ok = (tok[:, None] // DEC_T == new // DEC_T) & (gap >= 0)
    dc[:, C_DS + PAST:C_DS + PAST + NS] = np.where(ok, gap, FAR)
    dc[:, C_STK:C_STK + NS] = tok[:, None] == new
    qm = np.zeros((P, DEC_B + 1, 2, NS))
    for c in range(2):
        qm[c * DK:(c + 1) * DK, DEC_B, c, :] = 1
        for b in range(DEC_B):
            qm[c * DK:(c + 1) * DK, b, c, b * DEC_T:(b + 1) * DEC_T] = 1
    dc[:, C_QM:] = qm.reshape(P, -1)
    hc = np.zeros((H, P, HC_W), np.float64)
    for h in range(H):
        lg = np.log1p(-np.exp2(-5.0 - h))
        gap = qry - key
        decay = np.where(gap >= 0, np.exp(np.maximum(gap, 0) * lg), 0.0) * K_SCALE
        for t in range(TILES):
            c = slice(t * P, (t + 1) * P)
            hc[h, :, H_RM:][:, c] = decay if t < 4 else decay * same
            at = p if t < 4 else p % DEC_T
            hc[h, :, H_QD:][:, c] = np.exp((at + 1) * lg)[None, :]
            hc[h, :, H_KD + t] = np.exp(((P if t < 4 else DEC_T) - 1 - at) * lg) * K_SCALE
            hc[h, :, H_GT + t] = np.exp(P * lg)
        hc[h, :, H_G8:H_G8 + DEC_B] = np.exp(DEC_T * lg)
    layer = np.zeros((DEPTH, 3), f)
    for l in range(DEPTH):
        li = 0.8 - 0.6 * np.exp(-0.3 * l)
        layer[l] = (float(l > 0), li, 1.0 - li)
    return gc, dc, hc.astype(f), layer


def lay_out(i):
    c = np.ascontiguousarray
    i = {k: np.asarray(v) for k, v in i.items()}
    gc, dc, hc, layer = constants()
    a = {"gc": gc, "dc": dc, "hc": hc}
    x = np.concatenate([i["x_prompt"].reshape(SEQ, D), i["x_sample"].reshape(NS, D)])
    a["x"] = c(x.T.reshape(KD, P, N))
    w = i["w_in"]
    kt = lambda m: m.reshape(m.shape[0], KD, P, -1).transpose(0, 2, 1, 3)
    at = lambda o, h: slice(o + h * P, o + (h + 1) * P)
    rq, rk, rv, rg, hq, hf, hi, hg, gq, gk, gv, gg = (j * 512 for j in range(12))
    ga = 12 * 512
    dq = ga + 2 * H
    dk, dv = dq + 512, dq + 1024
    gate = dq + 1536
    cols = (rq, rk, rg, hq, hf, hg, gq, gk, gv, gg, dq, dk, dv)
    a["w_cm"] = c(np.stack([np.stack([kt(w[:, :, at(o, h)]) for o in cols], 1) for h in range(H)], 1))
    a["w_tm"] = c(np.stack([kt(np.concatenate([w[:, :, at(o, h)] for o in (rv, hi)], 2)) for h in range(H)], 1))
    a["w_ab"] = c(kt(w[:, :, ga:ga + 2 * H]))
    wg = w[:, :, gate:].reshape(DEPTH, KD, P, 4, KD, P).transpose(0, 4, 3, 2, 1, 5)
    wb = i["w_branch"].reshape(DEPTH, 4, 4, P, KD, P).transpose(0, 4, 1, 3, 2, 5)
    a["w_merge"] = c(np.concatenate([wg, wb], 4))
    a["w_out"] = c(i["w_out"].reshape(DEPTH, KD, P, KD, P).transpose(0, 3, 2, 1, 4))
    a["w_query"] = c(i["peer_wq"].reshape(DEPTH, KD, P, 2 * PH_HEADS, P).transpose(0, 3, 2, 1, 4))
    a["keys"] = c(i["peer_keys"].reshape(DEPTH, 2 * PH_HEADS, NKEY, P).transpose(0, 3, 1, 2))
    u = i["peer_u"].reshape(DEPTH, NKEY, PARTS, PART, KD, P)
    a["u"] = c(u.transpose(0, 2, 3, 5, 4, 1))
    v = i["peer_v"].reshape(DEPTH, NKEY, PARTS, PART // 2, 2, D)
    a["v"] = c(v.transpose(0, 2, 3, 1, 4, 5))
    rep = lambda m: np.repeat(m[:, None, :], P, 1)
    fk = lambda m: m.reshape(DEPTH, KD, P).transpose(0, 2, 1)
    a["pl"] = c(np.concatenate([fk(i["norm_mix"]), fk(i["norm_ffn"]), rep(i["gdn_a_log"]), rep(i["gdn_dt_bias"]),
                                rep(i["diff_lambda"].reshape(DEPTH, -1)), rep(layer)], 2))
    ph = np.zeros((DEPTH, H, P, PH_W), np.float32)
    for n, name in enumerate(("ret_norm", "hgrn_norm", "gdn_norm", "diff_norm")):
        ph[..., n] = i[name].reshape(DEPTH, H, P)
    taps = i["gdn_conv"].reshape(DEPTH, 4, 3, H, P).transpose(0, 3, 4, 2, 1)
    ph[..., Q_CONV:Q_CONV + 12] = taps.reshape(DEPTH, H, P, 12)
    ph[..., Q_LB:Q_LB + 2] = i["hgrn_lb_logits"].reshape(DEPTH, H, P).transpose(1, 2, 0)[None]
    ph[..., Q_SL] = -(2.0 ** (-8.0 * (np.arange(H)[None, :, None] + 1) / H)) / S_SCALE
    ph[..., Q_QN] = np.tile(i["diff_q_norm"], (1, 2))[:, None, :]
    ph[..., Q_KN] = np.tile(i["diff_k_norm"], (1, 2))[:, None, :]
    a["ph"] = ph
    a["conv_in"] = c(i["state_gdn_conv"].reshape(DEPTH, DEC_B, 3, 3, H, P).transpose(0, 4, 3, 5, 1, 2))
    for n in ("state_ret", "state_hgrn", "state_gdn"):
        a[n] = c(i[n])
    a["cache_k"] = c(i["cache_k"].reshape(DEPTH, N_PHYS, PAGE, H, P).transpose(0, 1, 3, 4, 2))
    a["cache_v"] = c(i["cache_v"].transpose(0, 1, 3, 2, 4))
    a["page_table"] = c(i["page_table"].reshape(1, -1).astype(np.int32))
    return a


_OUTS = {
    "y": (KD, P, N),
    "ret_prompt": (DEPTH, H, P, P), "ret_sample": (DEPTH, DEC_B, H, P, P),
    "hgrn_prompt": (DEPTH, H, P, P), "hgrn_sample": (DEPTH, DEC_B, H, P, P),
    "gdn_prompt": (DEPTH, H, P, P), "gdn_sample": (DEPTH, DEC_B, H, P, P),
    "conv_prompt": (DEPTH, H, 3, P, 3), "conv_sample": (DEPTH, H, 3, P, DEC_B, 3),
    "k_out": (DEPTH, H, P, N), "v_prompt": (DEPTH, H, SEQ, P), "v_sample": (DEPTH, H, NS, P),
}


def kernel(**inputs):
    import concourse.bacc as _bacc
    from concourse.bass_utils import run_bass_kernel_spmd as _run

    nc = _bacc.Bacc("TRN2", target_bir_lowering=False, num_devices=1)
    arrays = lay_out(inputs)
    d = {}
    for name, a in arrays.items():
        d[name] = nc.dram_tensor(f"in_{name}", a.shape, mybir.dt.from_np(a.dtype), kind="ExternalInput").ap()
    for name, shape in _OUTS.items():
        d[name] = nc.dram_tensor(f"out_{name}", shape, F32, kind="ExternalOutput").ap()
    d["xs"] = nc.dram_tensor("residual", (KD, P, N), F32, kind="Internal").ap()
    program(nc, d)
    r = _run(nc, [{f"in_{n}": a for n, a in arrays.items()}], core_ids=[0])
    o = {n: r.results[0][f"out_{n}"] for n in _OUTS}
    y = o["y"].reshape(D, N).T
    conv_p = o["conv_prompt"].transpose(0, 4, 2, 1, 3).reshape(DEPTH, 1, 3, 3 * 512)
    conv_s = o["conv_sample"].transpose(0, 4, 5, 2, 1, 3).reshape(DEPTH, DEC_B, 3, 3 * 512)
    k = o["k_out"].transpose(0, 3, 1, 2)
    return (y[:SEQ].reshape(1, SEQ, D), y[SEQ:].reshape(DEC_B, DEC_T, D),
            o["ret_prompt"][:, None], o["ret_sample"], o["hgrn_prompt"][:, None], o["hgrn_sample"],
            o["gdn_prompt"][:, None], o["gdn_sample"], conv_p, conv_s,
            k[:, :SEQ].reshape(DEPTH, 1, SEQ, H, 2, DK),
            o["v_prompt"].transpose(0, 2, 1, 3)[:, None],
            k[:, SEQ:].reshape(DEPTH, DEC_B, DEC_T, H, 2, DK),
            o["v_sample"].transpose(0, 2, 1, 3).reshape(DEPTH, DEC_B, DEC_T, H, P))
```
